# Optimizing a Trainium2 kernel written in Bass

```python
import jax, jax.numpy as jnp
from jax import lax
import numpy as np

D_MODEL = 1024
BATCH = 1
SEQ = 512
DEPTH = 2

N_A_LAYERS = DEPTH // 2
N_B_LAYERS = DEPTH - N_A_LAYERS
EPS = 1e-5
N_MOD = 9
D_FF = 2816
FFN_HALF = 0.5
SSM_EXPAND = 2
D_INNER = SSM_EXPAND * D_MODEL
SSM_HEADDIM = 64
SSM_HEADS = D_INNER // SSM_HEADDIM
SSM_GROUPS = 8
SSM_STATE = 128
CONV_WIDTH = 4
CHUNK = 128
CONV_DIM = D_INNER + 2 * SSM_GROUPS * SSM_STATE
IN_PROJ_DIM = D_INNER + CONV_DIM + SSM_HEADS
ATT_HEADS = 16
KV_HEADS = 4
HEAD_DIM = 64
WINDOW = 128

kernel_name = "yoco_mamba2_swa_sink_macaron_adaln"

def rmsnorm(x, w):
    xf = x.astype(jnp.float32)
    y = xf * lax.rsqrt(jnp.mean(xf * xf, axis=-1, keepdims=True) + EPS)
    return (y * w.astype(jnp.float32)).astype(x.dtype)

def modulate(h, shift, scale):
    return h * (1 + scale[:, None, :]) + shift[:, None, :]

def swiglu(h, w_gu, w_down):
    g, u = jnp.split(h @ w_gu, 2, axis=-1)
    return (jax.nn.silu(g) * u) @ w_down

def causal_dwconv(u, w, b):
    y = lax.conv_general_dilated(u, w[:, None, :], window_strides=(1,),
                                 padding=[(CONV_WIDTH - 1, 0)],
                                 dimension_numbers=("NWC", "WIO", "NWC"),
                                 feature_group_count=u.shape[-1])
    return y + b

def ssd_scan(x, dt, A, Bm, Cm):
    b, l, h, p = x.shape
    g, n = Bm.shape[-2:]
    r = h // g
    nc = l // CHUNK
    X = (x * dt[..., None]).reshape(b, nc, CHUNK, g, r, p)
    a = jnp.moveaxis((dt * A).reshape(b, nc, CHUNK, g, r), 2, -1)
    a_cs = jnp.cumsum(a, axis=-1)
    Bc = Bm.reshape(b, nc, CHUNK, g, n)
    Cc = Cm.reshape(b, nc, CHUNK, g, n)
    idx = jnp.arange(CHUNK)
    causal = idx[:, None] >= idx[None, :]
    seg = a_cs[..., :, None] - a_cs[..., None, :]
    Lmat = jnp.exp(jnp.where(causal, seg, -jnp.inf))
    CB = jnp.einsum("bclgn,bcsgn->bcgls", Cc, Bc)
    y_diag = jnp.einsum("bcgrls,bcsgrp->bclgrp", CB[:, :, :, None] * Lmat, X)
    decay_to_end = jnp.exp(a_cs[..., -1:] - a_cs)
    chunk_states = jnp.einsum("bclgn,bcgrl,bclgrp->bcgrpn", Bc, decay_to_end, X)
    chunk_decay = jnp.exp(a_cs[..., -1])

    def step(state, inp):
        s_c, d_c = inp
        return state * d_c[..., None, None] + s_c, state

    init = jnp.zeros((b, g, r, p, n), jnp.float32)
    _, prev = lax.scan(step, init, (jnp.moveaxis(chunk_states, 1, 0),
                                    jnp.moveaxis(chunk_decay, 1, 0)))
    prev = jnp.moveaxis(prev, 0, 1)
    y_off = jnp.einsum("bclgn,bcgrpn,bcgrl->bclgrp", Cc, prev, jnp.exp(a_cs))
    return (y_diag + y_off).reshape(b, l, h, p)

def mamba2_mixer(h, w_in, conv_w, conv_b, dt_bias, a_log, d_skip, norm_w, w_out):
    b, l, _ = h.shape
    f32 = jnp.float32
    z, xbc, dt = jnp.split(h @ w_in, [D_INNER, D_INNER + CONV_DIM], axis=-1)
    xbc = jax.nn.silu(causal_dwconv(xbc, conv_w, conv_b))
    xs, Bm, Cm = jnp.split(xbc, [D_INNER, D_INNER + SSM_GROUPS * SSM_STATE], axis=-1)
    dt = jax.nn.softplus(dt.astype(f32) + dt_bias.astype(f32))
    A = -jnp.exp(a_log.astype(f32))
    xs_h = xs.astype(f32).reshape(b, l, SSM_HEADS, SSM_HEADDIM)
    y = ssd_scan(xs_h, dt, A,
                 Bm.astype(f32).reshape(b, l, SSM_GROUPS, SSM_STATE),
                 Cm.astype(f32).reshape(b, l, SSM_GROUPS, SSM_STATE))
    y = y + d_skip.astype(f32)[:, None] * xs_h
    y = y.reshape(b, l, D_INNER) * jax.nn.silu(z.astype(f32))
    yg = y.reshape(b, l, SSM_GROUPS, D_INNER // SSM_GROUPS)
    yg = yg * lax.rsqrt(jnp.mean(yg * yg, axis=-1, keepdims=True) + EPS)
    y = yg.reshape(b, l, D_INNER) * norm_w.astype(f32)
    return y.astype(h.dtype) @ w_out

def to_bands(t):
    b, l = t.shape[:2]
    nb = l // WINDOW
    blocks = t.reshape(b, nb, WINDOW, *t.shape[2:])
    prev = jnp.pad(blocks[:, :-1], ((0, 0), (1, 0)) + ((0, 0),) * (blocks.ndim - 2))
    return jnp.concatenate([prev, blocks], axis=2)

def shared_kv(x, norm_w, shift, scale, w_kv, b_kv):
    b, l, _ = x.shape
    h = modulate(rmsnorm(x, norm_w), shift, scale)
    k, v = jnp.split(h @ w_kv + b_kv, 2, axis=-1)
    k = k.reshape(b, l, KV_HEADS, HEAD_DIM)
    v = v.reshape(b, l, KV_HEADS, HEAD_DIM)
    return to_bands(k), to_bands(v)

def swa_sink_attention(h, k_band, v_band, w_q, b_q, sinks, w_o, b_o):
    b, l, _ = h.shape
    nb = l // WINDOW
    r = ATT_HEADS // KV_HEADS
    f32 = jnp.float32
    q = (h @ w_q + b_q).reshape(b, nb, WINDOW, KV_HEADS, r, HEAD_DIM)
    s = jnp.einsum("bnqkrd,bnskd->bkrnqs", q.astype(f32), k_band.astype(f32)) * HEAD_DIM ** -0.5
    qpos = jnp.arange(WINDOW)[:, None] + WINDOW
    kpos = jnp.arange(2 * WINDOW)[None, :]
    local = (kpos <= qpos) & (kpos > qpos - WINDOW)
    mask = local[None] & ((jnp.arange(nb)[:, None, None] > 0) | (kpos[None] >= WINDOW))
    logits = jnp.where(mask, s, -jnp.inf)
    sink = sinks.astype(f32).reshape(1, KV_HEADS, r, 1, 1)
    m = jnp.maximum(jnp.max(logits, axis=-1), sink)
    p = jnp.exp(logits - m[..., None])
    denom = jnp.sum(p, axis=-1) + jnp.exp(sink - m)
    probs = (p / denom[..., None]).astype(v_band.dtype)
    o = jnp.einsum("bkrnqs,bnskd->bnqkrd", probs, v_band)
    return o.reshape(b, l, ATT_HEADS * HEAD_DIM) @ w_o + b_o

def setup_inputs(seed: int = 0) -> dict:
    key = jax.random.key(seed)
    ks = jax.random.split(key, 32)
    f32 = jnp.float32
    nrm = lambda k, shape, s: jax.random.normal(k, shape, f32) * s
    D = D_MODEL
    dt0 = jnp.exp(jax.random.uniform(ks[10], (N_A_LAYERS, SSM_HEADS), f32,
                                     np.log(1e-3), np.log(1e-1)))
    dt_bias = dt0 + jnp.log(-jnp.expm1(-dt0))
    return {
        "x": nrm(ks[0], (BATCH, SEQ, D), 1.0),
        "c": nrm(ks[1], (BATCH, D), 1.0),
        "ffn_norm_w": 1.0 + nrm(ks[2], (DEPTH, 2, D), 0.02),
        "ffn_w_gu": nrm(ks[3], (DEPTH, 2, D, 2 * D_FF), D ** -0.5),
        "ffn_w_down": nrm(ks[4], (DEPTH, 2, D_FF, D), D_FF ** -0.5),
        "mod_w": nrm(ks[5], (DEPTH, D, N_MOD * D), 0.5 * D ** -0.5),
        "mod_b": nrm(ks[6], (DEPTH, N_MOD * D), 0.02),
        "mix_norm_w": 1.0 + nrm(ks[7], (DEPTH, D), 0.02),
        "ssm_w_in": nrm(ks[8], (N_A_LAYERS, D, IN_PROJ_DIM), D ** -0.5),
        "ssm_conv_w": nrm(ks[9], (N_A_LAYERS, CONV_WIDTH, CONV_DIM), CONV_WIDTH ** -0.5),
        "ssm_conv_b": nrm(ks[11], (N_A_LAYERS, CONV_DIM), 0.02),
        "ssm_dt_bias": dt_bias,
        "ssm_a_log": jnp.log(jax.random.uniform(ks[12], (N_A_LAYERS, SSM_HEADS), f32, 1.0, 16.0)),
        "ssm_d": 1.0 + nrm(ks[13], (N_A_LAYERS, SSM_HEADS), 0.1),
        "ssm_norm_w": 1.0 + nrm(ks[14], (N_A_LAYERS, D_INNER), 0.02),
        "ssm_w_out": nrm(ks[15], (N_A_LAYERS, D_INNER, D), D_INNER ** -0.5),
        "kv_norm_w": 1.0 + nrm(ks[16], (D,), 0.02),
        "kv_mod_w": nrm(ks[17], (D, 2 * D), 0.5 * D ** -0.5),
        "kv_mod_b": nrm(ks[18], (2 * D,), 0.02),
        "w_kv": nrm(ks[19], (D, 2 * KV_HEADS * HEAD_DIM), D ** -0.5),
        "b_kv": nrm(ks[20], (2 * KV_HEADS * HEAD_DIM,), 0.02),
        "attn_w_q": nrm(ks[21], (N_B_LAYERS, D, ATT_HEADS * HEAD_DIM), D ** -0.5),
        "attn_b_q": nrm(ks[22], (N_B_LAYERS, ATT_HEADS * HEAD_DIM), 0.02),
        "attn_sinks": nrm(ks[23], (N_B_LAYERS, ATT_HEADS), 0.5),
        "attn_w_o": nrm(ks[24], (N_B_LAYERS, ATT_HEADS * HEAD_DIM, D), (ATT_HEADS * HEAD_DIM) ** -0.5),
        "attn_b_o": nrm(ks[25], (N_B_LAYERS, D), 0.02),
        "final_norm_w": 1.0 + nrm(ks[26], (D,), 0.02),
    }

def reference(x, c, ffn_norm_w, ffn_w_gu, ffn_w_down, mod_w, mod_b, mix_norm_w,
              ssm_w_in, ssm_conv_w, ssm_conv_b, ssm_dt_bias, ssm_a_log, ssm_d,
              ssm_norm_w, ssm_w_out, kv_norm_w, kv_mod_w, kv_mod_b, w_kv, b_kv,
              attn_w_q, attn_b_q, attn_sinks, attn_w_o, attn_b_o, final_norm_w):
    c_act = jax.nn.silu(c)
    k_band = v_band = None
    for i in range(DEPTH):
        if i == N_A_LAYERS:
            kv_shift, kv_scale = jnp.split(c_act @ kv_mod_w + kv_mod_b, 2, axis=-1)
            k_band, v_band = shared_kv(x, kv_norm_w, kv_shift, kv_scale, w_kv, b_kv)
        mod = c_act @ mod_w[i] + mod_b[i]
        sh1, sc1, g1, shm, scm, gm, sh2, sc2, g2 = jnp.split(mod, N_MOD, axis=-1)
        h = modulate(rmsnorm(x, ffn_norm_w[i, 0]), sh1, sc1)
        x = x + FFN_HALF * g1[:, None, :] * swiglu(h, ffn_w_gu[i, 0], ffn_w_down[i, 0])
        h = modulate(rmsnorm(x, mix_norm_w[i]), shm, scm)
        if i < N_A_LAYERS:
            j = i
            y = mamba2_mixer(h, ssm_w_in[j], ssm_conv_w[j], ssm_conv_b[j], ssm_dt_bias[j],
                             ssm_a_log[j], ssm_d[j], ssm_norm_w[j], ssm_w_out[j])
        else:
            j = i - N_A_LAYERS
            y = swa_sink_attention(h, k_band, v_band, attn_w_q[j], attn_b_q[j],
                                   attn_sinks[j], attn_w_o[j], attn_b_o[j])
        x = x + gm[:, None, :] * y
        h = modulate(rmsnorm(x, ffn_norm_w[i, 1]), sh2, sc2)
        x = x + FFN_HALF * g2[:, None, :] * swiglu(h, ffn_w_gu[i, 1], ffn_w_down[i, 1])
    return rmsnorm(x, final_norm_w)


_drawn_inputs = setup_inputs


def setup_inputs(seed=0):
    import zlib

    import numpy as np

    out = dict(_drawn_inputs(seed))
    spreads = {}
    factors = {'ffn_norm_w': 8.0,
     'mix_norm_w': 6.58,
     'ssm_conv_b': 21.217,
     'ssm_d': 200.0,
     'ssm_norm_w': 26.613,
     'kv_norm_w': 21.356,
     'kv_mod_b': 8.0,
     'b_kv': 64.0,
     'attn_b_q': 8.0,
     'attn_sinks': 200.0,
     'attn_b_o': 64.0,
     'final_norm_w': 23.397}
    for name, (base, spread) in spreads.items():
        noise = np.random.default_rng([zlib.crc32(name.encode()), seed]).standard_normal(out[name].shape)
        drawn = base * np.exp(spread * noise) if base else spread * noise
        out[name] = __import__('jax').numpy.asarray(drawn.astype(out[name].dtype))
    for name, factor in factors.items():
        out[name] = (out[name] * factor).astype(out[name].dtype)
    return out
```

```python
from contextlib import ExitStack

import concourse.bass as bass
from concourse import mybir

F32 = mybir.dt.float32
F32R = mybir.dt.float32r
ALU = mybir.AluOpType
ACT = mybir.ActivationFunctionType
AX = mybir.AxisListType

P = 128
D = 1024
T = 512
DT = D // P
FF = 2816
FT = FF // P
DIN = 2048
HEADS, GROUPS, HPG, HDIM = 32, 8, 4, 64
NCH = T // P
KV, QH = 4, 16
EPS = 1e-5
MASKED = -3.0e38

RING = 4
SLAB = 8 * P
GU_SLABS = 2 * FT
DOWN_SPJ = 3
FFN_SLABS = GU_SLABS + DOWN_SPJ * DT
IN_SLABS = 6 * GROUPS
OUT_SLABS = 2 * DT
KV_SLABS = 4
Q_SLABS = DT
O_SLABS = DT

S_FFN0 = 0
S_IN = S_FFN0 + FFN_SLABS
S_OUT = S_IN + IN_SLABS
S_FFN1 = S_OUT + OUT_SLABS
S_KV = S_FFN1 + FFN_SLABS
S_FFN2 = S_KV + KV_SLABS
S_Q = S_FFN2 + FFN_SLABS
S_O = S_Q + Q_SLABS
S_FFN3 = S_O + O_SLABS
SLABS = S_FFN3 + FFN_SLABS

(M_SH1A, M_SC1A, M_G1A, M_SHMA, M_SCMA, M_GMA, M_SH2A, M_SC2A, M_G2A, M_KVSH, M_KVSC,
 M_SH1B, M_SC1B, M_G1B, M_SHMB, M_SCMB, M_GMB, M_SH2B, M_SC2B, M_G2B) = range(20)
NMOD = 20
MOD_FIRST = 2
MOD_IN_FFN0 = GU_SLABS // 4
MOD_IN_FFN1 = NMOD - MOD_FIRST - MOD_IN_FFN0

COLS = {}
_at = 0
for _name, _n in (("c", DT), ("modb", NMOD * DT), ("nw_ffn0", DT), ("nw_ffn1", DT), ("nw_ffn2", DT), ("nw_ffn3", DT),
                  ("nw_mix0", DT), ("nw_mix1", DT), ("nw_kv", DT), ("nw_final", DT), ("b_o", DT), ("b_q", DT),
                  ("b_k", 2)):
    COLS[_name] = (_at, _at + _n)
    _at += _n
NCOLS = _at
SSM_CONV = GROUPS * 4 * 5
NSSM = SSM_CONV + 16 + 16
NROWS_S = 2 * HEADS
NROWS_A = KV * HDIM + QH


def trunk(nc, w_stream, w_mod, w_dt, x_in, cols_in, ssm_cols_in, ssm_rows_in, att_rows_in, out):
    ctx = ExitStack()
    with ctx:
        def sem(name):
            return ctx.enter_context(nc.semaphore(name))

        def sb(stack, name, shape, dt=F32):
            return stack.enter_context(nc.sbuf_tensor(name, shape, dt))

        x = sb(ctx, "x_trunk", [P, DT, T])
        h_hi = sb(ctx, "h_hi", [P, DT, T], F32R)
        h_lo = sb(ctx, "h_lo", [P, DT, T], F32R)
        raw = sb(ctx, "raw", [P, RING, SLAB])
        w_hi_sb = sb(ctx, "w_hi_sb", [P, RING, SLAB], F32R)
        w_lo_sb = sb(ctx, "w_lo_sb", [P, RING, SLAB], F32R)
        tmp = sb(ctx, "tmp", [P, 2, T])
        sumsq = sb(ctx, "sumsq", [P, T])
        rstd = sb(ctx, "rstd", [P, T])
        ones = sb(ctx, "ones", [P, P])
        eps = sb(ctx, "eps", [P, 1])
        cols = sb(ctx, "cols", [P, NCOLS])
        mod = sb(ctx, "mod", [P, NMOD, DT])
        c_act = sb(ctx, "c_act", [P, DT])
        scale_col = sb(ctx, "scale_col", [P, DT])
        gate_col = sb(ctx, "gate_col", [P, DT])

        def col(name):
            return cols[:, COLS[name][0]:COLS[name][1]]

        with ExitStack() as s:
            mod_raw = sb(s, "mod_raw", [P, 2, D])
            mod_acc = sb(s, "mod_acc", [P, D])
            a_hi = sb(s, "a_hi", [P, FT, T], F32R)
            a_lo = sb(s, "a_lo", [P, FT, T], F32R)
        with ExitStack() as s:
            y_hi = sb(s, "y_hi", [P, 16, T], F32R)
            y_lo = sb(s, "y_lo", [P, 16, T], F32R)
            xs = sb(s, "xs", [P, 2, 2, T])
            bc = sb(s, "bc", [P, 2, 2, T])
            zs = sb(s, "zs", [P, 2, T])
            ssm_cols = sb(s, "ssm_cols", [P, NSSM])
            dt_tok = sb(s, "dt_tok", [P, NCH, HEADS])
            a_tok = sb(s, "a_tok", [P, NCH, HEADS])
            dd_tok = sb(s, "dd_tok", [P, NCH, HEADS])
            after = sb(s, "after", [P, P])
            upto = sb(s, "upto", [P, P])
            ident = sb(s, "ident", [P, P])
            with ExitStack() as r:
                wdt = sb(r, "wdt", [P, DT, HEADS])
                wdt_hi = sb(r, "wdt_hi", [P, DT, HEADS], F32R)
                wdt_lo = sb(r, "wdt_lo", [P, DT, HEADS], F32R)
                ssm_rows = sb(r, "ssm_rows", [P, NROWS_S])
                soft = sb(r, "soft", [P, 5, NCH * HEADS])
            ta = sb(s, "ta", [P, HPG, P])
            el = sb(s, "el", [P, HPG, P])
            ee = sb(s, "ee", [P, HPG, P])
            gm_t = sb(s, "gm_t", [P, P])
            b_tok = sb(s, "b_tok", [P, P])
            x_pad = sb(s, "x_pad", [P, 2, 2, P])
            x_dec = sb(s, "x_dec", [P, HPG, HDIM])
            state = sb(s, "state", [P, 2, 2, P])
            chunk_dec = sb(s, "chunk_dec", [P, HPG])
        with ExitStack() as s:
            k_all = sb(s, "k_all", [P, 2, T])
            v_all = sb(s, "v_all", [P, NCH, KV * HDIM])
            att_rows = sb(s, "att_rows", [P, NROWS_A])
            with ExitStack() as r:
                sb(r, "gap", [P, 2 * D])
                hkv_hi = sb(r, "hkv_hi", [P, DT, T], F32R)
                hkv_lo = sb(r, "hkv_lo", [P, DT, T], F32R)
            q_all = sb(s, "q_all", [P, DT, T])
            q_cur = sb(s, "q_cur", [P, 2, T])
            k_pad = sb(s, "k_pad", [P, 2, P + T])
            v_pad = sb(s, "v_pad", [P, NCH, 2, P])
            o_hi = sb(s, "o_hi", [P, DT, T], F32R)
            o_lo = sb(s, "o_lo", [P, DT, T], F32R)
            probs = sb(s, "probs", [P, 2, 4, 2 * P])
            probs_t = sb(s, "probs_t", [P, 2, 4, P])
            mask = sb(s, "mask", [P, 2, 2, 2 * P])
            ident_a = sb(s, "ident_a", [P, P])
            bq8 = sb(s, "bq8", [P, DT])
            gb_o = sb(s, "gb_o", [P, DT])
            stat4 = sb(s, "stat4", [P, 2, 6, 4])

        bank = [ctx.enter_context(nc.psum_tensor(f"bank{i}", [P, T], F32)) for i in range(8)]

        raw_loaded = [sem(f"raw_loaded{i}") for i in range(RING)]
        w_hi, w_lo, slab_used = sem("w_hi"), sem("w_lo"), sem("slab_used")
        in_loaded, x_loaded, ssm_loaded, att_loaded = sem("in_loaded"), sem("x_loaded"), sem("ssm_loaded"), sem("att_loaded")
        consts, c_ready = sem("consts"), sem("c_ready")
        mod_loaded = [sem("mod_loaded0"), sem("mod_loaded1")]
        mod_step, mod_mm, mod_col = sem("mod_step"), sem("mod_mm"), sem("mod_col")
        col_step = sem("col_step")
        ss_step, sq_ready, x_ready, stat_done, rs_step = (
            sem("ss_step"), sem("sq_ready"), sem("x_ready"), sem("stat_done"), sem("rs_step"))
        t_ready, h_hi_ready, h_lo_ready = sem("t_ready"), sem("h_hi_ready"), sem("h_lo_ready")
        silu_done, a_ready, a_hi_ready, a_lo_ready = (
            sem("silu_done"), sem("a_ready"), sem("a_hi_ready"), sem("a_lo_ready"))
        out_ready, out_stored = sem("out_ready"), sem("out_stored")

        block = ctx.enter_context(nc.Block())

        def load_slab(sp, n, slot):
            sp.wait_ge(w_lo, n - RING + 1)
            sp.dma_start(raw[:, slot, :], w_stream[n]).then_inc(raw_loaded[slot], 16)

        def prep_hi(act, b4, l, width=SLAB):
            s = l % RING
            act.wait_ge(raw_loaded[s], 16 * (b4 + l // RING) + 16)
            act.wait_ge(slab_used, 4 * b4 + l + 1)
            nc.scalar.activation(w_hi_sb[:, s, 0:width], raw[:, s, 0:width], ACT.Copy).then_inc(w_hi, 1)

        def prep_lo(dve, b4, l, width=SLAB):
            s = l % RING
            dve.wait_ge(w_hi, 4 * b4 + l + 1)
            nc.vector.tensor_tensor(w_lo_sb[:, s, 0:width], raw[:, s, 0:width], w_hi_sb[:, s, 0:width],
                                    ALU.subtract).then_inc(w_lo, 1)

        def product3(ps, s_hi, s_lo, m_hi, m_lo, start, stop):
            nc.tensor.matmul(ps, s_hi, m_hi, start=start, stop=False)
            nc.tensor.matmul(ps, s_hi, m_lo, start=False, stop=False)
            return nc.tensor.matmul(ps, s_lo, m_hi, start=False, stop=stop)

        def use_slab(pe, b4, l, ps, m_hi, m_lo, k0=0, tiles=8, ktiles=8, ready=None):
            s = l % RING
            pe.wait_ge(w_lo, 4 * b4 + l + 1)
            for k in range(tiles):
                if ready is not None:
                    ready(k0 + k)
                w = slice(k * P, (k + 1) * P)
                mm = product3(ps, w_hi_sb[:, s, w], w_lo_sb[:, s, w], m_hi[:, k0 + k, :], m_lo[:, k0 + k, :],
                              k0 + k == 0, k0 + k == ktiles - 1)
            mm.then_inc(slab_used, 1)

        def mod_block(dve, v, k):
            dve.wait_ge(mod_loaded[k % 2], 16 * (4 * v + k // 2) + 16)
            if k == 0:
                dve.wait_ge(mod_mm, v)
                nc.vector.tensor_scalar(mod_acc[:, :], mod_raw[:, 0, :], c_act[:, 0:1], None,
                                        ALU.mult).then_inc(mod_step, 1)
            else:
                dve.wait_ge(mod_step, 8 * v + k)
                nc.vector.scalar_tensor_tensor(mod_acc[:, :], mod_raw[:, k % 2, :], c_act[:, k:k + 1], mod_acc[:, :],
                                               ALU.mult, ALU.add).then_inc(mod_step, 1)

        def mod_sum(pe, v):
            pe.wait_ge(mod_step, 8 * v + 8)
            pe.wait_ge(mod_col, v)
            for j in range(DT):
                mm = nc.tensor.matmul(bank[7][:, j:j + 1], mod_acc[:, j * P:(j + 1) * P], ones[:, 0:1],
                                      start=True, stop=True)
            mm.then_inc(mod_mm, 1)

        def mod_collect(dve, v):
            dve.wait_ge(mod_mm, v + 1)
            b = cols[:, COLS["modb"][0]:COLS["modb"][1]].rearrange("p (v j) -> p v j", j=DT)
            nc.vector.tensor_tensor(mod[:, v, :], bank[7][:, 0:DT], b[:, v, :], ALU.add).then_inc(mod_col, 1)

        def load_mod(sp, m, slot, first=False):
            if not first:
                sp.wait_ge(mod_step, m - 1)
            sp.dma_start(mod_raw[:, slot, :], w_mod[m]).then_inc(mod_loaded[slot], 16)

        def square(act, st, j):
            nc.scalar.activation(tmp[:, 0, :], x[:, j, :], ACT.Square).then_inc(sq_ready, 1)

        def clear_sum(dve):
            nc.vector.memset(sumsq[:, :], 0.0).then_inc(ss_step, 1)

        def add_square(dve, st, j):
            dve.wait_ge(sq_ready, 8 * st + j + 1)
            dve.wait_ge(ss_step, 9 * st + j + 1)
            nc.vector.tensor_tensor(sumsq[:, :], sumsq[:, :], tmp[:, 0, :], ALU.add).then_inc(ss_step, 1)

        def stat_tensor(pe, st):
            pe.wait_ge(ss_step, 9 * (st + 1))
            nc.tensor.matmul(bank[6][:, :], ones[:, :], sumsq[:, :], start=True, stop=True).then_inc(stat_done, 1)

        def rstd_scalar(act, st):
            act.wait_ge(stat_done, st + 1)
            nc.scalar.activation(rstd[:, :], bank[6][:, :], ACT.Ln, bias=eps[:, 0:1], scale=1.0 / D).then_inc(rs_step, 1)
            act.wait_ge(rs_step, 2 * st + 1)
            nc.scalar.activation(rstd[:, :], rstd[:, :], ACT.Exp, scale=-0.5).then_inc(rs_step, 1)

        def columns_vector(dve, count, sc, w):
            nc.vector.scalar_tensor_tensor(scale_col[:, :], mod[:, sc, :], 1.0, w, ALU.add, ALU.mult).then_inc(col_step, 1)
            dve.wait_ge(col_step, count)

        def norm_vector(dve, st, hs, sh, hi, lo):
            def rest(j):
                dve.wait_ge(h_hi_ready, 8 * hs + j + 1)
                nc.vector.scalar_tensor_tensor(lo[:, j, :], tmp[:, j % 2, :], mod[:, sh, j:j + 1], hi[:, j, :],
                                               ALU.add, ALU.subtract).then_inc(h_lo_ready, 1)

            dve.wait_ge(rs_step, 2 * st + 2)
            for j in range(DT):
                if 8 * hs + j > 1:
                    dve.wait_ge(h_lo_ready, 8 * hs + j - 1)
                nc.vector.scalar_tensor_tensor(tmp[:, j % 2, :], x[:, j, :], scale_col[:, j:j + 1], rstd[:, :],
                                               ALU.mult, ALU.mult).then_inc(t_ready, 1)
                if j:
                    rest(j - 1)
            rest(DT - 1)

        def norm_scalar(act, hs, sh, hi):
            for j in range(DT):
                act.wait_ge(t_ready, 8 * hs + j + 1)
                nc.scalar.activation(hi[:, j, :], tmp[:, j % 2, :], ACT.Identity, bias=mod[:, sh, j:j + 1],
                                     ).then_inc(h_hi_ready, 1)

        def project_turns(eng, body, last, turn):
            turns = DT // body
            if not last:
                with eng.Fori(0, turns) as i:
                    turn(i, False)
            else:
                with eng.Fori(0, turns - 1) as i:
                    turn(i, False)
                turn(turns - 1, True)

        def widths(l, spj):
            return 6 * P if spj == DOWN_SPJ and l % spj == spj - 1 else SLAB

        def project_tensor(pe, n0, ktiles, spj, body, m_hi, m_lo, ready, st, last=False):
            def turn(i, _):
                b4 = n0 // 4 + i * (body * spj // RING)
                for jj in range(body):
                    if spj == 1:
                        pe.wait_ge(x_ready, 8 * (st - 1) + body * i + jj - 1)
                    for s in range(spj):
                        use_slab(pe, b4, jj * spj + s, bank[4 + jj % 2][:, :], m_hi, m_lo, 8 * s,
                                 min(8, ktiles - 8 * s), ktiles, ready if jj == 0 else None)
            project_turns(pe, body, last, turn)
            stat_tensor(pe, st)

        def project_scalar(act, n0, spj, body, st, last=False):
            def turn(i, end):
                b4 = n0 // 4 + i * (body * spj // RING)
                for jj in range(body):
                    for s in range(spj):
                        l = jj * spj + s + 2
                        if not end or l < body * spj:
                            prep_hi(act, b4, l, widths(l, spj))
                    j = body * i + jj
                    act.wait_ge(x_ready, 8 * (st - 1) + j + 1)
                    square(act, st, j)
            project_turns(act, body, last, turn)

        def project_vector(dve, n0, spj, body, gate, st, last=False):
            clear_sum(dve)

            def turn(i, end):
                b4 = n0 // 4 + i * (body * spj // RING)
                for jj in range(body):
                    for s in range(spj):
                        l = jj * spj + s + 2
                        if not end or l < body * spj:
                            prep_lo(dve, b4, l, widths(l, spj))
                    j = body * i + jj
                    dve.wait_ge(slab_used, RING + 4 * b4 + (jj + 1) * spj)
                    nc.vector.scalar_tensor_tensor(x[:, j, :], bank[4 + jj % 2][:, :], gate(j), x[:, j, :],
                                                   ALU.mult, ALU.add).then_inc(x_ready, 1)
                    add_square(dve, st, j)
            project_turns(dve, body, last, turn)

        def ffn_tensor(pe, k, n0, hs, st, mods, last=False):
            def turn(i, v):
                b4 = n0 // 4 + i
                for u in range(2):
                    use_slab(pe, b4, 2 * u, bank[2 * u][:, :], h_hi, h_lo,
                             ready=(lambda j: pe.wait_ge(h_lo_ready, 8 * hs + j + 1)) if u == 0 else None)
                    use_slab(pe, b4, 2 * u + 1, bank[2 * u + 1][:, :], h_hi, h_lo)
                if v is not None:
                    mod_sum(pe, v)
            with_mods(pe, mods, turn)
            project_tensor(pe, n0 + GU_SLABS, FT, DOWN_SPJ, 4, a_hi, a_lo,
                           lambda f: pe.wait_ge(a_lo_ready, FT * k + f + 1), st, last)

        def with_mods(eng, mods, turn):
            turns = FT // 2
            if len(mods):
                with eng.Fori(0, len(mods)) as i:
                    turn(i, mods[0] + i)
            if len(mods) < turns:
                with eng.Fori(len(mods), turns) as i:
                    turn(i, None)

        def ffn_scalar(act, k, n0, st, mods, last=False):
            def turn(i, v):
                b4 = n0 // 4 + i
                for u in range(2):
                    f = 2 * i + u
                    prep_hi(act, b4, 2 * u + 2)
                    prep_hi(act, b4, 2 * u + 3)
                    act.wait_ge(slab_used, RING + 4 * b4 + 2 * u + 1)
                    act.wait_ge(a_ready, FT * k + f)
                    nc.scalar.activation(tmp[:, 0, :], bank[2 * u][:, :], ACT.Silu).then_inc(silu_done, 1)
                    act.wait_ge(a_ready, FT * k + f + 1)
                    nc.scalar.activation(a_hi[:, f, :], tmp[:, 1, :], ACT.Copy).then_inc(a_hi_ready, 1)
            with_mods(act, mods, turn)
            project_scalar(act, n0 + GU_SLABS, DOWN_SPJ, 4, st, last)

        def ffn_vector(dve, k, n0, g, st, mods, cols_before, last=False):
            def turn(i, v):
                b4 = n0 // 4 + i
                for u in range(2):
                    f = 2 * i + u
                    prep_lo(dve, b4, 2 * u + 2)
                    if v is not None:
                        mod_block(dve, v, 4 * u)
                    prep_lo(dve, b4, 2 * u + 3)
                    if v is not None:
                        for q in range(1, 4):
                            mod_block(dve, v, 4 * u + q)
                    dve.wait_ge(silu_done, FT * k + f + 1)
                    dve.wait_ge(slab_used, RING + 4 * b4 + 2 * u + 2)
                    dve.wait_ge(a_lo_ready, FT * k + f)
                    nc.vector.tensor_tensor(tmp[:, 1, :], tmp[:, 0, :], bank[2 * u + 1][:, :],
                                            ALU.mult).then_inc(a_ready, 1)
                    dve.wait_ge(a_hi_ready, FT * k + f + 1)
                    nc.vector.tensor_tensor(a_lo[:, f, :], tmp[:, 1, :], a_hi[:, f, :],
                                            ALU.subtract).then_inc(a_lo_ready, 1)
                if v is not None:
                    mod_collect(dve, v)
            with_mods(dve, mods, turn)
            dve.wait_ge(mod_col, min(g + 1, NMOD))
            nc.vector.tensor_scalar(gate_col[:, :], mod[:, g, :], 0.5, None, ALU.mult).then_inc(col_step, 1)
            dve.wait_ge(col_step, cols_before + 1)
            project_vector(dve, n0 + GU_SLABS, DOWN_SPJ, 4, lambda j: gate_col[:, bass.ds(j, 1)], st, last)

        wdt_split, dtp_done, soft_act, soft_dve, dec_done = (
            sem("wdt_split"), sem("dtp_done"), sem("soft_act"), sem("soft_dve"), sem("dec_done"))
        ssm_consts = sem("ssm_consts")
        z_read, conv_init, conv_step = sem("z_read"), sem("conv_init"), sem("conv_step")
        silu_x, silu_z = sem("silu_x"), sem("silu_z")
        ta_ready, turned, seg_ready, sum_ready = sem("ta_ready"), sem("turned"), sem("seg_ready"), sem("sum_ready")
        el_ready, ee_ready = sem("el_ready"), sem("ee_ready")
        cd_ready = sem("cd_ready")
        g_ready, mixed, y_done, st_done, state_ready = (
            sem("g_ready"), sem("mixed"), sem("y_done"), sem("st_done"), sem("state_ready"))
        gate_step, gsq_ready, gstat_done, grs_step = (
            sem("gate_step"), sem("gsq_ready"), sem("gstat_done"), sem("grs_step"))
        yn_ready, y_hi_ready, y_lo_ready = sem("yn_ready"), sem("y_hi_ready"), sem("y_lo_ready")

        cb = bank[4][:, 3 * P:4 * P]
        chunk = [slice(c * P, (c + 1) * P) for c in range(NCH)]

        def scan_a_tensor(pe, g, pp, c):
            if c == 0:
                pe.wait_ge(silu_x, 4 * g + 4)
                pe.wait_ge(ssm_consts, 6)
            for i in range(2):
                nc.tensor.transpose(bank[4][:, i * P:(i + 1) * P], xs[:, pp, i, chunk[c]], ident[:, :])
            nc.tensor.transpose(bank[4][:, 2 * P:3 * P], bc[:, pp, 0, chunk[c]], ident[:, :])
            nc.tensor.matmul(cb, bc[:, pp, 0, chunk[c]], bc[:, pp, 1, chunk[c]], start=True, stop=True).then_inc(turned, 1)
            pe.wait_ge(ta_ready, 4 * g + c + 1)
            tav = ta[:, :, :].rearrange("p h l -> p (h l)")
            nc.tensor.matmul(bank[5][:, :], after[:, :], tav, start=True, stop=True).then_inc(seg_ready, 1)
            nc.tensor.matmul(bank[6][:, :], ones[:, :], tav, start=True, stop=True).then_inc(sum_ready, 1)

        def scan_b_tensor(pe, g, c):
            pe.wait_ge(mixed, 4 * g + c + 1)
            if c:
                pe.wait_ge(state_ready, 3 * g + c)
            for pair in range(2):
                ps = bank[2 + pair][:, chunk[c]]
                for r in range(2):
                    mm = nc.tensor.matmul(ps, x_pad[:, r, pair, :], el[:, 2 * pair + r, :],
                                          start=(r == 0), stop=(c == 0 and r == 1))
                if c:
                    for r in range(2):
                        mm = nc.tensor.matmul(ps, state[:, r, pair, :], ee[:, 2 * pair + r, :],
                                              start=False, stop=(r == 1))
            mm.then_inc(y_done, 1)
            if c < NCH - 1:
                nc.tensor.matmul(bank[7][:, 0:HPG * HDIM], b_tok[:, :], x_dec[:, :, :].rearrange("p h d -> p (h d)"),
                                 start=True, stop=True).then_inc(st_done, 1)

        def ssm_tensor(pe):
            n4 = S_IN // 4
            ready = lambda j: pe.wait_ge(h_lo_ready, 8 * 1 + j + 1)
            for l in range(4):
                if l >= 2:
                    pe.wait_ge(conv_step, 3 * (l - 1))
                use_slab(pe, n4, l, bank[l % 2][:, :], h_hi, h_lo, ready=ready)
            pe.wait_ge(wdt_split, 2)
            for c in range(NCH):
                for k in range(DT):
                    mm = product3(bank[4][:, c * HEADS:(c + 1) * HEADS], h_hi[:, k, chunk[c]], h_lo[:, k, chunk[c]],
                                  wdt_hi[:, k, :], wdt_lo[:, k, :], k == 0, k == DT - 1)
            mm.then_inc(dtp_done, 1)
            pe.wait_ge(soft_dve, SOFT_A + 1)
            pe.wait_ge(ssm_consts, 6)
            nc.tensor.matmul(bank[5][:, 0:NCH * HEADS], after[:, :], a_tok[:, :, :].rearrange("p c h -> p (c h)"),
                             start=True, stop=True).then_inc(dec_done, 1)

            def group(i, pp, last=False):
                g = 2 * i + pp
                b4 = n4 + 1 + 3 * i

                def slab(s):
                    if s < 2:
                        pe.wait_ge(conv_step, 3 * (4 * g + 3 + s))
                    elif s < 4:
                        pe.wait_ge(z_read, 2 * g + s - 1)
                    else:
                        pe.wait_ge(conv_step, 3 * (4 * g + 1 + s))
                    use_slab(pe, b4, 6 * pp + s, bank[s % 2][:, :], h_hi, h_lo)

                slab(0)
                scan_a_tensor(pe, g, pp, 0)
                slab(1)
                for c in range(NCH):
                    if c and not last:
                        slab(c + 1)
                    scan_b_tensor(pe, g, c)
                    if c < NCH - 1:
                        scan_a_tensor(pe, g, pp, c + 1)
                if not last:
                    slab(5)
                for t in range(2):
                    pe.wait_ge(gsq_ready, 2 * g + t + 1)
                    mm = nc.tensor.matmul(bank[7][:, :], ones[:, :], zs[:, t, :], start=(t == 0), stop=(t == 1))
                mm.then_inc(gstat_done, 1)

            with pe.Fori(0, GROUPS // 2 - 1) as i:
                group(i, 0)
                group(i, 1)
            group(GROUPS // 2 - 1, 0)
            group(GROUPS // 2 - 1, 1, last=True)
            project_tensor(pe, S_OUT, 16, 2, 2, y_hi, y_lo, lambda f: pe.wait_ge(y_lo_ready, f + 1), 2)

        SOFT_A = 17

        def conv_cols(g, t, tap):
            v = ssm_cols[:, 0:SSM_CONV].rearrange("p (g t k) -> p g t k", g=GROUPS, t=4)
            return v[:, g, t, tap:tap + 1]

        def conv_tile(pp, t):
            return xs[:, pp, t, :] if t < 2 else bc[:, pp, t - 2, :]

        def conv_scalar(act, g, pp, t, used):
            act.wait_ge(slab_used, used)
            nc.scalar.activation(conv_tile(pp, t), bank[t % 2][:, :], ACT.Identity, bias=conv_cols(g, t, 4),
                                 scale=conv_cols(g, t, 3)).then_inc(conv_init, 1)

        def conv_vector(dve, g, pp, t):
            y = conv_tile(pp, t)
            dve.wait_ge(conv_init, 4 * g + t + 1)
            for back in range(1, 4):
                if back > 1:
                    dve.wait_ge(conv_step, 3 * (4 * g + t) + back - 1)
                nc.vector.scalar_tensor_tensor(y[:, back:], bank[t % 2][:, 0:T - back], conv_cols(g, t, 3 - back),
                                               y[:, back:], ALU.mult, ALU.add).then_inc(conv_step, 1)

        def silu_tiles(act, g, pp, tiles):
            for t in tiles:
                act.wait_ge(conv_step, 3 * (4 * g + t + 1))
                nc.scalar.activation(conv_tile(pp, t), conv_tile(pp, t), ACT.Silu).then_inc(silu_x, 1)

        def ssm_scalar(act):
            n4 = S_IN // 4
            act.wait_ge(ssm_loaded, 48)
            for l in range(4):
                prep_hi(act, n4, l + 2)
                conv_scalar(act, 0, 0, l, RING + S_IN + l + 1)
                if l == 0:
                    nc.scalar.activation(wdt_hi[:, :, :], wdt[:, :, :], ACT.Copy).then_inc(wdt_split, 1)
            silu_tiles(act, 0, 0, range(4))
            act.wait_ge(soft_dve, 2)
            nc.scalar.activation(soft[:, 2, :], soft[:, 1, :], ACT.Exp).then_inc(soft_act, 1)
            nc.scalar.activation(ssm_rows[:, HEADS:2 * HEADS], ssm_rows[:, HEADS:2 * HEADS], ACT.Exp).then_inc(soft_act, 1)
            act.wait_ge(dec_done, 1)
            nc.scalar.activation(dd_tok[:, :, :].rearrange("p c h -> p (c h)"), bank[5][:, 0:NCH * HEADS],
                                 ACT.Exp).then_inc(soft_act, 1)

            def group(i, pp, last=False):
                g = 2 * i + pp
                b4 = n4 + 1 + 3 * i
                used = RING + 4 * b4 + 6 * pp

                def z_copy(t):
                    act.wait_ge(slab_used, used + t + 1)
                    if t == 0:
                        act.wait_ge(gstat_done, g)
                    nc.scalar.activation(zs[:, t, :], bank[t][:, :], ACT.Copy).then_inc(z_read, 1)

                def scan(c):
                    act.wait_ge(seg_ready, 4 * g + c + 1)
                    nc.scalar.activation(el[:, :, :].rearrange("p h l -> p (h l)"), bank[5][:, :],
                                         ACT.Exp).then_inc(el_ready, 1)
                    act.wait_ge(sum_ready, 4 * g + c + 1)
                    nc.scalar.activation(ee[:, :, :].rearrange("p h l -> p (h l)"), bank[6][:, :],
                                         ACT.Exp).then_inc(ee_ready, 1)

                for s in range(6):
                    if not last or s < 2:
                        prep_hi(act, b4, 6 * pp + s + 2)
                    if not last and s >= 3:
                        conv_scalar(act, g + 1, 1 - pp, s - 3, used + s)
                    if 1 <= s <= 2:
                        z_copy(s - 1)
                    if 1 <= s <= 4:
                        scan(s - 1)
                for t in range(2):
                    act.wait_ge(z_read, 2 * g + t + 1)
                    nc.scalar.activation(zs[:, t, :], zs[:, t, :], ACT.Silu).then_inc(silu_z, 1)
                if not last:
                    silu_tiles(act, g + 1, 1 - pp, range(2))
                for t in range(2):
                    act.wait_ge(gate_step, 4 * g + 2 * t + 2)
                    nc.scalar.activation(zs[:, t, :], tmp[:, t, :], ACT.Square).then_inc(gsq_ready, 1)
                if not last:
                    conv_scalar(act, g + 1, 1 - pp, 3, used + 6)
                    silu_tiles(act, g + 1, 1 - pp, range(2, 4))
                act.wait_ge(gstat_done, g + 1)
                nc.scalar.activation(rstd[:, :], bank[7][:, :], ACT.Ln, bias=eps[:, 0:1],
                                     scale=1.0 / (2 * P)).then_inc(grs_step, 1)
                act.wait_ge(grs_step, 2 * g + 1)
                nc.scalar.activation(rstd[:, :], rstd[:, :], ACT.Exp, scale=-0.5).then_inc(grs_step, 1)
                for t in range(2):
                    act.wait_ge(yn_ready, 2 * g + t + 1)
                    nc.scalar.activation(y_hi[:, 2 * g + t, :], tmp[:, t, :], ACT.Copy).then_inc(y_hi_ready, 1)

            with act.Fori(0, GROUPS // 2 - 1) as i:
                group(i, 0)
                group(i, 1)
            group(GROUPS // 2 - 1, 0)
            group(GROUPS // 2 - 1, 1, last=True)
            project_scalar(act, S_OUT, 2, 2, 2)

        def ssm_vector(dve):
            n4 = S_IN // 4
            dve.wait_ge(ssm_loaded, 48)
            step = [0]

            def link(ins):
                step[0] += 1
                ins.then_inc(soft_dve, 1)
                dve.wait_ge(soft_dve, step[0])

            for l in range(4):
                prep_lo(dve, n4, l + 2)
                conv_vector(dve, 0, 0, l)
                if l == 0:
                    dve.wait_ge(wdt_split, 1)
                    nc.vector.tensor_tensor(wdt_lo[:, :, :], wdt[:, :, :], wdt_hi[:, :, :],
                                            ALU.subtract).then_inc(wdt_split, 1)
            v, na, e, sv, s2 = (soft[:, q, :] for q in range(5))
            dtv = dt_tok[:, :, :].rearrange("p c h -> p (c h)")
            bias = ssm_rows[:, 0:HEADS].unsqueeze(1).broadcast_to([P, NCH, HEADS])
            dve.wait_ge(dtp_done, 1)
            link(nc.vector.tensor_tensor(v.rearrange("p (c h) -> p c h", c=NCH),
                                         bank[4][:, 0:NCH * HEADS].rearrange("p (c h) -> p c h", c=NCH), bias, ALU.add))
            link(nc.vector.scalar_tensor_tensor(na, v, -1.0, v, ALU.mult, ALU.min))
            dve.wait_ge(soft_act, 1)
            link(nc.vector.tensor_scalar(sv, e, 2.0, None, ALU.add))
            link(nc.vector.reciprocal(na, sv))
            link(nc.vector.tensor_tensor(sv, e, na, ALU.mult))
            link(nc.vector.tensor_tensor(s2, sv, sv, ALU.mult))
            link(nc.vector.tensor_scalar(na, s2, 1.0 / 17, None, ALU.mult))
            for odd in (15, 13, 11, 9, 7, 5, 3):
                link(nc.vector.scalar_tensor_tensor(na, na, 1.0 / odd, s2, ALU.add, ALU.mult))
            link(nc.vector.scalar_tensor_tensor(na, na, 1.0, sv, ALU.add, ALU.mult))
            link(nc.vector.tensor_scalar(v, v, 0.0, None, ALU.max))
            link(nc.vector.scalar_tensor_tensor(dtv, na, 2.0, v, ALU.mult, ALU.add))
            dve.wait_ge(soft_act, 2)
            ea = ssm_rows[:, HEADS:2 * HEADS].unsqueeze(1).broadcast_to([P, NCH, HEADS])
            nc.vector.scalar_tensor_tensor(a_tok[:, :, :], dt_tok[:, :, :], -1.0, ea, ALU.mult, ALU.mult).then_inc(soft_dve, 1)
            dve.wait_ge(soft_dve, SOFT_A + 1)
            dve.wait_ge(soft_act, 3)
            nc.vector.tensor_tensor(dd_tok[:, :, :], dd_tok[:, :, :], dt_tok[:, :, :], ALU.mult).then_inc(soft_dve, 1)
            nc.vector.memset(x_pad[:, :, :, :], 0.0).then_inc(soft_dve, 1)
            nc.vector.memset(state[:, :, :, :], 0.0).then_inc(soft_dve, 1)
            dve.wait_ge(soft_dve, SOFT_A + 4)
            dve.wait_ge(ssm_consts, 6)

            def by_head(tok, c, g):
                return tok[:, c, :].rearrange("p (g h) -> p g h", h=HPG)[:, g, :]

            def group(i, pp, last=False):
                g = 2 * i + pp
                b4 = n4 + 1 + 3 * i

                def decays(c):
                    a = by_head(a_tok, c, g).unsqueeze(2).broadcast_to([P, HPG, P])
                    nc.vector.tensor_tensor(ta[:, :, :], upto[:, :].unsqueeze(1).broadcast_to([P, HPG, P]), a,
                                            ALU.mult).then_inc(ta_ready, 1)

                def mix(c):
                    dve.wait_ge(turned, 4 * g + c + 1)
                    xt = bank[4][:, 0:2 * P].rearrange("p (q r d) -> p q r d", q=2, r=2)
                    dt = by_head(dt_tok, c, g).rearrange("p (q r) -> p q r", q=2)
                    for r in range(2):
                        nc.vector.tensor_tensor(x_pad[:, r, :, r * HDIM:(r + 1) * HDIM], xt[:, :, r, :],
                                                dt[:, :, r].unsqueeze(2).broadcast_to([P, 2, HDIM]), ALU.mult)
                    dd = by_head(dd_tok, c, g).unsqueeze(2).broadcast_to([P, HPG, HDIM])
                    nc.vector.tensor_tensor(x_dec[:, :, :], bank[4][:, 0:2 * P].rearrange("p (h d) -> p h d", h=HPG), dd,
                                            ALU.mult)
                    nc.vector.tensor_copy(b_tok[:, :], bank[4][:, 2 * P:3 * P])
                    nc.vector.tensor_tensor(gm_t[:, :], cb, upto[:, :], ALU.mult).then_inc(g_ready, 1)
                    dve.wait_ge(g_ready, 4 * g + c + 1)
                    dve.wait_ge(el_ready, 4 * g + c + 1)
                    nc.vector.tensor_tensor(el[:, :, :], el[:, :, :], gm_t[:, :].unsqueeze(1).broadcast_to([P, HPG, P]),
                                            ALU.mult)
                    dve.wait_ge(ee_ready, 4 * g + c + 1)
                    nc.vector.tensor_copy(chunk_dec[:, :], ee[:, :, P - 1]).then_inc(cd_ready, 1)
                    dve.wait_ge(cd_ready, 4 * g + c + 1)
                    nc.vector.tensor_tensor(ee[:, :, :], ee[:, :, :],
                                            bc[:, pp, 1, chunk[c]].unsqueeze(1).broadcast_to([P, HPG, P]),
                                            ALU.mult).then_inc(mixed, 1)

                def carry(c):
                    dve.wait_ge(st_done, 3 * g + c + 1)
                    dve.wait_ge(mixed, 4 * g + c + 1)
                    for h in range(HPG):
                        r = h % 2
                        cur = state[:, r, h // 2, r * HDIM:(r + 1) * HDIM]
                        new = bank[7][:, h * HDIM:(h + 1) * HDIM]
                        if c == 0:
                            last_op = nc.vector.tensor_copy(cur, new)
                        else:
                            last_op = nc.vector.scalar_tensor_tensor(cur, cur, chunk_dec[:, h:h + 1], new,
                                                                     ALU.mult, ALU.add)
                    last_op.then_inc(state_ready, 1)
                    dve.wait_ge(state_ready, 3 * g + c + 1)

                for s in range(6):
                    if not last or s < 2:
                        prep_lo(dve, b4, 6 * pp + s + 2)
                    if not last and s >= 3:
                        conv_vector(dve, g + 1, 1 - pp, s - 3)
                    if 2 <= s <= 4:
                        carry(s - 2)
                    if 1 <= s <= 4:
                        mix(s - 1)
                    if s == 0:
                        decays(0)
                    if 1 <= s <= 3:
                        decays(s)
                dve.wait_ge(y_done, 4 * g + NCH)
                dve.wait_ge(silu_z, 2 * g + 2)
                dve.wait_ge(y_lo_ready, 2 * g)
                for t in range(2):
                    nc.vector.scalar_tensor_tensor(tmp[:, t, :], xs[:, pp, t, :],
                                                   ssm_cols[:, bass.ds(2 * g + (SSM_CONV + t), 1)],
                                                   bank[2 + t][:, :], ALU.mult, ALU.add).then_inc(gate_step, 1)
                    dve.wait_ge(gate_step, 4 * g + 2 * t + 1)
                    nc.vector.tensor_tensor(tmp[:, t, :], tmp[:, t, :], zs[:, t, :], ALU.mult).then_inc(gate_step, 1)
                if not last:
                    conv_vector(dve, g + 1, 1 - pp, 3)
                dve.wait_ge(grs_step, 2 * g + 2)
                for t in range(2):
                    dve.wait_ge(gate_step, 4 * g + 2 * t + 2)
                    nc.vector.scalar_tensor_tensor(tmp[:, t, :], tmp[:, t, :],
                                                   ssm_cols[:, bass.ds(2 * g + (SSM_CONV + 16 + t), 1)],
                                                   rstd[:, :], ALU.mult, ALU.mult).then_inc(yn_ready, 1)
                for t in range(2):
                    dve.wait_ge(y_hi_ready, 2 * g + t + 1)
                    nc.vector.tensor_tensor(y_lo[:, 2 * g + t, :], tmp[:, t, :], y_hi[:, 2 * g + t, :],
                                            ALU.subtract).then_inc(y_lo_ready, 1)

            with dve.Fori(0, GROUPS // 2 - 1) as i:
                group(i, 0)
                group(i, 1)
            group(GROUPS // 2 - 1, 0)
            group(GROUPS // 2 - 1, 1, last=True)
            project_vector(dve, S_OUT, 2, 2, lambda j: mod[:, M_GMA, bass.ds(j, 1)], 2)

        k_ready, v_ready = sem("k_ready"), sem("v_ready")

        def kv_tensor(pe):
            n4 = S_KV // 4
            ready = lambda j: pe.wait_ge(h_lo_ready, 8 * 3 + j + 1)
            for l in range(2):
                use_slab(pe, n4, l, bank[l][:, :], hkv_hi, hkv_lo, ready=ready)
            for l in range(2, 4):
                pe.wait_ge(w_lo, 4 * n4 + l + 1)
                for c in range(NCH):
                    for k in range(DT):
                        w = slice(k * P, (k + 1) * P)
                        mm = product3(bank[l][:, chunk[c]], hkv_hi[:, k, chunk[c]], hkv_lo[:, k, chunk[c]],
                                      w_hi_sb[:, l, w], w_lo_sb[:, l, w], k == 0, k == DT - 1)
                mm.then_inc(slab_used, 1)

        def kv_scalar(act):
            n4 = S_KV // 4
            for l in range(4):
                prep_hi(act, n4, l + 2)
                if l < 2:
                    act.wait_ge(slab_used, RING + S_KV + l + 1)
                    b = COLS["b_k"][0] + l
                    nc.scalar.activation(k_all[:, l, :], bank[l][:, :], ACT.Identity, bias=cols[:, b:b + 1]).then_inc(k_ready, 1)

        def kv_vector(dve):
            n4 = S_KV // 4
            dve.wait_ge(att_loaded, 16)
            for l in range(4):
                prep_lo(dve, n4, l + 2)
                if l >= 2:
                    dve.wait_ge(slab_used, RING + S_KV + l + 1)
                    o = slice((l - 2) * P, (l - 1) * P)
                    nc.vector.tensor_tensor(v_all[:, :, o], bank[l][:, :].rearrange("p (c d) -> p c d", c=NCH),
                                            att_rows[:, o].unsqueeze(1).broadcast_to([P, NCH, P]),
                                            ALU.add).then_inc(v_ready, 1)

        att_consts, bq_ready, q_ready, gb_step = sem("att_consts"), sem("bq_ready"), sem("q_ready"), sem("gb_step")
        pad_ready, q_cur_ready, scored = sem("pad_ready"), sem("q_cur_ready"), sem("scored")
        masked, max_step, exp_ready, sink_exp = sem("masked"), sem("max_step"), sem("exp_ready"), sem("sink_exp")
        den_step, normed, probs_turned = sem("den_step"), sem("normed"), sem("probs_turned")
        pt_a_ready, pt_b_ready, o_done, o_hi_ready, o_lo_ready = (
            sem("pt_a_ready"), sem("pt_b_ready"), sem("o_done"), sem("o_hi_ready"), sem("o_lo_ready"))

        def att_tensor(pe):
            ready = lambda j: pe.wait_ge(h_lo_ready, 8 * 5 + j + 1)
            with pe.Fori(0, 2) as i:
                for t in range(4):
                    if t >= 2:
                        pe.wait_ge(q_ready, 4 * i + t - 1)
                    else:
                        pe.wait_ge(q_ready, 4 * i)
                    use_slab(pe, S_Q // 4 + i, t, bank[t % 2][:, :], h_hi, h_lo, ready=ready)
            pe.wait_ge(att_consts, 6)

            def unit(kt, tt, half):
                u = 8 * kt + 2 * tt + half
                if tt == 0 and half == 0:
                    pe.wait_ge(pad_ready, 3 * kt + 3)
                if half == 0:
                    pe.wait_ge(q_cur_ready, 4 * kt + tt + 1)
                pe.wait_ge(masked, 2 * u)
                for ab in range(2):
                    for b in range(2):
                        q0 = (2 * half + b) * P
                        mm = nc.tensor.matmul(bank[2 + ab][:, b * 2 * P:(b + 1) * 2 * P], q_cur[:, tt % 2, q0:q0 + P],
                                              k_pad[:, ab, q0:q0 + 2 * P], start=True, stop=True)
                    mm.then_inc(scored, 1)

            def values(kt, tt, half):
                u = 8 * kt + 2 * tt + half
                pe.wait_ge(normed, u + 1)
                for ab in range(2):
                    for b in range(2):
                        for part in range(2):
                            if half == 0 and b == 0 and part == 0:
                                continue
                            mm = nc.tensor.transpose(bank[4 + ab][:, (2 * b + part) * P:(2 * b + part + 1) * P],
                                                     probs[:, half, 2 * ab + b, part * P:(part + 1) * P], ident_a[:, :])
                    mm.then_inc(probs_turned, 1)
                pe.wait_ge(pt_a_ready, u + 1)
                pe.wait_ge(pt_b_ready, u + 1)
                if half == 0:
                    pe.wait_ge(o_lo_ready, 4 * kt + tt)
                for b in range(2):
                    blk = 2 * half + b
                    parts = [(ab, part) for part in range(2) for ab in range(2) if blk + part > 0]
                    for n, (ab, part) in enumerate(parts):
                        mm = nc.tensor.matmul(bank[7][:, blk * P:(blk + 1) * P], v_pad[:, blk - 1 + part, ab, :],
                                              probs_t[:, ab, 2 * b + part, :], start=(n == 0), stop=(n == len(parts) - 1))
                mm.then_inc(o_done, 1)

            with pe.Fori(0, 2) as kt:
                unit(kt, 0, 0)
                for n in range(8):
                    if n < 7:
                        unit(kt, (n + 1) // 2, (n + 1) % 2)
                    values(kt, n // 2, n % 2)
            project_tensor(pe, S_O, 8, 1, 4, o_hi, o_lo, lambda f: pe.wait_ge(o_lo_ready, f + 1), 5)

        def att_scalar(act):
            act.wait_ge(bq_ready, 1)
            with act.Fori(0, 2) as i:
                for t in range(4):
                    prep_hi(act, S_Q // 4 + i, t + 2)
                    act.wait_ge(slab_used, RING + S_Q + 4 * i + t + 1)
                    nc.scalar.activation(q_all[:, 4 * i + t, :], bank[t % 2][:, :], ACT.Identity,
                                         bias=bq8[:, bass.ds(4 * i + t, 1)], scale=HDIM ** -0.5).then_inc(q_ready, 1)
            act.wait_ge(q_ready, 8)

            def copy_q(kt, tt):
                if tt >= 2:
                    act.wait_ge(scored, 2 * (8 * kt + 2 * tt - 2))
                else:
                    act.wait_ge(scored, 16 * kt)
                nc.scalar.activation(q_cur[:, tt % 2, :], q_all[:, 4 * kt + tt, :], ACT.Copy).then_inc(q_cur_ready, 1)

            def unit(kt, tt, half):
                u = 8 * kt + 2 * tt + half
                st = stat4[:, half, :, :]
                act.wait_ge(max_step, 4 * u + 4)
                for n in range(4):
                    nc.scalar.activation(probs[:, half, n, :], probs[:, half, n, :], ACT.Exp, bias=st[:, 1, n:n + 1],
                                         accum_out=st[:, 3, n:n + 1]).then_inc(exp_ready, 1)
                nc.scalar.activation(st[:, 2, :], st[:, 2, :], ACT.Exp).then_inc(sink_exp, 1)

            def turned_a(kt, tt, half):
                u = 8 * kt + 2 * tt + half
                lo = P if half == 0 else 0
                act.wait_ge(probs_turned, 2 * u + 2)
                nc.scalar.activation(probs_t[:, 0, :, :].rearrange("p n q -> p (n q)")[:, lo:], bank[4][:, lo:],
                                     ACT.Copy).then_inc(pt_a_ready, 1)
                if half == 1:
                    act.wait_ge(o_done, u + 1)
                    nc.scalar.activation(o_hi[:, 4 * kt + tt, :], bank[7][:, :], ACT.Copy).then_inc(o_hi_ready, 1)

            with act.Fori(0, 2) as kt:
                copy_q(kt, 0)
                copy_q(kt, 1)
                unit(kt, 0, 0)
                for n in range(8):
                    if n < 7:
                        unit(kt, (n + 1) // 2, (n + 1) % 2)
                    if n in (2, 4):
                        copy_q(kt, n // 2 + 1)
                    turned_a(kt, n // 2, n % 2)
            project_scalar(act, S_O, 1, 4, 5)

        def att_vector(dve):
            b = COLS["b_q"][0]
            nc.vector.tensor_scalar(bq8[:, :], cols[:, b:b + DT], HDIM ** -0.5, None, ALU.mult).then_inc(bq_ready, 1)
            nc.vector.tensor_tensor(gb_o[:, :], mod[:, M_GMB, :], col("b_o"), ALU.mult).then_inc(gb_step, 1)
            dve.wait_ge(gb_step, 1)
            for j in range(DT):
                nc.vector.tensor_scalar(x[:, j, :], x[:, j, :], gb_o[:, j:j + 1], None, ALU.add).then_inc(gb_step, 1)
            with dve.Fori(0, 2) as i:
                for t in range(4):
                    prep_lo(dve, S_Q // 4 + i, t + 2)
            dve.wait_ge(att_consts, 8)
            dve.wait_ge(k_ready, 2)
            dve.wait_ge(v_ready, 2)

            def pads(kt):
                dve.wait_ge(o_done, 8 * kt)
                for ab in range(2):
                    half = slice(ab * HDIM, (ab + 1) * HDIM)
                    nc.vector.tensor_copy(k_pad[half, ab, P:], k_all[half, kt, :]).then_inc(pad_ready, 1)
                v = v_all[:, :, :].rearrange("p c (k d) -> p c k d", k=2)
                for ab in range(2):
                    half = slice(ab * HDIM, (ab + 1) * HDIM)
                    op = nc.vector.tensor_copy(v_pad[:, :, ab, half], v[:, :, kt, half])
                op.then_inc(pad_ready, 1)

            def scores(kt, tt, half):
                u = 8 * kt + 2 * tt + half
                st = stat4[:, half, :, :]
                for ab in range(2):
                    dve.wait_ge(scored, 2 * u + ab + 1)
                    nc.vector.tensor_tensor(probs[:, half, 2 * ab:2 * ab + 2, :],
                                            bank[2 + ab][:, :].rearrange("p (b k) -> p b k", b=2), mask[:, half, :, :],
                                            ALU.add).then_inc(masked, 1)
                dve.wait_ge(masked, 2 * u + 2)
                nc.vector.tensor_reduce(st[:, 0, :], probs[:, half, :, :], AX.X, ALU.max).then_inc(max_step, 1)
                dve.wait_ge(max_step, 4 * u + 1)
                sink = att_rows[:, KV * HDIM:].rearrange("p (t a) -> p t a", a=2)[:, 4 * kt + tt, :]
                sink = sink.unsqueeze(2).broadcast_to([P, 2, 2])
                four = lambda r: st[:, r, :].rearrange("p (a b) -> p a b", a=2)
                nc.vector.tensor_tensor(four(0), four(0), sink, ALU.max).then_inc(max_step, 1)
                dve.wait_ge(max_step, 4 * u + 2)
                nc.vector.tensor_scalar(st[:, 1, :], st[:, 0, :], -1.0, None, ALU.mult).then_inc(max_step, 1)
                nc.vector.tensor_tensor(four(2), sink, four(0), ALU.subtract).then_inc(max_step, 1)

            def normalise(kt, tt, half):
                u = 8 * kt + 2 * tt + half
                st = stat4[:, half, :, :]
                dve.wait_ge(exp_ready, 4 * u + 4)
                dve.wait_ge(sink_exp, u + 1)
                nc.vector.tensor_tensor(st[:, 4, :], st[:, 3, :], st[:, 2, :], ALU.add).then_inc(den_step, 1)
                dve.wait_ge(den_step, 2 * u + 1)
                nc.vector.reciprocal(st[:, 5, :], st[:, 4, :]).then_inc(den_step, 1)
                dve.wait_ge(den_step, 2 * u + 2)
                for n in range(4):
                    op = nc.vector.tensor_scalar(probs[:, half, n, :], probs[:, half, n, :], st[:, 5, n:n + 1], None, ALU.mult)
                op.then_inc(normed, 1)

            def turned_b(kt, tt, half):
                u = 8 * kt + 2 * tt + half
                lo = P if half == 0 else 0
                dve.wait_ge(probs_turned, 2 * u + 2)
                nc.vector.tensor_copy(probs_t[:, 1, :, :].rearrange("p n q -> p (n q)")[:, lo:],
                                      bank[5][:, lo:]).then_inc(pt_b_ready, 1)
                if half == 1:
                    dve.wait_ge(o_hi_ready, 4 * kt + tt + 1)
                    nc.vector.tensor_tensor(o_lo[:, 4 * kt + tt, :], bank[7][:, :], o_hi[:, 4 * kt + tt, :],
                                            ALU.subtract).then_inc(o_lo_ready, 1)

            with dve.Fori(0, 2) as kt:
                pads(kt)
                scores(kt, 0, 0)
                for n in range(8):
                    normalise(kt, n // 2, n % 2)
                    if n < 7:
                        scores(kt, (n + 1) // 2, (n + 1) % 2)
                    turned_b(kt, n // 2, n % 2)
            dve.wait_ge(gb_step, 9)
            project_vector(dve, S_O, 1, 4, lambda j: mod[:, M_GMB, bass.ds(j, 1)], 5)

        mods0 = range(MOD_FIRST, MOD_FIRST + MOD_IN_FFN0)
        mods1 = range(MOD_FIRST + MOD_IN_FFN0, NMOD)

        @block.sync
        def _(sp):
            sp.dma_start(cols[:, :], cols_in).then_inc(in_loaded, 16)
            load_mod(sp, 0, 0, first=True)
            load_mod(sp, 1, 1, first=True)
            sp.dma_start(x[:, :, :].rearrange("p j t -> p (j t)"), x_in).then_inc(x_loaded, 16)
            for m in range(2, 8 * MOD_FIRST):
                load_mod(sp, m, m % 2)
                if m >= 10 and m < 10 + RING:
                    sp.dma_start(raw[:, m - 10, :], w_stream[m - 10]).then_inc(raw_loaded[m - 10], 16)
            for n in (4, 5):
                load_slab(sp, n, n % RING)

            def slabs_and_mods(n0, m0, turns):
                with sp.Fori(0, turns) as i:
                    for u in range(2):
                        load_slab(sp, 4 * i + (n0 + 2 * u), (n0 + 2 * u) % RING)
                        load_mod(sp, 8 * i + (m0 + 4 * u), 0)
                        load_slab(sp, 4 * i + (n0 + 2 * u + 1), (n0 + 2 * u + 1) % RING)
                        for q in range(1, 4):
                            load_mod(sp, 8 * i + (m0 + 4 * u + q), q % 2)

            def slabs(n0, n1):
                whole = (n1 - n0) // RING
                with sp.Fori(0, whole) as i:
                    for q in range(RING):
                        load_slab(sp, 4 * i + (n0 + q), (n0 + q) % RING)
                for n in range(n0 + whole * RING, n1):
                    load_slab(sp, n, n % RING)

            slabs_and_mods(6, 8 * MOD_FIRST, MOD_IN_FFN0)
            n = 6 + 4 * MOD_IN_FFN0
            slabs(n, S_IN)
            sp.wait_ge(slab_used, RING + S_IN)
            sp.dma_start(ssm_cols[:, :], ssm_cols_in).then_inc(ssm_loaded, 16)
            sp.dma_start(wdt[:, :, :].rearrange("p k h -> p (k h)"), w_dt).then_inc(ssm_loaded, 16)
            sp.dma_start(ssm_rows[:, :], ssm_rows_in.partition_broadcast(P)).then_inc(ssm_loaded, 16)
            slabs(S_IN, S_FFN1 + 6)
            sp.wait_ge(slab_used, RING + S_FFN1)
            slabs_and_mods(S_FFN1 + 6, 8 * mods1[0], MOD_IN_FFN1)
            slabs(S_FFN1 + 6 + 4 * MOD_IN_FFN1, S_KV)
            sp.wait_ge(mod_mm, NMOD)
            sp.dma_start(att_rows[:, :], att_rows_in.partition_broadcast(P)).then_inc(att_loaded, 16)
            slabs(S_KV, SLABS)
            for j in range(DT):
                sp.wait_ge(out_ready, j + 1)
                sp.dma_start(out[:, j, :], x[:, j, :]).then_inc(out_stored, 16)
            sp.wait_ge(out_stored, 16 * DT)

        @block.gpsimd
        def _(pool):
            nc.gpsimd.memset(ones[:, :], 1.0).then_inc(slab_used, RING)
            nc.gpsimd.memset(eps[:, :], EPS).then_inc(consts, 1)
            pool.wait_ge(slab_used, RING + S_IN)
            pool.wait_ge(a_lo_ready, FT)
            for m, fill in ((after, 0.0), (upto, 1.0), (ident, 0.0)):
                nc.gpsimd.memset(m[:, :], fill).then_inc(ssm_consts, 1)
            pool.wait_ge(ssm_consts, 3)
            nc.gpsimd.affine_select(out=after[:, :], in_=after[:, :], compare_op=ALU.is_ge, fill=1.0, base=0,
                                    pattern=[[1, P]], channel_multiplier=-1).then_inc(ssm_consts, 1)
            nc.gpsimd.affine_select(out=upto[:, :], in_=upto[:, :], compare_op=ALU.is_ge, fill=0.0, base=0,
                                    pattern=[[1, P]], channel_multiplier=-1).then_inc(ssm_consts, 1)
            nc.gpsimd.affine_select(out=ident[:, :], in_=ident[:, :], compare_op=ALU.not_equal, fill=1.0, base=0,
                                    pattern=[[-1, P]], channel_multiplier=1).then_inc(ssm_consts, 1)
            pool.wait_ge(slab_used, RING + S_Q)
            nc.gpsimd.memset(mask[:, :, :, :], 0.0).then_inc(att_consts, 1)
            nc.gpsimd.memset(ident_a[:, :], 0.0).then_inc(att_consts, 1)
            nc.gpsimd.memset(k_pad[:, :, :], 0.0).then_inc(att_consts, 1)
            nc.gpsimd.memset(v_pad[:, :, :, :], 0.0).then_inc(att_consts, 1)
            pool.wait_ge(att_consts, 4)
            nc.gpsimd.affine_select(out=ident_a[:, :], in_=ident_a[:, :], compare_op=ALU.not_equal, fill=1.0, base=0,
                                    pattern=[[-1, P]], channel_multiplier=1).then_inc(att_consts, 1)
            m4 = mask[:, :, :, :].rearrange("p h b k -> p (h b) k")
            nc.gpsimd.affine_select(out=m4, in_=m4, compare_op=ALU.is_gt, fill=MASKED, base=0,
                                    pattern=[[0, 4], [1, 2 * P]], channel_multiplier=-1).then_inc(att_consts, 1)
            pool.wait_ge(att_consts, 6)
            nc.gpsimd.affine_select(out=m4, in_=m4, compare_op=ALU.is_ge, fill=MASKED, base=P,
                                    pattern=[[0, 4], [-1, 2 * P]], channel_multiplier=1).then_inc(att_consts, 1)
            pool.wait_ge(att_consts, 7)
            nc.gpsimd.memset(mask[:, 0, 0, 0:P], MASKED).then_inc(att_consts, 1)

        @block.scalar
        def _(act):
            act.wait_ge(in_loaded, 16)
            nc.scalar.activation(c_act[:, :], col("c"), ACT.Silu).then_inc(c_ready, 1)
            act.wait_ge(x_loaded, 16)
            for j in range(DT):
                act.wait_ge(ss_step, j + 1)
                square(act, 0, j)
            prep_hi(act, 0, 0)
            prep_hi(act, 0, 1)
            act.wait_ge(consts, 1)
            rstd_scalar(act, 0)
            act.wait_ge(mod_col, 2)
            norm_scalar(act, 0, M_SH1A, h_hi)
            ffn_scalar(act, 0, S_FFN0, 1, mods0)
            rstd_scalar(act, 1)
            norm_scalar(act, 1, M_SHMA, h_hi)
            ssm_scalar(act)
            rstd_scalar(act, 2)
            norm_scalar(act, 2, M_SH2A, h_hi)
            ffn_scalar(act, 1, S_FFN1, 3, mods1)
            rstd_scalar(act, 3)
            norm_scalar(act, 3, M_KVSH, hkv_hi)
            norm_scalar(act, 4, M_SH1B, h_hi)
            kv_scalar(act)
            ffn_scalar(act, 2, S_FFN2, 4, ())
            rstd_scalar(act, 4)
            norm_scalar(act, 5, M_SHMB, h_hi)
            att_scalar(act)
            rstd_scalar(act, 5)
            norm_scalar(act, 6, M_SH2B, h_hi)
            ffn_scalar(act, 3, S_FFN3, 6, (), last=True)
            rstd_scalar(act, 6)

        @block.vector
        def _(dve):
            clear_sum(dve)
            dve.wait_ge(c_ready, 1)
            for k in range(8):
                mod_block(dve, 0, k)
                add_square(dve, 0, k)
            mod_collect(dve, 0)
            for k in range(8):
                mod_block(dve, 1, k)
            prep_lo(dve, 0, 0)
            prep_lo(dve, 0, 1)
            mod_collect(dve, 1)
            dve.wait_ge(mod_col, 2)
            columns_vector(dve, 1, M_SC1A, col("nw_ffn0"))
            norm_vector(dve, 0, 0, M_SH1A, h_hi, h_lo)
            ffn_vector(dve, 0, S_FFN0, M_G1A, 1, mods0, 1)
            columns_vector(dve, 3, M_SCMA, col("nw_mix0"))
            norm_vector(dve, 1, 1, M_SHMA, h_hi, h_lo)
            ssm_vector(dve)
            columns_vector(dve, 4, M_SC2A, col("nw_ffn1"))
            norm_vector(dve, 2, 2, M_SH2A, h_hi, h_lo)
            ffn_vector(dve, 1, S_FFN1, M_G2A, 3, mods1, 4)
            columns_vector(dve, 6, M_KVSC, col("nw_kv"))
            norm_vector(dve, 3, 3, M_KVSH, hkv_hi, hkv_lo)
            columns_vector(dve, 7, M_SC1B, col("nw_ffn2"))
            norm_vector(dve, 3, 4, M_SH1B, h_hi, h_lo)
            kv_vector(dve)
            ffn_vector(dve, 2, S_FFN2, M_G1B, 4, (), 7)
            columns_vector(dve, 9, M_SCMB, col("nw_mix1"))
            norm_vector(dve, 4, 5, M_SHMB, h_hi, h_lo)
            att_vector(dve)
            columns_vector(dve, 10, M_SC2B, col("nw_ffn3"))
            norm_vector(dve, 5, 6, M_SH2B, h_hi, h_lo)
            ffn_vector(dve, 3, S_FFN3, M_G2B, 6, (), 10, last=True)
            dve.wait_ge(rs_step, 14)
            w = COLS["nw_final"][0]
            for j in range(DT):
                nc.vector.scalar_tensor_tensor(x[:, j, :], x[:, j, :], cols[:, w + j:w + j + 1], rstd[:, :],
                                               ALU.mult, ALU.mult).then_inc(out_ready, 1)

        @block.tensor
        def _(pe):
            pe.wait_ge(slab_used, RING)
            mod_sum(pe, 0)
            mod_sum(pe, 1)
            stat_tensor(pe, 0)
            ffn_tensor(pe, 0, S_FFN0, 0, 1, mods0)
            ssm_tensor(pe)
            ffn_tensor(pe, 1, S_FFN1, 2, 3, mods1)
            kv_tensor(pe)
            ffn_tensor(pe, 2, S_FFN2, 4, 4, ())
            att_tensor(pe)
            ffn_tensor(pe, 3, S_FFN3, 6, 6, (), last=True)


def lay_out(i):
    import numpy as np

    def tiles(w):
        kt, nt = w.shape[0] // P, w.shape[1] // P
        return np.ascontiguousarray(w.reshape(kt, P, nt, P).transpose(2, 1, 0, 3)).reshape(nt, P, kt * P)

    def cut(w, per):
        n, _, width = w.shape
        full = np.zeros((n, P, per * SLAB), w.dtype)
        full[:, :, :width] = w
        return full.reshape(n, P, per, SLAB).transpose(0, 2, 1, 3).reshape(n * per, P, SLAB)

    def ffn(layer, half):
        gu = i["ffn_w_gu"][layer, half]
        pairs = np.stack([tiles(gu[:, :FF]), tiles(gu[:, FF:])], 1).reshape(GU_SLABS, P, SLAB)
        return [pairs, cut(tiles(i["ffn_w_down"][layer, half]), DOWN_SPJ)]

    def columns(v):
        return v.reshape(-1, P).T

    w_in = i["ssm_w_in"][0]
    z, xbc = tiles(w_in[:, :DIN]), tiles(w_in[:, DIN:DIN + DIN + 2 * GROUPS * P])

    def group_order(t, g):
        return [t[2 * g], t[2 * g + 1], t[16 + g], t[24 + g]]

    order = group_order(xbc, 0)
    for g in range(GROUPS):
        order += [z[2 * g], z[2 * g + 1]]
        if g < GROUPS - 1:
            order += group_order(xbc, g + 1)
    heads = [8 * kt + 4 * ab + tt for kt in range(2) for tt in range(4) for ab in range(2)]
    feats = np.concatenate([np.arange(HDIM) + h * HDIM for h in heads])
    stream = np.concatenate(
        ffn(0, 0) + [np.stack(order), cut(tiles(i["ssm_w_out"][0]), 2)] + ffn(0, 1) + [tiles(i["w_kv"])] + ffn(1, 0)
        + [tiles(i["attn_w_q"][0][:, feats]), tiles(i["attn_w_o"][0][feats])] + ffn(1, 1))
    mods = np.concatenate([i["mod_w"][0], i["kv_mod_w"], i["mod_w"][1]], 1)
    w_mod = np.ascontiguousarray(mods.reshape(DT, P, NMOD, D).transpose(2, 0, 1, 3)).reshape(NMOD * DT, P, D)
    mod_b = np.concatenate([i["mod_b"][0], i["kv_mod_b"], i["mod_b"][1]])
    w_dt = np.ascontiguousarray(w_in[:, -HEADS:].reshape(DT, P, HEADS).transpose(1, 0, 2)).reshape(P, DT * HEADS)
    cols = np.concatenate([columns(v) for v in (
        i["c"], mod_b, i["ffn_norm_w"][0, 0], i["ffn_norm_w"][0, 1], i["ffn_norm_w"][1, 0], i["ffn_norm_w"][1, 1],
        i["mix_norm_w"][0], i["mix_norm_w"][1], i["kv_norm_w"], i["final_norm_w"], i["attn_b_o"][0],
        i["attn_b_q"][0][feats], i["b_kv"][:KV * HDIM])], 1)
    taps = np.concatenate([i["ssm_conv_w"][0], i["ssm_conv_b"]], 0).reshape(5, 32, P)
    taps = np.stack([np.stack(group_order(taps.transpose(1, 2, 0), g)) for g in range(GROUPS)])
    ssm_cols = np.concatenate([taps.transpose(2, 0, 1, 3).reshape(P, SSM_CONV),
                               columns(np.repeat(i["ssm_d"][0], HDIM)), columns(i["ssm_norm_w"][0])], 1)
    ssm_rows = np.concatenate([i["ssm_dt_bias"][0], i["ssm_a_log"][0]])
    att_rows = np.concatenate([i["b_kv"][KV * HDIM:], i["attn_sinks"][0][np.array(heads)]])
    x_t = np.ascontiguousarray(i["x"][0].T.reshape(DT, P, T).transpose(1, 0, 2)).reshape(P, DT * T)
    return {"w_stream": stream, "w_mod": w_mod, "w_dt": w_dt, "x_in": x_t, "cols_in": np.ascontiguousarray(cols),
            "ssm_cols_in": np.ascontiguousarray(ssm_cols), "ssm_rows_in": ssm_rows, "att_rows_in": att_rows}


def kernel(**inputs):
    import numpy as np
    import concourse.bacc as bacc
    from concourse.bass_utils import run_bass_kernel_spmd

    arrays = lay_out({k: np.asarray(v) for k, v in inputs.items()})
    nc = bacc.Bacc("TRN2", target_bir_lowering=False, num_devices=1)
    args = [nc.dram_tensor(n, a.shape, mybir.dt.from_np(a.dtype), kind="ExternalInput").ap() for n, a in arrays.items()]
    out = nc.dram_tensor("trunk_out", (P, DT, T), F32, kind="ExternalOutput").ap()
    trunk(nc, *args, out)
    r = run_bass_kernel_spmd(nc, [arrays], core_ids=[0])
    got = r.results[0]["trunk_out"]
    return got.transpose(2, 1, 0).reshape(1, T, D)
```

```python
from contextlib import ExitStack

import concourse.bass as bass
from concourse import mybir

F32 = mybir.dt.float32
F32R = mybir.dt.float32r
ALU = mybir.AluOpType
ACT = mybir.ActivationFunctionType
AX = mybir.AxisListType

P = 128
D = 1024
T = 512
DT = D // P
FF = 2816
FT = FF // P
DIN = 2048
HEADS, GROUPS, HPG, HDIM = 32, 8, 4, 64
NCH = T // P
KV, QH = 4, 16
EPS = 1e-5
MASKED = -3.0e38

RING = 4
ONE = 1
SLAB = 8 * P
GU_SLABS = 2 * FT
DOWN_SPJ = 3
FFN_SLABS = GU_SLABS + DOWN_SPJ * DT
IN_SLABS = 6 * GROUPS
OUT_SLABS = 2 * DT
KV_SLABS = 4
Q_SLABS = DT
O_SLABS = DT

S_FFN0 = 0
S_IN = S_FFN0 + FFN_SLABS
S_OUT = S_IN + IN_SLABS
S_FFN1 = S_OUT + OUT_SLABS
S_KV = S_FFN1 + FFN_SLABS
S_FFN2 = S_KV + KV_SLABS
S_Q = S_FFN2 + FFN_SLABS
S_O = S_Q + Q_SLABS
S_FFN3 = S_O + O_SLABS
SLABS = S_FFN3 + FFN_SLABS

(M_SH1A, M_SC1A, M_G1A, M_SHMA, M_SCMA, M_GMA, M_SH2A, M_SC2A, M_G2A, M_KVSH, M_KVSC,
 M_SH1B, M_SC1B, M_G1B, M_SHMB, M_SCMB, M_GMB, M_SH2B, M_SC2B, M_G2B) = range(20)
NMOD = 20
MOD_FIRST = 2
MOD_IN_FFN0 = GU_SLABS // 4
MOD_IN_FFN1 = NMOD - MOD_FIRST - MOD_IN_FFN0

COLS = {}
_at = 0
for _name, _n in (("c", DT), ("modb", NMOD * DT), ("nw_ffn0", DT), ("nw_ffn1", DT), ("nw_ffn2", DT), ("nw_ffn3", DT),
                  ("nw_mix0", DT), ("nw_mix1", DT), ("nw_kv", DT), ("nw_final", DT), ("b_o", DT), ("b_q", DT),
                  ("b_k", 2)):
    COLS[_name] = (_at, _at + _n)
    _at += _n
NCOLS = _at
SSM_CONV = GROUPS * 4 * 5
NSSM = SSM_CONV + 16 + 16
NROWS_S = 2 * HEADS
NROWS_A = KV * HDIM + QH


def trunk(nc, w_stream, w_mod, w_dt, x_in, cols_in, ssm_cols_in, ssm_rows_in, att_rows_in, out):
    ctx = ExitStack()
    with ctx:
        def sem(name):
            return ctx.enter_context(nc.semaphore(name))

        def sb(stack, name, shape, dt=F32):
            return stack.enter_context(nc.sbuf_tensor(name, shape, dt))

        x = sb(ctx, "x_trunk", [P, DT, T])
        h_hi = sb(ctx, "h_hi", [P, DT, T], F32R)
        h_lo = sb(ctx, "h_lo", [P, DT, T], F32R)
        raw = sb(ctx, "raw", [P, RING, SLAB])
        w_hi_sb = sb(ctx, "w_hi_sb", [P, RING, SLAB], F32R)
        w_lo_sb = sb(ctx, "w_lo_sb", [P, RING, SLAB], F32R)
        tmp = sb(ctx, "tmp", [P, 2, T])
        sumsq = sb(ctx, "sumsq", [P, T])
        rstd = sb(ctx, "rstd", [P, T])
        ones = sb(ctx, "ones", [P, P])
        eps = sb(ctx, "eps", [P, 1])
        spare = sb(ctx, "spare", [P, 16])
        cols = sb(ctx, "cols", [P, NCOLS])
        mod = sb(ctx, "mod", [P, NMOD, DT])
        c_act = sb(ctx, "c_act", [P, DT])
        scale_col = sb(ctx, "scale_col", [P, DT])
        gate_col = sb(ctx, "gate_col", [P, DT])

        def col(name):
            return cols[:, COLS[name][0]:COLS[name][1]]

        with ExitStack() as s:
            mod_raw = sb(s, "mod_raw", [P, 2, D])
            mod_acc = sb(s, "mod_acc", [P, D])
            a_hi = sb(s, "a_hi", [P, FT, T], F32R)
            a_lo = sb(s, "a_lo", [P, FT, T], F32R)
        with ExitStack() as s:
            sb(s, "gap0", [P, 3 * D])
            first_mod = sb(s, "first_mod", [P, 8 * MOD_FIRST, D])
            first_sq = sb(s, "first_sq", [P, DT, T])
        with ExitStack() as s:
            y_hi = sb(s, "y_hi", [P, 16, T], F32R)
            y_lo = sb(s, "y_lo", [P, 16, T], F32R)
            xs = sb(s, "xs", [P, 2, 2, T])
            bc = sb(s, "bc", [P, 2, 2, T])
            zs = sb(s, "zs", [P, 2, T])
            ssm_cols = sb(s, "ssm_cols", [P, NSSM])
            dt_tok = sb(s, "dt_tok", [P, NCH, HEADS])
            a_tok = sb(s, "a_tok", [P, NCH, HEADS])
            dd_tok = sb(s, "dd_tok", [P, NCH, HEADS])
            after = sb(s, "after", [P, P])
            upto = sb(s, "upto", [P, P])
            ident = sb(s, "ident", [P, P])
            with ExitStack() as r:
                wdt = sb(r, "wdt", [P, DT, HEADS])
                wdt_hi = sb(r, "wdt_hi", [P, DT, HEADS], F32R)
                wdt_lo = sb(r, "wdt_lo", [P, DT, HEADS], F32R)
                ssm_rows = sb(r, "ssm_rows", [P, NROWS_S])
                soft = sb(r, "soft", [P, 5, NCH * HEADS])
            ta = sb(s, "ta", [P, HPG, P])
            el = sb(s, "el", [P, HPG, P])
            ee = sb(s, "ee", [P, HPG, P])
            gm_t = sb(s, "gm_t", [P, P])
            b_tok = sb(s, "b_tok", [P, P])
            x_pad = sb(s, "x_pad", [P, 2, 2, P])
            x_dec = sb(s, "x_dec", [P, HPG, HDIM])
            state = sb(s, "state", [P, 2, 2, P])
            chunk_dec = sb(s, "chunk_dec", [P, HPG])
        with ExitStack() as s:
            k_all = sb(s, "k_all", [P, 2, T])
            v_all = sb(s, "v_all", [P, NCH, KV * HDIM])
            att_rows = sb(s, "att_rows", [P, NROWS_A])
            with ExitStack() as r:
                sb(r, "gap", [P, 2 * D])
                hkv_hi = sb(r, "hkv_hi", [P, DT, T], F32R)
                hkv_lo = sb(r, "hkv_lo", [P, DT, T], F32R)
            q_all = sb(s, "q_all", [P, DT, T])
            q_cur = sb(s, "q_cur", [P, 2, T])
            k_pad = sb(s, "k_pad", [P, 2, P + T])
            v_pad = sb(s, "v_pad", [P, NCH, 2, P])
            o_hi = sb(s, "o_hi", [P, DT, T], F32R)
            o_lo = sb(s, "o_lo", [P, DT, T], F32R)
            probs = sb(s, "probs", [P, 2, 4, 2 * P])
            probs_t = sb(s, "probs_t", [P, 2, 4, P])
            mask = sb(s, "mask", [P, 2, 2, 2 * P])
            ident_a = sb(s, "ident_a", [P, P])
            bq8 = sb(s, "bq8", [P, DT])
            gb_o = sb(s, "gb_o", [P, DT])
            stat4 = sb(s, "stat4", [P, 2, 6, 4])

        bank = [ctx.enter_context(nc.psum_tensor(f"bank{i}", [P, T], F32)) for i in range(8)]

        raw_loaded = [sem(f"raw_loaded{i}") for i in range(RING)]
        w_hi, w_lo, slab_used = sem("w_hi"), sem("w_lo"), sem("slab_used")
        in_loaded, x_loaded, ssm_loaded, att_loaded = sem("in_loaded"), sem("x_loaded"), sem("ssm_loaded"), sem("att_loaded")
        consts, c_ready = sem("consts"), sem("c_ready")
        mod_loaded = [sem("mod_loaded0"), sem("mod_loaded1")]
        first_loaded = [sem(f"first_loaded{i}") for i in range(4 * MOD_FIRST)]
        first_sq_ready = sem("first_sq_ready")
        mod_step, mod_mm, mod_col = sem("mod_step"), sem("mod_mm"), sem("mod_col")
        col_step = sem("col_step")
        ss_step, sq_ready, x_ready, stat_done, rs_step = (
            sem("ss_step"), sem("sq_ready"), sem("x_ready"), sem("stat_done"), sem("rs_step"))
        t_ready, h_hi_ready, h_lo_ready = sem("t_ready"), sem("h_hi_ready"), sem("h_lo_ready")
        silu_done, a_ready, a_hi_ready, a_lo_ready = (
            sem("silu_done"), sem("a_ready"), sem("a_hi_ready"), sem("a_lo_ready"))
        out_ready, out_stored = sem("out_ready"), sem("out_stored")

        block = ctx.enter_context(nc.Block())

        def load_slab(sp, n, slot):
            sp.wait_ge(w_lo, n - RING + 1)
            sp.dma_start(raw[:, slot, :], w_stream[n]).then_inc(raw_loaded[slot], 16)

        def prep_hi(act, b4, l, width=SLAB):
            s = l % RING
            act.wait_ge(raw_loaded[s], 16 * (b4 + l // RING) + 16)
            act.wait_ge(slab_used, 4 * b4 + l + 1)
            nc.scalar.activation(w_hi_sb[:, s, 0:width], raw[:, s, 0:width], ACT.Copy).then_inc(w_hi, 1)

        def prep_lo(dve, b4, l, width=SLAB):
            s = l % RING
            dve.wait_ge(w_hi, 4 * b4 + l + 1)
            nc.vector.tensor_tensor(w_lo_sb[:, s, 0:width], raw[:, s, 0:width], w_hi_sb[:, s, 0:width],
                                    ALU.subtract).then_inc(w_lo, 1)

        def product3(ps, s_hi, s_lo, m_hi, m_lo, start, stop):
            nc.tensor.matmul(ps, s_hi, m_hi, start=start, stop=False)
            nc.tensor.matmul(ps, s_hi, m_lo, start=False, stop=False)
            return nc.tensor.matmul(ps, s_lo, m_hi, start=False, stop=stop)

        def use_slab(pe, b4, l, ps, m_hi, m_lo, k0=0, tiles=8, ktiles=8, ready=None):
            s = l % RING
            pe.wait_ge(w_lo, 4 * b4 + l + 1)
            for k in range(tiles):
                if ready is not None:
                    ready(k0 + k)
                w = slice(k * P, (k + 1) * P)
                mm = product3(ps, w_hi_sb[:, s, w], w_lo_sb[:, s, w], m_hi[:, k0 + k, :], m_lo[:, k0 + k, :],
                              k0 + k == 0, k0 + k == ktiles - 1)
            mm.then_inc(slab_used, 1)

        def use_pair(pe, b4, l, banks, m_hi, m_lo, ready=None):
            for k in range(8):
                if ready is not None:
                    ready(k)
                w = slice(k * P, (k + 1) * P)
                for q in range(2):
                    s = (l + q) % RING
                    if k == 0:
                        pe.wait_ge(w_lo, 4 * b4 + l + q + 1)
                    mm = product3(banks[q][:, :], w_hi_sb[:, s, w], w_lo_sb[:, s, w], m_hi[:, k, :], m_lo[:, k, :],
                                  k == 0, k == 7)
                    if k == 7:
                        mm.then_inc(slab_used, 1)

        def mod_block(dve, v, k, first=False):
            if first:
                dve.wait_ge(first_loaded[4 * v + k // 2], 16)
                w = first_mod[:, 8 * v + k, :]
            else:
                dve.wait_ge(mod_loaded[k % 2], 16 * (4 * (v - MOD_FIRST) + k // 2) + 16)
                w = mod_raw[:, k % 2, :]
            if k == 0:
                if not first or v > 0:
                    dve.wait_ge(mod_mm, v)
                nc.vector.tensor_scalar(mod_acc[:, :], w, c_act[:, 0:1], None, ALU.mult).then_inc(mod_step, 1)
            else:
                dve.wait_ge(mod_step, 8 * v + k)
                nc.vector.scalar_tensor_tensor(mod_acc[:, :], w, c_act[:, k:k + 1], mod_acc[:, :],
                                               ALU.mult, ALU.add).then_inc(mod_step, 1)

        def mod_sum(pe, v, first=False):
            pe.wait_ge(mod_step, 8 * v + 8)
            if not first:
                pe.wait_ge(mod_col, v)
            for j in range(DT):
                mm = nc.tensor.matmul(bank[7][:, j:j + 1], mod_acc[:, j * P:(j + 1) * P], ones[:, 0:1],
                                      start=True, stop=True)
            mm.then_inc(mod_mm, 1)

        def mod_collect(dve, v):
            dve.wait_ge(mod_mm, v + 1)
            b = cols[:, COLS["modb"][0]:COLS["modb"][1]].rearrange("p (v j) -> p v j", j=DT)
            nc.vector.tensor_tensor(mod[:, v, :], bank[7][:, 0:DT], b[:, v, :], ALU.add).then_inc(mod_col, 1)

        def load_mod(sp, m, slot, first=False):
            if not first:
                sp.wait_ge(mod_step, m - 1)
            sp.dma_start(mod_raw[:, slot, :], w_mod[m]).then_inc(mod_loaded[slot], 16)

        def square(act, st, j):
            nc.scalar.activation(tmp[:, 0, :], x[:, j, :], ACT.Square).then_inc(sq_ready, 1)

        def clear_sum(dve):
            nc.vector.memset(sumsq[:, :], 0.0).then_inc(ss_step, 1)

        def add_square(dve, st, j):
            dve.wait_ge(sq_ready, 8 * (st - 1) + j + 1)
            dve.wait_ge(ss_step, 9 * (st - 1) + j + 1)
            nc.vector.tensor_tensor(sumsq[:, :], sumsq[:, :], tmp[:, 0, :], ALU.add).then_inc(ss_step, 1)

        def stat_tensor(pe, st):
            pe.wait_ge(ss_step, 9 * st)
            nc.tensor.matmul(bank[6][:, :], ones[:, :], sumsq[:, :], start=True, stop=True).then_inc(stat_done, 1)

        def rstd_scalar(act, st):
            act.wait_ge(stat_done, st + 1)
            nc.scalar.activation(rstd[:, :], bank[6][:, :], ACT.Ln, bias=eps[:, 0:1], scale=1.0 / D).then_inc(rs_step, 1)
            act.wait_ge(rs_step, 2 * st + 1)
            nc.scalar.activation(rstd[:, :], rstd[:, :], ACT.Exp, scale=-0.5).then_inc(rs_step, 1)

        def columns_vector(dve, count, sc, w):
            nc.vector.scalar_tensor_tensor(scale_col[:, :], mod[:, sc, :], 1.0, w, ALU.add, ALU.mult).then_inc(col_step, 1)
            dve.wait_ge(col_step, count)

        def norm_vector(dve, st, hs, sh, hi, lo):
            def rest(j):
                dve.wait_ge(h_hi_ready, 8 * hs + j + 1)
                nc.vector.scalar_tensor_tensor(lo[:, j, :], tmp[:, j % 2, :], mod[:, sh, j:j + 1], hi[:, j, :],
                                               ALU.add, ALU.subtract).then_inc(h_lo_ready, 1)

            dve.wait_ge(rs_step, 2 * st + 2)
            for j in range(DT):
                if 8 * hs + j > 1:
                    dve.wait_ge(h_lo_ready, 8 * hs + j - 1)
                nc.vector.scalar_tensor_tensor(tmp[:, j % 2, :], x[:, j, :], scale_col[:, j:j + 1], rstd[:, :],
                                               ALU.mult, ALU.mult).then_inc(t_ready, 1)
                if j:
                    rest(j - 1)
            rest(DT - 1)

        def norm_scalar(act, hs, sh, hi):
            for j in range(DT):
                act.wait_ge(t_ready, 8 * hs + j + 1)
                nc.scalar.activation(hi[:, j, :], tmp[:, j % 2, :], ACT.Identity, bias=mod[:, sh, j:j + 1],
                                     ).then_inc(h_hi_ready, 1)

        def project_turns(eng, body, last, turn):
            turns = DT // body
            if not last:
                with eng.Fori(0, turns) as i:
                    turn(i, False)
            else:
                with eng.Fori(0, turns - 1) as i:
                    turn(i, False)
                turn(turns - 1, True)

        def widths(l, spj):
            return 6 * P if spj == DOWN_SPJ and l % spj == spj - 1 else SLAB

        def project_tensor(pe, n0, ktiles, spj, body, m_hi, m_lo, ready, st, last=False):
            def turn(i, _):
                b4 = n0 // 4 + i * (body * spj // RING)
                for jj in range(body):
                    if spj == 1:
                        pe.wait_ge(x_ready, 8 * (st - 1) + body * i + jj - 1)
                    for s in range(spj):
                        use_slab(pe, b4, jj * spj + s, bank[4 + jj % 2][:, :], m_hi, m_lo, 8 * s,
                                 min(8, ktiles - 8 * s), ktiles, ready if jj == 0 else None)
            project_turns(pe, body, last, turn)
            stat_tensor(pe, st)

        def project_scalar(act, n0, spj, body, st, last=False):
            def turn(i, end):
                b4 = n0 // 4 + i * (body * spj // RING)
                for jj in range(body):
                    for s in range(spj):
                        l = jj * spj + s + 2
                        if not end or l < body * spj:
                            prep_hi(act, b4, l, widths(l, spj))
                    j = body * i + jj
                    act.wait_ge(x_ready, 8 * (st - 1) + j + 1)
                    square(act, st, j)
            project_turns(act, body, last, turn)

        def project_vector(dve, n0, spj, body, gate, st, last=False):
            clear_sum(dve)

            def turn(i, end):
                b4 = n0 // 4 + i * (body * spj // RING)
                for jj in range(body):
                    for s in range(spj):
                        l = jj * spj + s + 2
                        if not end or l < body * spj:
                            prep_lo(dve, b4, l, widths(l, spj))
                    j = body * i + jj
                    dve.wait_ge(slab_used, RING + 4 * b4 + (jj + 1) * spj)
                    nc.vector.scalar_tensor_tensor(x[:, j, :], bank[4 + jj % 2][:, :], gate(j), x[:, j, :],
                                                   ALU.mult, ALU.add).then_inc(x_ready, 1)
                    add_square(dve, st, j)
            project_turns(dve, body, last, turn)

        def ffn_tensor(pe, k, n0, hs, st, mods, last=False):
            def turn(i, v):
                b4 = n0 // 4 + i
                for u in range(2):
                    use_pair(pe, b4, 2 * u, bank[2 * u:2 * u + 2], h_hi, h_lo,
                             (lambda j: pe.wait_ge(h_lo_ready, 8 * hs + j + 1)) if u == 0 else None)
                if v is not None:
                    mod_sum(pe, v)
            with_mods(pe, mods, turn)
            project_tensor(pe, n0 + GU_SLABS, FT, DOWN_SPJ, 4, a_hi, a_lo,
                           lambda f: pe.wait_ge(a_lo_ready, ONE + FT * k + f + 1), st, last)

        def with_mods(eng, mods, turn):
            turns = FT // 2
            if len(mods):
                with eng.Fori(0, len(mods)) as i:
                    turn(i, mods[0] + i)
            if len(mods) < turns:
                with eng.Fori(len(mods), turns) as i:
                    turn(i, None)

        def ffn_scalar(act, k, n0, st, mods, last=False):
            def turn(i, v):
                b4 = n0 // 4 + i
                for u in range(2):
                    f = 2 * i + u
                    prep_hi(act, b4, 2 * u + 2)
                    prep_hi(act, b4, 2 * u + 3)
                    act.wait_ge(slab_used, RING + 4 * b4 + 2 * u + 1)
                    act.wait_ge(a_ready, ONE + FT * k + f)
                    nc.scalar.activation(tmp[:, 0, :], bank[2 * u][:, :], ACT.Silu).then_inc(silu_done, 1)
                    act.wait_ge(a_ready, ONE + FT * k + f + 1)
                    nc.scalar.activation(a_hi[:, f, :], tmp[:, 1, :], ACT.Copy).then_inc(a_hi_ready, 1)
            with_mods(act, mods, turn)
            project_scalar(act, n0 + GU_SLABS, DOWN_SPJ, 4, st, last)

        def ffn_vector(dve, k, n0, g, st, mods, cols_before, last=False):
            def turn(i, v):
                b4 = n0 // 4 + i
                for u in range(2):
                    f = 2 * i + u
                    for q in range(2):
                        if v is not None:
                            mod_block(dve, v, 4 * u + q)
                        prep_lo(dve, b4, 2 * u + 2 + q)
                    if v is not None:
                        mod_block(dve, v, 4 * u + 2)
                    dve.wait_ge(silu_done, FT * k + f + 1)
                    dve.wait_ge(slab_used, RING + 4 * b4 + 2 * u + 2)
                    dve.wait_ge(a_lo_ready, ONE + FT * k + f)
                    nc.vector.tensor_tensor(tmp[:, 1, :], tmp[:, 0, :], bank[2 * u + 1][:, :],
                                            ALU.mult).then_inc(a_ready, 1)
                    if v is not None:
                        mod_block(dve, v, 4 * u + 3)
                    dve.wait_ge(a_hi_ready, FT * k + f + 1)
                    nc.vector.tensor_tensor(a_lo[:, f, :], tmp[:, 1, :], a_hi[:, f, :],
                                            ALU.subtract).then_inc(a_lo_ready, 1)
                if v is not None:
                    mod_collect(dve, v)
            with_mods(dve, mods, turn)
            dve.wait_ge(mod_col, min(g + 1, NMOD))
            nc.vector.tensor_scalar(gate_col[:, :], mod[:, g, :], 0.5, None, ALU.mult).then_inc(col_step, 1)
            dve.wait_ge(col_step, cols_before + 1)
            project_vector(dve, n0 + GU_SLABS, DOWN_SPJ, 4, lambda j: gate_col[:, bass.ds(j, 1)], st, last)

        wdt_split, dtp_done, soft_act, soft_dve, dec_done = (
            sem("wdt_split"), sem("dtp_done"), sem("soft_act"), sem("soft_dve"), sem("dec_done"))
        ssm_consts = sem("ssm_consts")
        z_read, conv_init, conv_step = sem("z_read"), sem("conv_init"), sem("conv_step")
        silu_x, silu_z = sem("silu_x"), sem("silu_z")
        ta_ready, turned, seg_ready, sum_ready = sem("ta_ready"), sem("turned"), sem("seg_ready"), sem("sum_ready")
        el_ready, ee_ready = sem("el_ready"), sem("ee_ready")
        cd_ready = sem("cd_ready")
        g_ready, mixed, y_done, st_done, state_ready = (
            sem("g_ready"), sem("mixed"), sem("y_done"), sem("st_done"), sem("state_ready"))
        gate_step, gsq_ready, gstat_done, grs_step = (
            sem("gate_step"), sem("gsq_ready"), sem("gstat_done"), sem("grs_step"))
        yn_ready, y_hi_ready, y_lo_ready = sem("yn_ready"), sem("y_hi_ready"), sem("y_lo_ready")

        cb = bank[4][:, 3 * P:4 * P]
        chunk = [slice(c * P, (c + 1) * P) for c in range(NCH)]

        def scan_a_tensor(pe, g, pp, c):
            if c == 0:
                pe.wait_ge(silu_x, 4 * g + 4)
                pe.wait_ge(ssm_consts, 6)
            for i in range(2):
                nc.tensor.transpose(bank[4][:, i * P:(i + 1) * P], xs[:, pp, i, chunk[c]], ident[:, :])
            nc.tensor.transpose(bank[4][:, 2 * P:3 * P], bc[:, pp, 0, chunk[c]], ident[:, :])
            nc.tensor.matmul(cb, bc[:, pp, 0, chunk[c]], bc[:, pp, 1, chunk[c]], start=True, stop=True).then_inc(turned, 1)
            pe.wait_ge(ta_ready, 4 * g + c + 1)
            tav = ta[:, :, :].rearrange("p h l -> p (h l)")
            nc.tensor.matmul(bank[5][:, :], after[:, :], tav, start=True, stop=True).then_inc(seg_ready, 1)
            nc.tensor.matmul(bank[6][:, :], ones[:, :], tav, start=True, stop=True).then_inc(sum_ready, 1)

        def scan_b_tensor(pe, g, c):
            pe.wait_ge(mixed, 4 * g + c + 1)
            if c:
                pe.wait_ge(state_ready, 3 * g + c)
            for pair in range(2):
                ps = bank[2 + pair][:, chunk[c]]
                for r in range(2):
                    mm = nc.tensor.matmul(ps, x_pad[:, r, pair, :], el[:, 2 * pair + r, :],
                                          start=(r == 0), stop=(c == 0 and r == 1))
                if c:
                    for r in range(2):
                        mm = nc.tensor.matmul(ps, state[:, r, pair, :], ee[:, 2 * pair + r, :],
                                              start=False, stop=(r == 1))
            mm.then_inc(y_done, 1)
            if c < NCH - 1:
                nc.tensor.matmul(bank[7][:, 0:HPG * HDIM], b_tok[:, :], x_dec[:, :, :].rearrange("p h d -> p (h d)"),
                                 start=True, stop=True).then_inc(st_done, 1)

        def ssm_tensor(pe):
            n4 = S_IN // 4
            ready = lambda j: pe.wait_ge(h_lo_ready, 8 * 1 + j + 1)
            use_pair(pe, n4, 0, bank[0:2], h_hi, h_lo, ready)
            pe.wait_ge(wdt_split, 2)
            for c in range(NCH):
                for k in range(DT):
                    mm = product3(bank[4][:, c * HEADS:(c + 1) * HEADS], h_hi[:, k, chunk[c]], h_lo[:, k, chunk[c]],
                                  wdt_hi[:, k, :], wdt_lo[:, k, :], k == 0, k == DT - 1)
            mm.then_inc(dtp_done, 1)
            use_pair(pe, n4, 2, bank[2:4], h_hi, h_lo)
            pe.wait_ge(soft_dve, SOFT_A + 1)
            pe.wait_ge(ssm_consts, 6)
            nc.tensor.matmul(bank[5][:, 0:NCH * HEADS], after[:, :], a_tok[:, :, :].rearrange("p c h -> p (c h)"),
                             start=True, stop=True).then_inc(dec_done, 1)

            def group(i, pp, last=False):
                g = 2 * i + pp
                b4 = n4 + 1 + 3 * i

                def slab(s):
                    if s < 2:
                        pe.wait_ge(conv_step, 3 * (4 * g + 3 + s))
                    elif s < 4:
                        pe.wait_ge(z_read, 2 * g + s - 1)
                    else:
                        pe.wait_ge(conv_step, 3 * (4 * g + 1 + s))
                    use_slab(pe, b4, 6 * pp + s, bank[s % 2][:, :], h_hi, h_lo)

                slab(0)
                scan_a_tensor(pe, g, pp, 0)
                slab(1)
                for c in range(NCH):
                    if c and not last:
                        slab(c + 1)
                    scan_b_tensor(pe, g, c)
                    if c < NCH - 1:
                        scan_a_tensor(pe, g, pp, c + 1)
                if not last:
                    slab(5)
                for t in range(2):
                    pe.wait_ge(gsq_ready, 2 * g + t + 1)
                    mm = nc.tensor.matmul(bank[7][:, :], ones[:, :], zs[:, t, :], start=(t == 0), stop=(t == 1))
                mm.then_inc(gstat_done, 1)

            with pe.Fori(0, GROUPS // 2 - 1) as i:
                group(i, 0)
                group(i, 1)
            group(GROUPS // 2 - 1, 0)
            group(GROUPS // 2 - 1, 1, last=True)
            project_tensor(pe, S_OUT, 16, 2, 2, y_hi, y_lo, lambda f: pe.wait_ge(y_lo_ready, ONE + f + 1), 2)

        SOFT_A = 17

        def conv_cols(g, t, tap):
            v = ssm_cols[:, 0:SSM_CONV].rearrange("p (g t k) -> p g t k", g=GROUPS, t=4)
            return v[:, g, t, tap:tap + 1]

        def conv_tile(pp, t):
            return xs[:, pp, t, :] if t < 2 else bc[:, pp, t - 2, :]

        def conv_scalar(act, g, pp, t, used, ps):
            act.wait_ge(slab_used, used)
            nc.scalar.activation(conv_tile(pp, t), ps, ACT.Identity, bias=conv_cols(g, t, 4),
                                 scale=conv_cols(g, t, 3)).then_inc(conv_init, 1)

        def conv_vector(dve, g, pp, t, ps):
            y = conv_tile(pp, t)
            dve.wait_ge(conv_init, 4 * g + t + 1)
            for back in range(1, 4):
                if back > 1:
                    dve.wait_ge(conv_step, 3 * (4 * g + t) + back - 1)
                nc.vector.scalar_tensor_tensor(y[:, back:], ps[:, 0:T - back], conv_cols(g, t, 3 - back),
                                               y[:, back:], ALU.mult, ALU.add).then_inc(conv_step, 1)

        def silu_tiles(act, g, pp, tiles):
            for t in tiles:
                act.wait_ge(conv_step, 3 * (4 * g + t + 1))
                nc.scalar.activation(conv_tile(pp, t), conv_tile(pp, t), ACT.Silu).then_inc(silu_x, 1)

        def ssm_scalar(act):
            n4 = S_IN // 4
            act.wait_ge(ssm_loaded, 48)
            nc.scalar.activation(wdt_hi[:, :, :], wdt[:, :, :], ACT.Copy).then_inc(wdt_split, 1)
            prep_hi(act, n4, 2)
            prep_hi(act, n4, 3)
            conv_scalar(act, 0, 0, 0, RING + S_IN + 1, bank[0][:, :])
            conv_scalar(act, 0, 0, 1, RING + S_IN + 2, bank[1][:, :])
            prep_hi(act, n4, 4)
            prep_hi(act, n4, 5)
            act.wait_ge(soft_dve, 2)
            nc.scalar.activation(soft[:, 2, :], soft[:, 1, :], ACT.Exp).then_inc(soft_act, 1)
            nc.scalar.activation(ssm_rows[:, HEADS:2 * HEADS], ssm_rows[:, HEADS:2 * HEADS], ACT.Exp).then_inc(soft_act, 1)
            conv_scalar(act, 0, 0, 2, RING + S_IN + 3, bank[2][:, :])
            conv_scalar(act, 0, 0, 3, RING + S_IN + 4, bank[3][:, :])
            silu_tiles(act, 0, 0, range(4))
            act.wait_ge(dec_done, 1)
            nc.scalar.activation(dd_tok[:, :, :].rearrange("p c h -> p (c h)"), bank[5][:, 0:NCH * HEADS],
                                 ACT.Exp).then_inc(soft_act, 1)

            def group(i, pp, last=False):
                g = 2 * i + pp
                b4 = n4 + 1 + 3 * i
                used = RING + 4 * b4 + 6 * pp

                def z_copy(t):
                    act.wait_ge(slab_used, used + t + 1)
                    if t == 0:
                        act.wait_ge(gstat_done, ONE + g)
                    nc.scalar.activation(zs[:, t, :], bank[t][:, :], ACT.Copy).then_inc(z_read, 1)

                def scan(c):
                    act.wait_ge(seg_ready, 4 * g + c + 1)
                    nc.scalar.activation(el[:, :, :].rearrange("p h l -> p (h l)"), bank[5][:, :],
                                         ACT.Exp).then_inc(el_ready, 1)
                    act.wait_ge(sum_ready, 4 * g + c + 1)
                    nc.scalar.activation(ee[:, :, :].rearrange("p h l -> p (h l)"), bank[6][:, :],
                                         ACT.Exp).then_inc(ee_ready, 1)

                for s in range(6):
                    if not last or s < 2:
                        prep_hi(act, b4, 6 * pp + s + 2)
                    if not last and s >= 3:
                        conv_scalar(act, g + 1, 1 - pp, s - 3, used + s, bank[(s - 3) % 2][:, :])
                    if 1 <= s <= 2:
                        z_copy(s - 1)
                    if 1 <= s <= 4:
                        scan(s - 1)
                for t in range(2):
                    act.wait_ge(z_read, 2 * g + t + 1)
                    nc.scalar.activation(zs[:, t, :], zs[:, t, :], ACT.Silu).then_inc(silu_z, 1)
                if not last:
                    silu_tiles(act, g + 1, 1 - pp, range(2))
                for t in range(2):
                    act.wait_ge(gate_step, 4 * g + 2 * t + 2)
                    nc.scalar.activation(zs[:, t, :], tmp[:, t, :], ACT.Square).then_inc(gsq_ready, 1)
                if not last:
                    conv_scalar(act, g + 1, 1 - pp, 3, used + 6, bank[1][:, :])
                    silu_tiles(act, g + 1, 1 - pp, range(2, 4))
                act.wait_ge(gstat_done, ONE + g + 1)
                nc.scalar.activation(rstd[:, :], bank[7][:, :], ACT.Ln, bias=eps[:, 0:1],
                                     scale=1.0 / (2 * P)).then_inc(grs_step, 1)
                act.wait_ge(grs_step, 2 * g + 1)
                nc.scalar.activation(rstd[:, :], rstd[:, :], ACT.Exp, scale=-0.5).then_inc(grs_step, 1)
                for t in range(2):
                    act.wait_ge(yn_ready, 2 * g + t + 1)
                    nc.scalar.activation(y_hi[:, 2 * g + t, :], tmp[:, t, :], ACT.Copy).then_inc(y_hi_ready, 1)

            with act.Fori(0, GROUPS // 2 - 1) as i:
                group(i, 0)
                group(i, 1)
            group(GROUPS // 2 - 1, 0)
            group(GROUPS // 2 - 1, 1, last=True)
            project_scalar(act, S_OUT, 2, 2, 2)

        def ssm_vector(dve):
            n4 = S_IN // 4
            dve.wait_ge(ssm_loaded, 48)
            step = [0]

            def link(ins):
                step[0] += 1
                ins.then_inc(soft_dve, 1)
                dve.wait_ge(soft_dve, step[0])

            dve.wait_ge(wdt_split, 1)
            nc.vector.tensor_tensor(wdt_lo[:, :, :], wdt[:, :, :], wdt_hi[:, :, :], ALU.subtract).then_inc(wdt_split, 1)
            prep_lo(dve, n4, 2)
            prep_lo(dve, n4, 3)
            conv_vector(dve, 0, 0, 0, bank[0])
            conv_vector(dve, 0, 0, 1, bank[1])
            prep_lo(dve, n4, 4)
            prep_lo(dve, n4, 5)
            v, na, e, sv, s2 = (soft[:, q, :] for q in range(5))
            dtv = dt_tok[:, :, :].rearrange("p c h -> p (c h)")
            bias = ssm_rows[:, 0:HEADS].unsqueeze(1).broadcast_to([P, NCH, HEADS])
            dve.wait_ge(dtp_done, 1)
            link(nc.vector.tensor_tensor(v.rearrange("p (c h) -> p c h", c=NCH),
                                         bank[4][:, 0:NCH * HEADS].rearrange("p (c h) -> p c h", c=NCH), bias, ALU.add))
            link(nc.vector.scalar_tensor_tensor(na, v, -1.0, v, ALU.mult, ALU.min))
            dve.wait_ge(soft_act, 1)
            link(nc.vector.tensor_scalar(sv, e, 2.0, None, ALU.add))
            link(nc.vector.reciprocal(na, sv))
            link(nc.vector.tensor_tensor(sv, e, na, ALU.mult))
            link(nc.vector.tensor_tensor(s2, sv, sv, ALU.mult))
            link(nc.vector.tensor_scalar(na, s2, 1.0 / 17, None, ALU.mult))
            for odd in (15, 13, 11, 9, 7, 5, 3):
                link(nc.vector.scalar_tensor_tensor(na, na, 1.0 / odd, s2, ALU.add, ALU.mult))
            link(nc.vector.scalar_tensor_tensor(na, na, 1.0, sv, ALU.add, ALU.mult))
            link(nc.vector.tensor_scalar(v, v, 0.0, None, ALU.max))
            link(nc.vector.scalar_tensor_tensor(dtv, na, 2.0, v, ALU.mult, ALU.add))
            dve.wait_ge(soft_act, 2)
            ea = ssm_rows[:, HEADS:2 * HEADS].unsqueeze(1).broadcast_to([P, NCH, HEADS])
            nc.vector.scalar_tensor_tensor(a_tok[:, :, :], dt_tok[:, :, :], -1.0, ea, ALU.mult, ALU.mult).then_inc(soft_dve, 1)
            dve.wait_ge(soft_dve, SOFT_A + 1)
            conv_vector(dve, 0, 0, 2, bank[2])
            conv_vector(dve, 0, 0, 3, bank[3])
            dve.wait_ge(soft_act, 3)
            nc.vector.tensor_tensor(dd_tok[:, :, :], dd_tok[:, :, :], dt_tok[:, :, :], ALU.mult).then_inc(soft_dve, 1)
            nc.vector.memset(x_pad[:, :, :, :], 0.0).then_inc(soft_dve, 1)
            nc.vector.memset(state[:, :, :, :], 0.0).then_inc(soft_dve, 1)
            dve.wait_ge(soft_dve, SOFT_A + 4)
            dve.wait_ge(ssm_consts, 6)

            def by_head(tok, c, g):
                return tok[:, c, :].rearrange("p (g h) -> p g h", h=HPG)[:, g, :]

            def group(i, pp, last=False):
                g = 2 * i + pp
                b4 = n4 + 1 + 3 * i

                def decays(c):
                    a = by_head(a_tok, c, g).unsqueeze(2).broadcast_to([P, HPG, P])
                    nc.vector.tensor_tensor(ta[:, :, :], upto[:, :].unsqueeze(1).broadcast_to([P, HPG, P]), a,
                                            ALU.mult).then_inc(ta_ready, 1)

                def mix(c):
                    dve.wait_ge(turned, 4 * g + c + 1)
                    xt = bank[4][:, 0:2 * P].rearrange("p (q r d) -> p q r d", q=2, r=2)
                    dt = by_head(dt_tok, c, g).rearrange("p (q r) -> p q r", q=2)
                    for r in range(2):
                        nc.vector.tensor_tensor(x_pad[:, r, :, r * HDIM:(r + 1) * HDIM], xt[:, :, r, :],
                                                dt[:, :, r].unsqueeze(2).broadcast_to([P, 2, HDIM]), ALU.mult)
                    dd = by_head(dd_tok, c, g).unsqueeze(2).broadcast_to([P, HPG, HDIM])
                    nc.vector.tensor_tensor(x_dec[:, :, :], bank[4][:, 0:2 * P].rearrange("p (h d) -> p h d", h=HPG), dd,
                                            ALU.mult)
                    nc.vector.tensor_copy(b_tok[:, :], bank[4][:, 2 * P:3 * P])
                    nc.vector.tensor_tensor(gm_t[:, :], cb, upto[:, :], ALU.mult).then_inc(g_ready, 1)
                    dve.wait_ge(g_ready, 4 * g + c + 1)
                    dve.wait_ge(el_ready, 4 * g + c + 1)
                    nc.vector.tensor_tensor(el[:, :, :], el[:, :, :], gm_t[:, :].unsqueeze(1).broadcast_to([P, HPG, P]),
                                            ALU.mult)
                    dve.wait_ge(ee_ready, 4 * g + c + 1)
                    nc.vector.tensor_copy(chunk_dec[:, :], ee[:, :, P - 1]).then_inc(cd_ready, 1)
                    dve.wait_ge(cd_ready, 4 * g + c + 1)
                    nc.vector.tensor_tensor(ee[:, :, :], ee[:, :, :],
                                            bc[:, pp, 1, chunk[c]].unsqueeze(1).broadcast_to([P, HPG, P]),
                                            ALU.mult).then_inc(mixed, 1)

                def carry(c):
                    dve.wait_ge(st_done, 3 * g + c + 1)
                    dve.wait_ge(mixed, 4 * g + c + 1)
                    for h in range(HPG):
                        r = h % 2
                        cur = state[:, r, h // 2, r * HDIM:(r + 1) * HDIM]
                        new = bank[7][:, h * HDIM:(h + 1) * HDIM]
                        if c == 0:
                            last_op = nc.vector.tensor_copy(cur, new)
                        else:
                            last_op = nc.vector.scalar_tensor_tensor(cur, cur, chunk_dec[:, h:h + 1], new,
                                                                     ALU.mult, ALU.add)
                    last_op.then_inc(state_ready, 1)
                    dve.wait_ge(state_ready, 3 * g + c + 1)

                for s in range(6):
                    if not last or s < 2:
                        prep_lo(dve, b4, 6 * pp + s + 2)
                    if not last and s >= 3:
                        conv_vector(dve, g + 1, 1 - pp, s - 3, bank[(s - 3) % 2])
                    if 2 <= s <= 4:
                        carry(s - 2)
                    if 1 <= s <= 4:
                        mix(s - 1)
                    if s == 0:
                        decays(0)
                    if 1 <= s <= 3:
                        decays(s)
                dve.wait_ge(y_done, 4 * g + NCH)
                dve.wait_ge(silu_z, 2 * g + 2)
                dve.wait_ge(y_lo_ready, ONE + 2 * g)
                for t in range(2):
                    nc.vector.scalar_tensor_tensor(tmp[:, t, :], xs[:, pp, t, :],
                                                   ssm_cols[:, bass.ds(2 * g + (SSM_CONV + t), 1)],
                                                   bank[2 + t][:, :], ALU.mult, ALU.add).then_inc(gate_step, 1)
                    dve.wait_ge(gate_step, 4 * g + 2 * t + 1)
                    nc.vector.tensor_tensor(tmp[:, t, :], tmp[:, t, :], zs[:, t, :], ALU.mult).then_inc(gate_step, 1)
                if not last:
                    conv_vector(dve, g + 1, 1 - pp, 3, bank[1])
                dve.wait_ge(grs_step, 2 * g + 2)
                for t in range(2):
                    dve.wait_ge(gate_step, 4 * g + 2 * t + 2)
                    nc.vector.scalar_tensor_tensor(tmp[:, t, :], tmp[:, t, :],
                                                   ssm_cols[:, bass.ds(2 * g + (SSM_CONV + 16 + t), 1)],
                                                   rstd[:, :], ALU.mult, ALU.mult).then_inc(yn_ready, 1)
                for t in range(2):
                    dve.wait_ge(y_hi_ready, 2 * g + t + 1)
                    nc.vector.tensor_tensor(y_lo[:, 2 * g + t, :], tmp[:, t, :], y_hi[:, 2 * g + t, :],
                                            ALU.subtract).then_inc(y_lo_ready, 1)

            with dve.Fori(0, GROUPS // 2 - 1) as i:
                group(i, 0)
                group(i, 1)
            group(GROUPS // 2 - 1, 0)
            group(GROUPS // 2 - 1, 1, last=True)
            project_vector(dve, S_OUT, 2, 2, lambda j: mod[:, M_GMA, bass.ds(j, 1)], 2)

        k_ready, v_ready = sem("k_ready"), sem("v_ready")

        def kv_tensor(pe):
            n4 = S_KV // 4
            ready = lambda j: pe.wait_ge(h_lo_ready, 8 * 3 + j + 1)
            use_pair(pe, n4, 0, bank[0:2], hkv_hi, hkv_lo, ready)
            for l in range(2, 4):
                pe.wait_ge(w_lo, 4 * n4 + l + 1)
                for c in range(NCH):
                    for k in range(DT):
                        w = slice(k * P, (k + 1) * P)
                        mm = product3(bank[l][:, chunk[c]], hkv_hi[:, k, chunk[c]], hkv_lo[:, k, chunk[c]],
                                      w_hi_sb[:, l, w], w_lo_sb[:, l, w], k == 0, k == DT - 1)
                mm.then_inc(slab_used, 1)

        def kv_scalar(act):
            n4 = S_KV // 4
            prep_hi(act, n4, 2)
            prep_hi(act, n4, 3)
            norm_scalar(act, 4, M_SH1B, h_hi)
            for l in range(2):
                act.wait_ge(slab_used, RING + S_KV + l + 1)
                b = COLS["b_k"][0] + l
                nc.scalar.activation(k_all[:, l, :], bank[l][:, :], ACT.Identity, bias=cols[:, b:b + 1]).then_inc(k_ready, 1)
            prep_hi(act, n4, 4)
            prep_hi(act, n4, 5)

        def kv_vector(dve):
            n4 = S_KV // 4
            prep_lo(dve, n4, 2)
            prep_lo(dve, n4, 3)
            columns_vector(dve, 7, M_SC1B, col("nw_ffn2"))
            norm_vector(dve, 3, 4, M_SH1B, h_hi, h_lo)
            dve.wait_ge(att_loaded, 16)
            for l in range(2, 4):
                prep_lo(dve, n4, l + 2)
            for l in range(2, 4):
                dve.wait_ge(slab_used, RING + S_KV + l + 1)
                o = slice((l - 2) * P, (l - 1) * P)
                nc.vector.tensor_tensor(v_all[:, :, o], bank[l][:, :].rearrange("p (c d) -> p c d", c=NCH),
                                        att_rows[:, o].unsqueeze(1).broadcast_to([P, NCH, P]), ALU.add).then_inc(v_ready, 1)

        att_consts, bq_ready, q_ready, gb_step = sem("att_consts"), sem("bq_ready"), sem("q_ready"), sem("gb_step")
        pad_ready, q_cur_ready, scored = sem("pad_ready"), sem("q_cur_ready"), sem("scored")
        masked, max_step, exp_ready, sink_exp = sem("masked"), sem("max_step"), sem("exp_ready"), sem("sink_exp")
        den_step, normed, probs_turned = sem("den_step"), sem("normed"), sem("probs_turned")
        pt_a_ready, pt_b_ready, o_done, o_hi_ready, o_lo_ready = (
            sem("pt_a_ready"), sem("pt_b_ready"), sem("o_done"), sem("o_hi_ready"), sem("o_lo_ready"))

        def att_tensor(pe):
            ready = lambda j: pe.wait_ge(h_lo_ready, 8 * 5 + j + 1)
            with pe.Fori(0, 2) as i:
                pe.wait_ge(q_ready, ONE + 4 * i)
                use_pair(pe, S_Q // 4 + i, 0, bank[0:2], h_hi, h_lo, ready)
                use_pair(pe, S_Q // 4 + i, 2, bank[2:4], h_hi, h_lo)
            pe.wait_ge(att_consts, 6)

            def unit(kt, tt, half):
                u = 8 * kt + 2 * tt + half
                if tt == 0 and half == 0:
                    pe.wait_ge(pad_ready, 3 * kt + 3)
                if half == 0:
                    pe.wait_ge(q_cur_ready, 4 * kt + tt + 1)
                pe.wait_ge(masked, ONE + 2 * u)
                for ab in range(2):
                    for b in range(2):
                        q0 = (2 * half + b) * P
                        mm = nc.tensor.matmul(bank[2 + ab][:, b * 2 * P:(b + 1) * 2 * P], q_cur[:, tt % 2, q0:q0 + P],
                                              k_pad[:, ab, q0:q0 + 2 * P], start=True, stop=True)
                    mm.then_inc(scored, 1)

            def values(kt, tt, half):
                u = 8 * kt + 2 * tt + half
                pe.wait_ge(normed, u + 1)
                for ab in range(2):
                    for b in range(2):
                        for part in range(2):
                            if half == 0 and b == 0 and part == 0:
                                continue
                            mm = nc.tensor.transpose(bank[4 + ab][:, (2 * b + part) * P:(2 * b + part + 1) * P],
                                                     probs[:, half, 2 * ab + b, part * P:(part + 1) * P], ident_a[:, :])
                    mm.then_inc(probs_turned, 1)
                pe.wait_ge(pt_a_ready, u + 1)
                pe.wait_ge(pt_b_ready, u + 1)
                if half == 0:
                    pe.wait_ge(o_lo_ready, ONE + 4 * kt + tt)
                for b in range(2):
                    blk = 2 * half + b
                    parts = [(ab, part) for part in range(2) for ab in range(2) if blk + part > 0]
                    for n, (ab, part) in enumerate(parts):
                        mm = nc.tensor.matmul(bank[7][:, blk * P:(blk + 1) * P], v_pad[:, blk - 1 + part, ab, :],
                                              probs_t[:, ab, 2 * b + part, :], start=(n == 0), stop=(n == len(parts) - 1))
                mm.then_inc(o_done, 1)

            with pe.Fori(0, 2) as kt:
                unit(kt, 0, 0)
                for n in range(8):
                    if n < 7:
                        unit(kt, (n + 1) // 2, (n + 1) % 2)
                    values(kt, n // 2, n % 2)
            project_tensor(pe, S_O, 8, 1, 4, o_hi, o_lo, lambda f: pe.wait_ge(o_lo_ready, ONE + f + 1), 5)

        def att_scalar(act):
            act.wait_ge(bq_ready, 1)
            with act.Fori(0, 2) as i:
                for u in range(2):
                    prep_hi(act, S_Q // 4 + i, 2 * u + 2)
                    prep_hi(act, S_Q // 4 + i, 2 * u + 3)
                    for t in range(2 * u, 2 * u + 2):
                        act.wait_ge(slab_used, RING + S_Q + 4 * i + t + 1)
                        nc.scalar.activation(q_all[:, 4 * i + t, :], bank[t][:, :], ACT.Identity,
                                             bias=bq8[:, bass.ds(4 * i + t, 1)], scale=HDIM ** -0.5).then_inc(q_ready, 1)
            act.wait_ge(q_ready, ONE + 8)

            def copy_q(kt, tt):
                if tt >= 2:
                    act.wait_ge(scored, ONE + 2 * (8 * kt + 2 * tt - 2))
                else:
                    act.wait_ge(scored, ONE + 16 * kt)
                nc.scalar.activation(q_cur[:, tt % 2, :], q_all[:, 4 * kt + tt, :], ACT.Copy).then_inc(q_cur_ready, 1)

            def unit(kt, tt, half):
                u = 8 * kt + 2 * tt + half
                st = stat4[:, half, :, :]
                act.wait_ge(max_step, 4 * u + 4)
                for n in range(4):
                    nc.scalar.activation(probs[:, half, n, :], probs[:, half, n, :], ACT.Exp, bias=st[:, 1, n:n + 1],
                                         accum_out=st[:, 3, n:n + 1]).then_inc(exp_ready, 1)
                nc.scalar.activation(st[:, 2, :], st[:, 2, :], ACT.Exp).then_inc(sink_exp, 1)

            def turned_a(kt, tt, half):
                u = 8 * kt + 2 * tt + half
                lo = P if half == 0 else 0
                act.wait_ge(probs_turned, 2 * u + 2)
                nc.scalar.activation(probs_t[:, 0, :, :].rearrange("p n q -> p (n q)")[:, lo:], bank[4][:, lo:],
                                     ACT.Copy).then_inc(pt_a_ready, 1)
                if half == 1:
                    act.wait_ge(o_done, ONE + u + 1)
                    nc.scalar.activation(o_hi[:, 4 * kt + tt, :], bank[7][:, :], ACT.Copy).then_inc(o_hi_ready, 1)

            with act.Fori(0, 2) as kt:
                copy_q(kt, 0)
                copy_q(kt, 1)
                unit(kt, 0, 0)
                for n in range(8):
                    if n < 7:
                        unit(kt, (n + 1) // 2, (n + 1) % 2)
                    if n in (2, 4):
                        copy_q(kt, n // 2 + 1)
                    turned_a(kt, n // 2, n % 2)
            project_scalar(act, S_O, 1, 4, 5)

        def att_vector(dve):
            b = COLS["b_q"][0]
            nc.vector.tensor_scalar(bq8[:, :], cols[:, b:b + DT], HDIM ** -0.5, None, ALU.mult).then_inc(bq_ready, 1)
            nc.vector.tensor_tensor(gb_o[:, :], mod[:, M_GMB, :], col("b_o"), ALU.mult).then_inc(gb_step, 1)
            dve.wait_ge(gb_step, 1)
            for j in range(DT):
                nc.vector.tensor_scalar(x[:, j, :], x[:, j, :], gb_o[:, j:j + 1], None, ALU.add).then_inc(gb_step, 1)
            with dve.Fori(0, 2) as i:
                for t in range(4):
                    prep_lo(dve, S_Q // 4 + i, t + 2)
            dve.wait_ge(att_consts, 8)
            dve.wait_ge(k_ready, 2)
            dve.wait_ge(v_ready, 2)

            def pads(kt):
                dve.wait_ge(o_done, ONE + 8 * kt)
                for ab in range(2):
                    half = slice(ab * HDIM, (ab + 1) * HDIM)
                    nc.vector.tensor_copy(k_pad[half, ab, P:], k_all[half, kt, :]).then_inc(pad_ready, 1)
                v = v_all[:, :, :].rearrange("p c (k d) -> p c k d", k=2)
                for ab in range(2):
                    half = slice(ab * HDIM, (ab + 1) * HDIM)
                    op = nc.vector.tensor_copy(v_pad[:, :, ab, half], v[:, :, kt, half])
                op.then_inc(pad_ready, 1)

            def scores(kt, tt, half):
                u = 8 * kt + 2 * tt + half
                st = stat4[:, half, :, :]
                for ab in range(2):
                    dve.wait_ge(scored, ONE + 2 * u + ab + 1)
                    nc.vector.tensor_tensor(probs[:, half, 2 * ab:2 * ab + 2, :],
                                            bank[2 + ab][:, :].rearrange("p (b k) -> p b k", b=2), mask[:, half, :, :],
                                            ALU.add).then_inc(masked, 1)
                dve.wait_ge(masked, ONE + 2 * u + 2)
                nc.vector.tensor_reduce(st[:, 0, :], probs[:, half, :, :], AX.X, ALU.max).then_inc(max_step, 1)
                dve.wait_ge(max_step, 4 * u + 1)
                sink = att_rows[:, KV * HDIM:].rearrange("p (t a) -> p t a", a=2)[:, 4 * kt + tt, :]
                sink = sink.unsqueeze(2).broadcast_to([P, 2, 2])
                four = lambda r: st[:, r, :].rearrange("p (a b) -> p a b", a=2)
                nc.vector.tensor_tensor(four(0), four(0), sink, ALU.max).then_inc(max_step, 1)
                dve.wait_ge(max_step, 4 * u + 2)
                nc.vector.tensor_scalar(st[:, 1, :], st[:, 0, :], -1.0, None, ALU.mult).then_inc(max_step, 1)
                nc.vector.tensor_tensor(four(2), sink, four(0), ALU.subtract).then_inc(max_step, 1)

            def normalise(kt, tt, half):
                u = 8 * kt + 2 * tt + half
                st = stat4[:, half, :, :]
                dve.wait_ge(exp_ready, 4 * u + 4)
                dve.wait_ge(sink_exp, u + 1)
                nc.vector.tensor_tensor(st[:, 4, :], st[:, 3, :], st[:, 2, :], ALU.add).then_inc(den_step, 1)
                dve.wait_ge(den_step, 2 * u + 1)
                nc.vector.reciprocal(st[:, 5, :], st[:, 4, :]).then_inc(den_step, 1)
                dve.wait_ge(den_step, 2 * u + 2)
                for n in range(4):
                    op = nc.vector.tensor_scalar(probs[:, half, n, :], probs[:, half, n, :], st[:, 5, n:n + 1], None, ALU.mult)
                op.then_inc(normed, 1)

            def turned_b(kt, tt, half):
                u = 8 * kt + 2 * tt + half
                lo = P if half == 0 else 0
                dve.wait_ge(probs_turned, 2 * u + 2)
                nc.vector.tensor_copy(probs_t[:, 1, :, :].rearrange("p n q -> p (n q)")[:, lo:],
                                      bank[5][:, lo:]).then_inc(pt_b_ready, 1)
                if half == 1:
                    dve.wait_ge(o_hi_ready, 4 * kt + tt + 1)
                    nc.vector.tensor_tensor(o_lo[:, 4 * kt + tt, :], bank[7][:, :], o_hi[:, 4 * kt + tt, :],
                                            ALU.subtract).then_inc(o_lo_ready, 1)

            with dve.Fori(0, 2) as kt:
                pads(kt)
                scores(kt, 0, 0)
                for n in range(8):
                    normalise(kt, n // 2, n % 2)
                    if n < 7:
                        scores(kt, (n + 1) // 2, (n + 1) % 2)
                    turned_b(kt, n // 2, n % 2)
            dve.wait_ge(gb_step, 9)
            project_vector(dve, S_O, 1, 4, lambda j: mod[:, M_GMB, bass.ds(j, 1)], 5)

        mods0 = range(MOD_FIRST, MOD_FIRST + MOD_IN_FFN0)
        mods1 = range(MOD_FIRST + MOD_IN_FFN0, NMOD)

        @block.sync
        def _(sp):
            sp.dma_start(cols[:, :], cols_in).then_inc(in_loaded, 16)
            for q in range(4 * MOD_FIRST):
                sp.dma_start(first_mod[:, 2 * q:2 * q + 2, :],
                             w_mod[2 * q:2 * q + 2].rearrange("m p d -> p m d")).then_inc(first_loaded[q], 16)
                if q == 0:
                    sp.dma_start(x[:, :, :].rearrange("p j t -> p (j t)"), x_in).then_inc(x_loaded, 16)
                if q >= 6:
                    sp.dma_start(raw[:, q - 6, :], w_stream[q - 6]).then_inc(raw_loaded[q - 6], 16)
            for n in (2, 3):
                sp.dma_start(raw[:, n, :], w_stream[n]).then_inc(raw_loaded[n], 16)
            for m in range(2):
                load_mod(sp, 8 * MOD_FIRST + m, m, first=True)
            for n in (4, 5):
                load_slab(sp, n, n % RING)

            def slabs_and_mods(n0, m0, turns):
                def turn(i, last):
                    for u in range(2):
                        for q in range(4):
                            if not last or 4 * u + q < 6:
                                load_mod(sp, 8 * i + (m0 + 4 * u + q + 2), q % 2)
                            if q < 2:
                                load_slab(sp, 4 * i + (n0 + 2 * u + q), (n0 + 2 * u + q) % RING)
                with sp.Fori(0, turns - 1) as i:
                    turn(i, False)
                turn(turns - 1, True)

            def slabs(n0, n1):
                whole = (n1 - n0) // RING
                with sp.Fori(0, whole) as i:
                    for q in range(RING):
                        load_slab(sp, 4 * i + (n0 + q), (n0 + q) % RING)
                for n in range(n0 + whole * RING, n1):
                    load_slab(sp, n, n % RING)

            slabs_and_mods(6, 8 * MOD_FIRST, MOD_IN_FFN0)
            n = 6 + 4 * MOD_IN_FFN0
            slabs(n, S_IN)
            sp.wait_ge(slab_used, RING + S_IN)
            sp.dma_start(ssm_cols[:, :], ssm_cols_in).then_inc(ssm_loaded, 16)
            sp.dma_start(wdt[:, :, :].rearrange("p k h -> p (k h)"), w_dt).then_inc(ssm_loaded, 16)
            sp.dma_start(ssm_rows[:, :], ssm_rows_in.partition_broadcast(P)).then_inc(ssm_loaded, 16)
            slabs(S_IN, S_FFN1 + 6)
            sp.wait_ge(slab_used, RING + S_FFN1)
            for m in range(2):
                load_mod(sp, 8 * mods1[0] + m, m)
            slabs_and_mods(S_FFN1 + 6, 8 * mods1[0], MOD_IN_FFN1)
            slabs(S_FFN1 + 6 + 4 * MOD_IN_FFN1, S_KV)
            sp.wait_ge(mod_mm, NMOD)
            sp.dma_start(att_rows[:, :], att_rows_in.partition_broadcast(P)).then_inc(att_loaded, 16)
            slabs(S_KV, SLABS)
            for j in range(DT):
                sp.wait_ge(out_ready, j + 1)
                sp.dma_start(out[:, j, :], x[:, j, :]).then_inc(out_stored, 16)
            sp.wait_ge(out_stored, 16 * DT)

        @block.gpsimd
        def _(pool):
            nc.gpsimd.memset(ones[:, :], 1.0).then_inc(slab_used, RING)
            nc.gpsimd.memset(eps[:, :], EPS).then_inc(consts, 1)
            for n, starts_at_one in enumerate((a_ready, a_lo_ready, y_lo_ready, gstat_done, q_ready, scored, masked,
                                               o_done, o_lo_ready)):
                nc.gpsimd.memset(spare[:, n:n + 1], 0.0).then_inc(starts_at_one, 1)
            pool.wait_ge(slab_used, RING + S_IN)
            pool.wait_ge(a_lo_ready, ONE + FT)
            for m, fill in ((after, 0.0), (upto, 1.0), (ident, 0.0)):
                nc.gpsimd.memset(m[:, :], fill).then_inc(ssm_consts, 1)
            pool.wait_ge(ssm_consts, 3)
            nc.gpsimd.affine_select(out=after[:, :], in_=after[:, :], compare_op=ALU.is_ge, fill=1.0, base=0,
                                    pattern=[[1, P]], channel_multiplier=-1).then_inc(ssm_consts, 1)
            nc.gpsimd.affine_select(out=upto[:, :], in_=upto[:, :], compare_op=ALU.is_ge, fill=0.0, base=0,
                                    pattern=[[1, P]], channel_multiplier=-1).then_inc(ssm_consts, 1)
            nc.gpsimd.affine_select(out=ident[:, :], in_=ident[:, :], compare_op=ALU.not_equal, fill=1.0, base=0,
                                    pattern=[[-1, P]], channel_multiplier=1).then_inc(ssm_consts, 1)
            pool.wait_ge(slab_used, RING + S_Q)
            nc.gpsimd.memset(mask[:, :, :, :], 0.0).then_inc(att_consts, 1)
            nc.gpsimd.memset(ident_a[:, :], 0.0).then_inc(att_consts, 1)
            nc.gpsimd.memset(k_pad[:, :, :], 0.0).then_inc(att_consts, 1)
            nc.gpsimd.memset(v_pad[:, :, :, :], 0.0).then_inc(att_consts, 1)
            pool.wait_ge(att_consts, 4)
            nc.gpsimd.affine_select(out=ident_a[:, :], in_=ident_a[:, :], compare_op=ALU.not_equal, fill=1.0, base=0,
                                    pattern=[[-1, P]], channel_multiplier=1).then_inc(att_consts, 1)
            m4 = mask[:, :, :, :].rearrange("p h b k -> p (h b) k")
            nc.gpsimd.affine_select(out=m4, in_=m4, compare_op=ALU.is_gt, fill=MASKED, base=0,
                                    pattern=[[0, 4], [1, 2 * P]], channel_multiplier=-1).then_inc(att_consts, 1)
            pool.wait_ge(att_consts, 6)
            nc.gpsimd.affine_select(out=m4, in_=m4, compare_op=ALU.is_ge, fill=MASKED, base=P,
                                    pattern=[[0, 4], [-1, 2 * P]], channel_multiplier=1).then_inc(att_consts, 1)
            pool.wait_ge(att_consts, 7)
            nc.gpsimd.memset(mask[:, 0, 0, 0:P], MASKED).then_inc(att_consts, 1)

        @block.scalar
        def _(act):
            act.wait_ge(in_loaded, 16)
            nc.scalar.activation(c_act[:, :], col("c"), ACT.Silu).then_inc(c_ready, 1)
            act.wait_ge(x_loaded, 16)
            for j in range(DT):
                nc.scalar.activation(first_sq[:, j, :], x[:, j, :], ACT.Square).then_inc(first_sq_ready, 1)
            prep_hi(act, 0, 0)
            prep_hi(act, 0, 1)
            act.wait_ge(consts, 1)
            rstd_scalar(act, 0)
            act.wait_ge(mod_col, 2)
            norm_scalar(act, 0, M_SH1A, h_hi)
            ffn_scalar(act, 0, S_FFN0, 1, mods0)
            rstd_scalar(act, 1)
            norm_scalar(act, 1, M_SHMA, h_hi)
            ssm_scalar(act)
            rstd_scalar(act, 2)
            norm_scalar(act, 2, M_SH2A, h_hi)
            ffn_scalar(act, 1, S_FFN1, 3, mods1)
            rstd_scalar(act, 3)
            norm_scalar(act, 3, M_KVSH, hkv_hi)
            kv_scalar(act)
            ffn_scalar(act, 2, S_FFN2, 4, ())
            rstd_scalar(act, 4)
            norm_scalar(act, 5, M_SHMB, h_hi)
            att_scalar(act)
            rstd_scalar(act, 5)
            norm_scalar(act, 6, M_SH2B, h_hi)
            ffn_scalar(act, 3, S_FFN3, 6, (), last=True)
            rstd_scalar(act, 6)

        @block.vector
        def _(dve):
            dve.wait_ge(c_ready, 1)
            for v in range(MOD_FIRST):
                for k in range(8):
                    mod_block(dve, v, k, first=True)
                if v == MOD_FIRST - 1:
                    prep_lo(dve, 0, 0)
                    prep_lo(dve, 0, 1)
                mod_collect(dve, v)
            dve.wait_ge(mod_col, 2)
            columns_vector(dve, 1, M_SC1A, col("nw_ffn0"))
            norm_vector(dve, 0, 0, M_SH1A, h_hi, h_lo)
            ffn_vector(dve, 0, S_FFN0, M_G1A, 1, mods0, 1)
            columns_vector(dve, 3, M_SCMA, col("nw_mix0"))
            norm_vector(dve, 1, 1, M_SHMA, h_hi, h_lo)
            ssm_vector(dve)
            columns_vector(dve, 4, M_SC2A, col("nw_ffn1"))
            norm_vector(dve, 2, 2, M_SH2A, h_hi, h_lo)
            ffn_vector(dve, 1, S_FFN1, M_G2A, 3, mods1, 4)
            columns_vector(dve, 6, M_KVSC, col("nw_kv"))
            norm_vector(dve, 3, 3, M_KVSH, hkv_hi, hkv_lo)
            kv_vector(dve)
            ffn_vector(dve, 2, S_FFN2, M_G1B, 4, (), 7)
            columns_vector(dve, 9, M_SCMB, col("nw_mix1"))
            norm_vector(dve, 4, 5, M_SHMB, h_hi, h_lo)
            att_vector(dve)
            columns_vector(dve, 10, M_SC2B, col("nw_ffn3"))
            norm_vector(dve, 5, 6, M_SH2B, h_hi, h_lo)
            ffn_vector(dve, 3, S_FFN3, M_G2B, 6, (), 10, last=True)
            dve.wait_ge(rs_step, 14)
            w = COLS["nw_final"][0]
            for j in range(DT):
                nc.vector.scalar_tensor_tensor(x[:, j, :], x[:, j, :], cols[:, w + j:w + j + 1], rstd[:, :],
                                               ALU.mult, ALU.mult).then_inc(out_ready, 1)

        @block.tensor
        def _(pe):
            pe.wait_ge(slab_used, RING)
            for j in range(DT):
                pe.wait_ge(first_sq_ready, j + 1)
                mm = nc.tensor.matmul(bank[6][:, :], ones[:, :], first_sq[:, j, :], start=(j == 0), stop=(j == DT - 1))
            mm.then_inc(stat_done, 1)
            mod_sum(pe, 0, first=True)
            mod_sum(pe, 1)
            ffn_tensor(pe, 0, S_FFN0, 0, 1, mods0)
            ssm_tensor(pe)
            ffn_tensor(pe, 1, S_FFN1, 2, 3, mods1)
            kv_tensor(pe)
            ffn_tensor(pe, 2, S_FFN2, 4, 4, ())
            att_tensor(pe)
            ffn_tensor(pe, 3, S_FFN3, 6, 6, (), last=True)


def lay_out(i):
    import numpy as np

    def tiles(w):
        kt, nt = w.shape[0] // P, w.shape[1] // P
        return np.ascontiguousarray(w.reshape(kt, P, nt, P).transpose(2, 1, 0, 3)).reshape(nt, P, kt * P)

    def cut(w, per):
        n, _, width = w.shape
        full = np.zeros((n, P, per * SLAB), w.dtype)
        full[:, :, :width] = w
        return full.reshape(n, P, per, SLAB).transpose(0, 2, 1, 3).reshape(n * per, P, SLAB)

    def ffn(layer, half):
        gu = i["ffn_w_gu"][layer, half]
        pairs = np.stack([tiles(gu[:, :FF]), tiles(gu[:, FF:])], 1).reshape(GU_SLABS, P, SLAB)
        return [pairs, cut(tiles(i["ffn_w_down"][layer, half]), DOWN_SPJ)]

    def columns(v):
        return v.reshape(-1, P).T

    w_in = i["ssm_w_in"][0]
    z, xbc = tiles(w_in[:, :DIN]), tiles(w_in[:, DIN:DIN + DIN + 2 * GROUPS * P])

    def group_order(t, g):
        return [t[2 * g], t[2 * g + 1], t[16 + g], t[24 + g]]

    order = group_order(xbc, 0)
    for g in range(GROUPS):
        order += [z[2 * g], z[2 * g + 1]]
        if g < GROUPS - 1:
            order += group_order(xbc, g + 1)
    heads = [8 * kt + 4 * ab + tt for kt in range(2) for tt in range(4) for ab in range(2)]
    feats = np.concatenate([np.arange(HDIM) + h * HDIM for h in heads])
    stream = np.concatenate(
        ffn(0, 0) + [np.stack(order), cut(tiles(i["ssm_w_out"][0]), 2)] + ffn(0, 1) + [tiles(i["w_kv"])] + ffn(1, 0)
        + [tiles(i["attn_w_q"][0][:, feats]), tiles(i["attn_w_o"][0][feats])] + ffn(1, 1))
    mods = np.concatenate([i["mod_w"][0], i["kv_mod_w"], i["mod_w"][1]], 1)
    w_mod = np.ascontiguousarray(mods.reshape(DT, P, NMOD, D).transpose(2, 0, 1, 3)).reshape(NMOD * DT, P, D)
    mod_b = np.concatenate([i["mod_b"][0], i["kv_mod_b"], i["mod_b"][1]])
    w_dt = np.ascontiguousarray(w_in[:, -HEADS:].reshape(DT, P, HEADS).transpose(1, 0, 2)).reshape(P, DT * HEADS)
    cols = np.concatenate([columns(v) for v in (
        i["c"], mod_b, i["ffn_norm_w"][0, 0], i["ffn_norm_w"][0, 1], i["ffn_norm_w"][1, 0], i["ffn_norm_w"][1, 1],
        i["mix_norm_w"][0], i["mix_norm_w"][1], i["kv_norm_w"], i["final_norm_w"], i["attn_b_o"][0],
        i["attn_b_q"][0][feats], i["b_kv"][:KV * HDIM])], 1)
    taps = np.concatenate([i["ssm_conv_w"][0], i["ssm_conv_b"]], 0).reshape(5, 32, P)
    taps = np.stack([np.stack(group_order(taps.transpose(1, 2, 0), g)) for g in range(GROUPS)])
    ssm_cols = np.concatenate([taps.transpose(2, 0, 1, 3).reshape(P, SSM_CONV),
                               columns(np.repeat(i["ssm_d"][0], HDIM)), columns(i["ssm_norm_w"][0])], 1)
    ssm_rows = np.concatenate([i["ssm_dt_bias"][0], i["ssm_a_log"][0]])
    att_rows = np.concatenate([i["b_kv"][KV * HDIM:], i["attn_sinks"][0][np.array(heads)]])
    x_t = np.ascontiguousarray(i["x"][0].T.reshape(DT, P, T).transpose(1, 0, 2)).reshape(P, DT * T)
    return {"w_stream": stream, "w_mod": w_mod, "w_dt": w_dt, "x_in": x_t, "cols_in": np.ascontiguousarray(cols),
            "ssm_cols_in": np.ascontiguousarray(ssm_cols), "ssm_rows_in": ssm_rows, "att_rows_in": att_rows}


def kernel(**inputs):
    import numpy as np
    import concourse.bacc as bacc
    from concourse.bass_utils import run_bass_kernel_spmd

    arrays = lay_out({k: np.asarray(v) for k, v in inputs.items()})
    nc = bacc.Bacc("TRN2", target_bir_lowering=False, num_devices=1)
    args = [nc.dram_tensor(n, a.shape, mybir.dt.from_np(a.dtype), kind="ExternalInput").ap() for n, a in arrays.items()]
    out = nc.dram_tensor("trunk_out", (P, DT, T), F32, kind="ExternalOutput").ap()
    trunk(nc, *args, out)
    r = run_bass_kernel_spmd(nc, [arrays], core_ids=[0])
    got = r.results[0]["trunk_out"]
    return got.transpose(2, 1, 0).reshape(1, T, D)
```

```python
from contextlib import ExitStack

import concourse.bass as bass
from concourse import mybir

F32 = mybir.dt.float32
F32R = mybir.dt.float32r
ALU = mybir.AluOpType
ACT = mybir.ActivationFunctionType
AX = mybir.AxisListType

P = 128
D = 1024
T = 512
DT = D // P
FF = 2816
FT = FF // P
DIN = 2048
HEADS, GROUPS, HPG, HDIM = 32, 8, 4, 64
NCH = T // P
KV, QH = 4, 16
EPS = 1e-5
MASKED = -3.0e38

RING = 4
ONE = 1
SLAB = 8 * P
GU_SLABS = 2 * FT
DOWN_SPJ = 3
FFN_SLABS = GU_SLABS + DOWN_SPJ * DT
IN_SLABS = 6 * GROUPS
OUT_SLABS = 2 * DT
KV_SLABS = 4
Q_SLABS = DT
O_SLABS = DT

S_FFN0 = 0
S_IN = S_FFN0 + FFN_SLABS
S_OUT = S_IN + IN_SLABS
S_FFN1 = S_OUT + OUT_SLABS
S_KV = S_FFN1 + FFN_SLABS
S_FFN2 = S_KV + KV_SLABS
S_Q = S_FFN2 + FFN_SLABS
S_O = S_Q + Q_SLABS
S_FFN3 = S_O + O_SLABS
SLABS = S_FFN3 + FFN_SLABS

(M_SH1A, M_SC1A, M_G1A, M_SHMA, M_SCMA, M_GMA, M_SH2A, M_SC2A, M_G2A, M_KVSH, M_KVSC,
 M_SH1B, M_SC1B, M_G1B, M_SHMB, M_SCMB, M_GMB, M_SH2B, M_SC2B, M_G2B) = range(20)
NMOD = 20
MOD_FIRST = 2
MOD_GU = GU_SLABS // 8
MOD_DOWN = 4
MOD_FFN = MOD_GU + MOD_DOWN

COLS = {}
_at = 0
for _name, _n in (("c", DT), ("modb", NMOD * DT), ("nw_ffn0", DT), ("nw_ffn1", DT), ("nw_ffn2", DT), ("nw_ffn3", DT),
                  ("nw_mix0", DT), ("nw_mix1", DT), ("nw_kv", DT), ("nw_final", DT), ("b_o", DT), ("b_q", DT),
                  ("b_k", 2)):
    COLS[_name] = (_at, _at + _n)
    _at += _n
NCOLS = _at
SSM_CONV = GROUPS * 4 * 5
NSSM = SSM_CONV + 16 + 16
NROWS_S = 2 * HEADS
NROWS_A = KV * HDIM + QH


def trunk(nc, w_stream, w_mod, w_dt, x_in, cols_in, ssm_cols_in, ssm_rows_in, att_rows_in, out):
    ctx = ExitStack()
    with ctx:
        def sem(name):
            return ctx.enter_context(nc.semaphore(name))

        def sb(stack, name, shape, dt=F32):
            return stack.enter_context(nc.sbuf_tensor(name, shape, dt))

        x = sb(ctx, "x_trunk", [P, DT, T])
        h_hi = sb(ctx, "h_hi", [P, DT, T], F32R)
        h_lo = sb(ctx, "h_lo", [P, DT, T], F32R)
        raw = sb(ctx, "raw", [P, RING, SLAB])
        w_hi_sb = sb(ctx, "w_hi_sb", [P, RING, SLAB], F32R)
        w_lo_sb = sb(ctx, "w_lo_sb", [P, RING, SLAB], F32R)
        tmp = sb(ctx, "tmp", [P, 2, T])
        sumsq = sb(ctx, "sumsq", [P, T])
        rstd = sb(ctx, "rstd", [P, T])
        ones = sb(ctx, "ones", [P, P])
        eps = sb(ctx, "eps", [P, 1])
        spare = sb(ctx, "spare", [P, 17])
        cols = sb(ctx, "cols", [P, NCOLS])
        mod = sb(ctx, "mod", [P, NMOD, DT])
        c_act = sb(ctx, "c_act", [P, DT])
        scale_col = sb(ctx, "scale_col", [P, DT])
        gate_col = sb(ctx, "gate_col", [P, DT])

        def col(name):
            return cols[:, COLS[name][0]:COLS[name][1]]

        with ExitStack() as s:
            mod_raw = sb(s, "mod_raw", [P, 2, D])
            mod_acc = sb(s, "mod_acc", [P, D])
            a_hi = sb(s, "a_hi", [P, FT, T], F32R)
            a_lo = sb(s, "a_lo", [P, FT, T], F32R)
        with ExitStack() as s:
            sb(s, "gap0", [P, 3 * D])
            first_mod = sb(s, "first_mod", [P, 8 * MOD_FIRST, D])
            first_sq = sb(s, "first_sq", [P, DT, T])
        with ExitStack() as s:
            y_hi = sb(s, "y_hi", [P, 16, T], F32R)
            y_lo = sb(s, "y_lo", [P, 16, T], F32R)
            xs = sb(s, "xs", [P, 2, 2, T])
            bc = sb(s, "bc", [P, 2, 2, T])
            zs = sb(s, "zs", [P, 2, T])
            ssm_cols = sb(s, "ssm_cols", [P, NSSM])
            dt_tok = sb(s, "dt_tok", [P, NCH, HEADS])
            a_tok = sb(s, "a_tok", [P, NCH, HEADS])
            dd_tok = sb(s, "dd_tok", [P, NCH, HEADS])
            a_hi_tok = sb(s, "a_hi_tok", [P, NCH, HEADS], F32R)
            a_lo_tok = sb(s, "a_lo_tok", [P, NCH, HEADS], F32R)
            after_r = sb(s, "after_r", [P, P], F32R)
            ones_r = sb(s, "ones_r", [P, P], F32R)
            upto = sb(s, "upto", [P, P])
            ident = sb(s, "ident", [P, P])
            with ExitStack() as r:
                wdt = sb(r, "wdt", [P, DT, HEADS])
                wdt_hi = sb(r, "wdt_hi", [P, DT, HEADS], F32R)
                wdt_lo = sb(r, "wdt_lo", [P, DT, HEADS], F32R)
                ssm_rows = sb(r, "ssm_rows", [P, NROWS_S])
                soft = sb(r, "soft", [P, 5, NCH * HEADS])
                after = sb(r, "after", [P, P])
            ta_hi = sb(s, "ta_hi", [P, HPG, P], F32R)
            ta_lo = sb(s, "ta_lo", [P, HPG, P], F32R)
            el = sb(s, "el", [P, HPG, P])
            ee = sumsq[:, :].rearrange("p (h l) -> p h l", h=HPG)
            gm_t = sb(s, "gm_t", [P, P])
            b_tok = sb(s, "b_tok", [P, P])
            x_pad = sb(s, "x_pad", [P, 2, 2, P])
            x_dec = sb(s, "x_dec", [P, HPG, HDIM])
            state = sb(s, "state", [P, 2, 2, P])
            chunk_dec = sb(s, "chunk_dec", [P, HPG])
        with ExitStack() as s:
            k_all = sb(s, "k_all", [P, 2, T])
            v_all = sb(s, "v_all", [P, NCH, KV * HDIM])
            att_rows = sb(s, "att_rows", [P, NROWS_A])
            with ExitStack() as r:
                sb(r, "gap", [P, 2 * D])
                hkv_hi = sb(r, "hkv_hi", [P, DT, T], F32R)
                hkv_lo = sb(r, "hkv_lo", [P, DT, T], F32R)
            q_all = sb(s, "q_all", [P, DT, T])
            q_cur = sb(s, "q_cur", [P, 2, T])
            k_pad = sb(s, "k_pad", [P, 2, P + T])
            v_pad = sb(s, "v_pad", [P, NCH, 2, P])
            o_hi = sb(s, "o_hi", [P, DT, T], F32R)
            o_lo = sb(s, "o_lo", [P, DT, T], F32R)
            probs = sb(s, "probs", [P, 3, 4, 2 * P])
            probs_t = sb(s, "probs_t", [P, 2, 4, P])
            mask = sb(s, "mask", [P, 2, 2, 2 * P])
            ident_a = sb(s, "ident_a", [P, P])
            bq8 = sb(s, "bq8", [P, DT])
            gb_o = sb(s, "gb_o", [P, DT])
            stat4 = sb(s, "stat4", [P, 3, 6, 4])

        bank = [ctx.enter_context(nc.psum_tensor(f"bank{i}", [P, T], F32)) for i in range(8)]

        raw_loaded = [sem(f"raw_loaded{i}") for i in range(RING)]
        w_hi, w_lo, slab_used = sem("w_hi"), sem("w_lo"), sem("slab_used")
        in_loaded, x_loaded, ssm_loaded, att_loaded = sem("in_loaded"), sem("x_loaded"), sem("ssm_loaded"), sem("att_loaded")
        consts, c_ready = sem("consts"), sem("c_ready")
        mod_loaded = [sem("mod_loaded0"), sem("mod_loaded1")]
        first_loaded = [sem(f"first_loaded{i}") for i in range(8 * MOD_FIRST)]
        first_sq_ready = sem("first_sq_ready")
        mod_step, mod_mm, mod_col = sem("mod_step"), sem("mod_mm"), sem("mod_col")
        col_step = sem("col_step")
        ss_step, sq_ready, x_ready, stat_done, rs_step = (
            sem("ss_step"), sem("sq_ready"), sem("x_ready"), sem("stat_done"), sem("rs_step"))
        t_ready, h_hi_ready, h_lo_ready = sem("t_ready"), sem("h_hi_ready"), sem("h_lo_ready")
        silu_done, a_ready, a_hi_ready, a_lo_ready = (
            sem("silu_done"), sem("a_ready"), sem("a_hi_ready"), sem("a_lo_ready"))
        out_ready, out_stored = sem("out_ready"), sem("out_stored")

        block = ctx.enter_context(nc.Block())

        def load_slab(sp, n, slot):
            sp.wait_ge(w_lo, n - RING + 1)
            sp.dma_start(raw[:, slot, :], w_stream[n]).then_inc(raw_loaded[slot], 16)

        def prep_hi(act, b4, l, width=SLAB):
            s = l % RING
            act.wait_ge(raw_loaded[s], 16 * (b4 + l // RING) + 16)
            act.wait_ge(slab_used, 4 * b4 + l + 1)
            nc.scalar.activation(w_hi_sb[:, s, 0:width], raw[:, s, 0:width], ACT.Copy).then_inc(w_hi, 1)

        def prep_lo(dve, b4, l, width=SLAB):
            s = l % RING
            dve.wait_ge(w_hi, 4 * b4 + l + 1)
            nc.vector.tensor_tensor(w_lo_sb[:, s, 0:width], raw[:, s, 0:width], w_hi_sb[:, s, 0:width],
                                    ALU.subtract).then_inc(w_lo, 1)

        def product3(ps, s_hi, s_lo, m_hi, m_lo, start, stop):
            nc.tensor.matmul(ps, s_hi, m_hi, start=start, stop=False)
            nc.tensor.matmul(ps, s_hi, m_lo, start=False, stop=False)
            return nc.tensor.matmul(ps, s_lo, m_hi, start=False, stop=stop)

        def use_slab(pe, b4, l, ps, m_hi, m_lo, k0=0, tiles=8, ktiles=8, ready=None):
            s = l % RING
            pe.wait_ge(w_lo, 4 * b4 + l + 1)
            for k in range(tiles):
                if ready is not None:
                    ready(k0 + k)
                w = slice(k * P, (k + 1) * P)
                mm = product3(ps, w_hi_sb[:, s, w], w_lo_sb[:, s, w], m_hi[:, k0 + k, :], m_lo[:, k0 + k, :],
                              k0 + k == 0, k0 + k == ktiles - 1)
            mm.then_inc(slab_used, 1)

        def use_pair(pe, b4, l, banks, m_hi, m_lo, ready=None):
            for k in range(8):
                if ready is not None:
                    ready(k)
                w = slice(k * P, (k + 1) * P)
                for q in range(2):
                    s = (l + q) % RING
                    if k == 0:
                        pe.wait_ge(w_lo, 4 * b4 + l + q + 1)
                    mm = product3(banks[q][:, :], w_hi_sb[:, s, w], w_lo_sb[:, s, w], m_hi[:, k, :], m_lo[:, k, :],
                                  k == 0, k == 7)
                    if k == 7:
                        mm.then_inc(slab_used, 1)

        def mod_block(dve, v, k, first=False):
            if first:
                dve.wait_ge(first_loaded[8 * v + k], 16)
                w = first_mod[:, 8 * v + k, :]
            else:
                dve.wait_ge(mod_loaded[k % 2], 16 * (4 * (v - MOD_FIRST) + k // 2) + 16)
                w = mod_raw[:, k % 2, :]
            if k == 0:
                if not first or v > 0:
                    dve.wait_ge(mod_mm, v)
                nc.vector.tensor_scalar(mod_acc[:, :], w, c_act[:, 0:1], None, ALU.mult).then_inc(mod_step, 1)
            else:
                dve.wait_ge(mod_step, 8 * v + k)
                nc.vector.scalar_tensor_tensor(mod_acc[:, :], w, c_act[:, k:k + 1], mod_acc[:, :],
                                               ALU.mult, ALU.add).then_inc(mod_step, 1)

        def mod_sum(pe, v, first=False):
            pe.wait_ge(mod_step, 8 * v + 8)
            if not first:
                pe.wait_ge(mod_col, v)
            for j in range(DT):
                mm = nc.tensor.matmul(bank[7][:, j:j + 1], mod_acc[:, j * P:(j + 1) * P], ones[:, 0:1],
                                      start=True, stop=True)
            mm.then_inc(mod_mm, 1)

        def mod_collect(dve, v):
            dve.wait_ge(mod_mm, v + 1)
            b = cols[:, COLS["modb"][0]:COLS["modb"][1]].rearrange("p (v j) -> p v j", j=DT)
            nc.vector.tensor_tensor(mod[:, v, :], bank[7][:, 0:DT], b[:, v, :], ALU.add).then_inc(mod_col, 1)

        def load_mod(sp, m, slot, first=False):
            if not first:
                sp.wait_ge(mod_step, m - 1)
            sp.dma_start(mod_raw[:, slot, :], w_mod[m]).then_inc(mod_loaded[slot], 16)

        def square(act, st, j):
            nc.scalar.activation(tmp[:, 0, :], x[:, j, :], ACT.Square).then_inc(sq_ready, 1)

        def clear_sum(dve):
            nc.vector.memset(sumsq[:, :], 0.0)
            nc.vector.memset(tmp[:, 0, :], 0.0).then_inc(ss_step, 1)

        def add_square(dve, st, j):
            dve.wait_ge(sq_ready, ONE + 8 * (st - 1) + j)
            dve.wait_ge(ss_step, 9 * (st - 1) + j + 1)
            nc.vector.tensor_tensor(sumsq[:, :], sumsq[:, :], tmp[:, 0, :], ALU.add).then_inc(ss_step, 1)

        def stat_tensor(pe, st):
            pe.wait_ge(ss_step, 9 * st)
            nc.tensor.matmul(bank[6][:, :], ones[:, :], sumsq[:, :], start=True, stop=False)
            pe.wait_ge(sq_ready, ONE + 8 * st)
            nc.tensor.matmul(bank[6][:, :], ones[:, :], tmp[:, 0, :], start=False, stop=True).then_inc(stat_done, 1)

        def rstd_scalar(act, st):
            nc.scalar.activation(spare[:, 10 + st:11 + st], eps[:, 0:1], ACT.Ln)
            act.wait_ge(stat_done, st + 1)
            nc.scalar.activation(rstd[:, :], bank[6][:, :], ACT.Ln, bias=eps[:, 0:1], scale=1.0 / D).then_inc(rs_step, 1)
            act.wait_ge(rs_step, 2 * st + 1)
            nc.scalar.activation(rstd[:, :], rstd[:, :], ACT.Exp, scale=-0.5).then_inc(rs_step, 1)

        def columns_vector(dve, count, sc, w):
            nc.vector.scalar_tensor_tensor(scale_col[:, :], mod[:, sc, :], 1.0, w, ALU.add, ALU.mult).then_inc(col_step, 1)
            dve.wait_ge(col_step, count)

        def norm_vector(dve, st, hs, sh, hi, lo):
            def rest(j):
                dve.wait_ge(h_hi_ready, 8 * hs + j + 1)
                nc.vector.scalar_tensor_tensor(lo[:, j, :], tmp[:, j % 2, :], mod[:, sh, j:j + 1], hi[:, j, :],
                                               ALU.add, ALU.subtract).then_inc(h_lo_ready, 1)

            dve.wait_ge(rs_step, 2 * st + 2)
            for j in range(DT):
                if 8 * hs + j > 1:
                    dve.wait_ge(h_lo_ready, 8 * hs + j - 1)
                nc.vector.scalar_tensor_tensor(tmp[:, j % 2, :], x[:, j, :], scale_col[:, j:j + 1], rstd[:, :],
                                               ALU.mult, ALU.mult).then_inc(t_ready, 1)
                if j:
                    rest(j - 1)
            rest(DT - 1)

        def norm_scalar(act, hs, sh, hi):
            for j in range(DT):
                act.wait_ge(t_ready, 8 * hs + j + 1)
                nc.scalar.activation(hi[:, j, :], tmp[:, j % 2, :], ACT.Identity, bias=mod[:, sh, j:j + 1],
                                     ).then_inc(h_hi_ready, 1)

        def project_turns(eng, body, last, turn):
            turns = DT // body
            if not last:
                with eng.Fori(0, turns) as i:
                    turn(i, False)
            else:
                with eng.Fori(0, turns - 1) as i:
                    turn(i, False)
                turn(turns - 1, True)

        def widths(l, spj):
            return 6 * P if spj == DOWN_SPJ and l % spj == spj - 1 else SLAB

        def project_tensor(pe, n0, ktiles, spj, body, m_hi, m_lo, ready, st, last=False, mod0=None):
            def turn(i, _):
                b4 = n0 // 4 + i * (body * spj // RING)
                for jj in range(body):
                    if spj == 1:
                        pe.wait_ge(x_ready, 8 * (st - 1) + body * i + jj - 1)
                    for s in range(spj):
                        if mod0 is not None and jj % 2 == 1 and s == spj - 1:
                            mod_sum(pe, mod0 + 2 * i + jj // 2)
                        use_slab(pe, b4, jj * spj + s, bank[4 + jj % 2][:, :], m_hi, m_lo, 8 * s,
                                 min(8, ktiles - 8 * s), ktiles, ready if jj == 0 else None)
            project_turns(pe, body, last, turn)
            stat_tensor(pe, st)

        def project_scalar(act, n0, spj, body, st, last=False):
            def turn(i, end):
                b4 = n0 // 4 + i * (body * spj // RING)
                for jj in range(body):
                    for s in range(spj):
                        l = jj * spj + s + 2
                        if not end or l < body * spj:
                            prep_hi(act, b4, l, widths(l, spj))
                    j = body * i + jj
                    act.wait_ge(x_ready, 8 * (st - 1) + j + 1)
                    square(act, st, j)
            project_turns(act, body, last, turn)

        def project_vector(dve, n0, spj, body, gate, st, last=False, mod0=None):
            clear_sum(dve)

            def turn(i, end):
                b4 = n0 // 4 + i * (body * spj // RING)
                for jj in range(body):
                    v = None if mod0 is None else mod0 + 2 * i + jj // 2
                    at = 5 * (jj % 2)
                    for s in range(spj):
                        if v is not None:
                            mod_block(dve, v, at + s)
                        l = jj * spj + s + 2
                        if not end or l < body * spj:
                            prep_lo(dve, b4, l, widths(l, spj))
                    if v is not None:
                        for k in range(at + spj, 8 if jj % 2 else 5):
                            mod_block(dve, v, k)
                        if jj % 2 == 1:
                            mod_collect(dve, v)
                    j = body * i + jj
                    add_square(dve, st, j)
                    dve.wait_ge(slab_used, RING + 4 * b4 + (jj + 1) * spj)
                    nc.vector.scalar_tensor_tensor(x[:, j, :], bank[4 + jj % 2][:, :], gate(j), x[:, j, :],
                                                   ALU.mult, ALU.add).then_inc(x_ready, 1)
            project_turns(dve, body, last, turn)
            if mod0 is not None:
                dve.wait_ge(mod_col, mod0 + MOD_DOWN)

        def ffn_turns(eng, mod0, turn):
            turns = FT // 2
            if mod0 is None:
                with eng.Fori(0, turns) as i:
                    turn(i, None, 0)
            else:
                with eng.Fori(0, MOD_GU) as v:
                    for part in range(2):
                        turn(2 * v + part, mod0 + v, part)
                turn(turns - 1, None, 0)

        def down_mod(mod0):
            return None if mod0 is None else mod0 + MOD_GU

        def ffn_tensor(pe, k, n0, hs, st, mod0=None, last=False):
            def turn(i, v, part):
                b4 = n0 // 4 + i
                for u in range(2):
                    use_pair(pe, b4, 2 * u, bank[2 * u:2 * u + 2], h_hi, h_lo,
                             (lambda j: pe.wait_ge(h_lo_ready, 8 * hs + j + 1)) if u == 0 else None)
                if part == 1:
                    mod_sum(pe, v)
            ffn_turns(pe, mod0, turn)
            project_tensor(pe, n0 + GU_SLABS, FT, DOWN_SPJ, 4, a_hi, a_lo,
                           lambda f: pe.wait_ge(a_lo_ready, ONE + FT * k + f + 1), st, last, down_mod(mod0))

        def ffn_scalar(act, k, n0, st, mod0=None, last=False):
            def turn(i, v, part):
                b4 = n0 // 4 + i
                for u in range(2):
                    f = 2 * i + u
                    prep_hi(act, b4, 2 * u + 2)
                    prep_hi(act, b4, 2 * u + 3)
                    act.wait_ge(slab_used, RING + 4 * b4 + 2 * u + 1)
                    act.wait_ge(a_ready, ONE + FT * k + f)
                    nc.scalar.activation(tmp[:, 0, :], bank[2 * u][:, :], ACT.Silu).then_inc(silu_done, 1)
                    act.wait_ge(a_ready, ONE + FT * k + f + 1)
                    nc.scalar.activation(a_hi[:, f, :], tmp[:, 1, :], ACT.Copy).then_inc(a_hi_ready, 1)
            ffn_turns(act, mod0, turn)
            project_scalar(act, n0 + GU_SLABS, DOWN_SPJ, 4, st, last)

        def ffn_vector(dve, k, n0, g, st, mod0, cols_before, last=False):
            def turn(i, v, part):
                b4 = n0 // 4 + i
                for u in range(2):
                    f = 2 * i + u
                    for q in range(2):
                        if v is not None:
                            mod_block(dve, v, 4 * part + 2 * u + q)
                        prep_lo(dve, b4, 2 * u + 2 + q)
                    dve.wait_ge(silu_done, FT * k + f + 1)
                    dve.wait_ge(slab_used, RING + 4 * b4 + 2 * u + 2)
                    dve.wait_ge(a_lo_ready, ONE + FT * k + f)
                    nc.vector.tensor_tensor(tmp[:, 1, :], tmp[:, 0, :], bank[2 * u + 1][:, :],
                                            ALU.mult).then_inc(a_ready, 1)
                    dve.wait_ge(a_hi_ready, FT * k + f + 1)
                    nc.vector.tensor_tensor(a_lo[:, f, :], tmp[:, 1, :], a_hi[:, f, :],
                                            ALU.subtract).then_inc(a_lo_ready, 1)
                if part == 1:
                    mod_collect(dve, v)
            ffn_turns(dve, mod0, turn)
            dve.wait_ge(mod_col, g + 1)
            nc.vector.tensor_scalar(gate_col[:, :], mod[:, g, :], 0.5, None, ALU.mult).then_inc(col_step, 1)
            dve.wait_ge(col_step, cols_before + 1)
            project_vector(dve, n0 + GU_SLABS, DOWN_SPJ, 4, lambda j: gate_col[:, bass.ds(j, 1)], st, last,
                           down_mod(mod0))

        wdt_split, dtp_done, soft_act, soft_dve, dec_done = (
            sem("wdt_split"), sem("dtp_done"), sem("soft_act"), sem("soft_dve"), sem("dec_done"))
        ssm_consts = sem("ssm_consts")
        z_read, conv_init, conv_step = sem("z_read"), sem("conv_init"), sem("conv_step")
        silu_x, silu_z = sem("silu_x"), sem("silu_z")
        ta_ready, turned, seg_ready, sum_ready = sem("ta_ready"), sem("turned"), sem("seg_ready"), sem("sum_ready")
        el_ready, ee_ready = sem("el_ready"), sem("ee_ready")
        cd_ready = sem("cd_ready")
        g_ready, mixed, y_done, st_done, state_ready = (
            sem("g_ready"), sem("mixed"), sem("y_done"), sem("st_done"), sem("state_ready"))
        gate_step, gsq_ready, gstat_done, grs_step = (
            sem("gate_step"), sem("gsq_ready"), sem("gstat_done"), sem("grs_step"))
        yn_ready, y_hi_ready, y_lo_ready = sem("yn_ready"), sem("y_hi_ready"), sem("y_lo_ready")

        cb = bank[4][:, 3 * P:4 * P]
        chunk = [slice(c * P, (c + 1) * P) for c in range(NCH)]

        def scan_a_tensor(pe, g, pp, c):
            if c == 0:
                pe.wait_ge(silu_x, 4 * g + 4)
            for i in range(2):
                nc.tensor.transpose(bank[4][:, i * P:(i + 1) * P], xs[:, pp, i, chunk[c]], ident[:, :])
            nc.tensor.transpose(bank[4][:, 2 * P:3 * P], bc[:, pp, 0, chunk[c]], ident[:, :])
            nc.tensor.matmul(cb, bc[:, pp, 0, chunk[c]], bc[:, pp, 1, chunk[c]], start=True, stop=True).then_inc(turned, 1)
            pe.wait_ge(ta_ready, 4 * g + c + 1)
            for n, (tri, ready) in enumerate(((after_r, seg_ready), (ones_r, sum_ready))):
                for part in (ta_hi, ta_lo):
                    mm = nc.tensor.matmul(bank[5 + n][:, :], tri[:, :], part[:, :, :].rearrange("p h l -> p (h l)"),
                                          start=(part is ta_hi), stop=(part is ta_lo))
                mm.then_inc(ready, 1)

        def scan_b_tensor(pe, g, c):
            pe.wait_ge(mixed, 4 * g + c + 1)
            if c:
                pe.wait_ge(state_ready, 3 * g + c)
            for pair in range(2):
                ps = bank[2 + pair][:, chunk[c]]
                for r in range(2):
                    mm = nc.tensor.matmul(ps, x_pad[:, r, pair, :], el[:, 2 * pair + r, :],
                                          start=(r == 0), stop=(c == 0 and r == 1))
                if c:
                    for r in range(2):
                        mm = nc.tensor.matmul(ps, state[:, r, pair, :], ee[:, 2 * pair + r, :],
                                              start=False, stop=(r == 1))
            mm.then_inc(y_done, 1)
            if c < NCH - 1:
                nc.tensor.matmul(bank[7][:, 0:HPG * HDIM], b_tok[:, :], x_dec[:, :, :].rearrange("p h d -> p (h d)"),
                                 start=True, stop=True).then_inc(st_done, 1)

        def ssm_tensor(pe):
            n4 = S_IN // 4
            ready = lambda j: pe.wait_ge(h_lo_ready, 8 * 1 + j + 1)
            use_pair(pe, n4, 0, bank[0:2], h_hi, h_lo, ready)
            pe.wait_ge(wdt_split, 2)
            for k in range(DT):
                mm = product3(bank[4][0:HEADS, :], wdt_hi[:, k, :], wdt_lo[:, k, :], h_hi[:, k, :], h_lo[:, k, :],
                              k == 0, k == DT - 1)
            mm.then_inc(dtp_done, 1)
            use_slab(pe, n4, 2, bank[2][:, :], h_hi, h_lo)
            pe.wait_ge(soft_act, 1)
            pe.wait_ge(ssm_consts, 6)
            for c in range(NCH):
                mm = nc.tensor.transpose(bank[5][:, c * HEADS:(c + 1) * HEADS], rstd[0:HEADS, chunk[c]],
                                         ident[0:HEADS, 0:HEADS])
            mm.then_inc(dtp_done, 1)
            use_slab(pe, n4, 3, bank[3][:, :], h_hi, h_lo)
            pe.wait_ge(soft_dve, SOFT_A + 1)
            nc.tensor.matmul(bank[5][:, 0:NCH * HEADS], after[:, :], a_tok[:, :, :].rearrange("p c h -> p (c h)"),
                             start=True, stop=True).then_inc(dec_done, 1)

            def group(i, pp, last=False):
                g = 2 * i + pp
                b4 = n4 + 1 + 3 * i

                def slab(s):
                    if s < 2:
                        pe.wait_ge(conv_step, 3 * (4 * g + 3 + s))
                    elif s < 4:
                        pe.wait_ge(z_read, 2 * g + s - 1)
                    else:
                        pe.wait_ge(conv_step, 3 * (4 * g + 1 + s))
                    use_slab(pe, b4, 6 * pp + s, bank[s % 2][:, :], h_hi, h_lo)

                slab(0)
                scan_a_tensor(pe, g, pp, 0)
                slab(1)
                for c in range(NCH):
                    if c and not last:
                        slab(c + 1)
                    if c in (1, 2) and last:
                        pe.wait_ge(z_read, 2 * g + c)
                        pe.wait_ge(y_lo_ready, ONE + 8)
                        use_slab(pe, b4, 6 * pp + c + 1, bank[c - 1][:, :], y_hi, y_lo, 0, 8, 16)
                    scan_b_tensor(pe, g, c)
                    if c < NCH - 1:
                        scan_a_tensor(pe, g, pp, c + 1)
                if not last:
                    slab(5)
                for t in range(2):
                    pe.wait_ge(gsq_ready, 2 * g + t + 1)
                    mm = nc.tensor.matmul(bank[7][:, :], ones[:, :], zs[:, t, :], start=(t == 0), stop=(t == 1))
                mm.then_inc(gstat_done, 1)

            with pe.Fori(0, GROUPS // 2 - 1) as i:
                group(i, 0)
                group(i, 1)
            group(GROUPS // 2 - 1, 0)
            group(GROUPS // 2 - 1, 1, last=True)
            def turn(i, first):
                for part in range(1 if first else 0, 2):
                    for jj in range(2):
                        if part == 0:
                            pe.wait_ge(x_ready, 8 + 2 * i - 1 + jj)
                        use_slab(pe, S_OUT // 4 + i, 2 * part + jj, bank[jj][:, :], y_hi, y_lo, 8 * part, 8, 16,
                                 (lambda f: pe.wait_ge(y_lo_ready, ONE + f + 1)) if first else None)
            turn(0, True)
            with pe.Fori(1, DT // 2) as i:
                turn(i, False)
            stat_tensor(pe, 2)

        SOFT_A = 17

        def conv_cols(g, t, tap):
            v = ssm_cols[:, 0:SSM_CONV].rearrange("p (g t k) -> p g t k", g=GROUPS, t=4)
            return v[:, g, t, tap:tap + 1]

        def conv_tile(pp, t):
            return xs[:, pp, t, :] if t < 2 else bc[:, pp, t - 2, :]

        def conv_scalar(act, g, pp, t, used, ps):
            act.wait_ge(slab_used, used)
            nc.scalar.activation(conv_tile(pp, t), ps, ACT.Identity, bias=conv_cols(g, t, 4),
                                 scale=conv_cols(g, t, 3)).then_inc(conv_init, 1)

        def conv_vector(dve, g, pp, t, ps):
            y = conv_tile(pp, t)
            dve.wait_ge(conv_init, 4 * g + t + 1)
            for back in range(1, 4):
                if back > 1:
                    dve.wait_ge(conv_step, 3 * (4 * g + t) + back - 1)
                nc.vector.scalar_tensor_tensor(y[:, back:], ps[:, 0:T - back], conv_cols(g, t, 3 - back),
                                               y[:, back:], ALU.mult, ALU.add).then_inc(conv_step, 1)

        def silu_tiles(act, g, pp, tiles):
            for t in tiles:
                act.wait_ge(conv_step, 3 * (4 * g + t + 1))
                nc.scalar.activation(conv_tile(pp, t), conv_tile(pp, t), ACT.Silu).then_inc(silu_x, 1)

        def ssm_scalar(act):
            n4 = S_IN // 4
            act.wait_ge(ssm_loaded, 48)
            nc.scalar.activation(wdt_hi[:, :, :], wdt[:, :, :], ACT.Copy).then_inc(wdt_split, 1)
            prep_hi(act, n4, 2)
            prep_hi(act, n4, 3)
            conv_scalar(act, 0, 0, 0, RING + S_IN + 1, bank[0][:, :])
            conv_scalar(act, 0, 0, 1, RING + S_IN + 2, bank[1][:, :])
            prep_hi(act, n4, 4)
            prep_hi(act, n4, 5)
            act.wait_ge(dtp_done, 1)
            nc.scalar.activation(rstd[0:HEADS, :], bank[4][0:HEADS, :], ACT.Copy).then_inc(soft_act, 1)
            act.wait_ge(soft_dve, 2)
            nc.scalar.activation(soft[:, 2, :], soft[:, 1, :], ACT.Exp).then_inc(soft_act, 1)
            nc.scalar.activation(ssm_rows[:, HEADS:2 * HEADS], ssm_rows[:, HEADS:2 * HEADS], ACT.Exp).then_inc(soft_act, 1)
            conv_scalar(act, 0, 0, 2, RING + S_IN + 3, bank[2][:, :])
            conv_scalar(act, 0, 0, 3, RING + S_IN + 4, bank[3][:, :])
            silu_tiles(act, 0, 0, range(4))
            act.wait_ge(dec_done, 1)
            nc.scalar.activation(a_hi_tok[:, :, :], a_tok[:, :, :], ACT.Copy)
            nc.scalar.activation(after_r[:, :], after[:, :], ACT.Copy)
            nc.scalar.activation(ones_r[:, :], ones[:, :], ACT.Copy)
            nc.scalar.activation(dd_tok[:, :, :].rearrange("p c h -> p (c h)"), bank[5][:, 0:NCH * HEADS],
                                 ACT.Exp).then_inc(soft_act, 1)

            def group(i, pp, last=False):
                g = 2 * i + pp
                b4 = n4 + 1 + 3 * i
                used = RING + 4 * b4 + 6 * pp

                def z_copy(t):
                    act.wait_ge(slab_used, used + t + 1)
                    if t == 0:
                        act.wait_ge(gstat_done, ONE + g)
                    nc.scalar.activation(zs[:, t, :], bank[t][:, :], ACT.Copy).then_inc(z_read, 1)

                def scan(c):
                    act.wait_ge(seg_ready, 4 * g + c + 1)
                    nc.scalar.activation(el[:, :, :].rearrange("p h l -> p (h l)"), bank[5][:, :],
                                         ACT.Exp).then_inc(el_ready, 1)
                    act.wait_ge(sum_ready, 4 * g + c + 1)
                    nc.scalar.activation(sumsq[:, :], bank[6][:, :],
                                         ACT.Exp).then_inc(ee_ready, 1)

                for s in range(6):
                    if 1 < s < (4 if last else 6):
                        prep_hi(act, b4, 6 * pp + s + 2)
                    if not last and s >= 3:
                        conv_scalar(act, g + 1, 1 - pp, s - 3, used + s, bank[(s - 3) % 2][:, :])
                    if 1 <= s <= 2:
                        z_copy(s - 1)
                    if 1 <= s <= 4:
                        scan(s - 1)
                    if s == 1:
                        prep_hi(act, b4, 6 * pp + 2)
                        prep_hi(act, b4, 6 * pp + 3)
                for t in range(2):
                    act.wait_ge(z_read, 2 * g + t + 1)
                    nc.scalar.activation(zs[:, t, :], zs[:, t, :], ACT.Silu).then_inc(silu_z, 1)
                if not last:
                    silu_tiles(act, g + 1, 1 - pp, range(2))
                for t in range(2):
                    act.wait_ge(gate_step, 4 * g + 2 * t + 2)
                    nc.scalar.activation(zs[:, t, :], tmp[:, t, :], ACT.Square).then_inc(gsq_ready, 1)
                if not last:
                    conv_scalar(act, g + 1, 1 - pp, 3, used + 6, bank[1][:, :])
                    silu_tiles(act, g + 1, 1 - pp, range(2, 4))
                act.wait_ge(gstat_done, ONE + g + 1)
                nc.scalar.activation(rstd[:, :], bank[7][:, :], ACT.Ln, bias=eps[:, 0:1],
                                     scale=1.0 / (2 * P)).then_inc(grs_step, 1)
                act.wait_ge(grs_step, 2 * g + 1)
                nc.scalar.activation(rstd[:, :], rstd[:, :], ACT.Exp, scale=-0.5).then_inc(grs_step, 1)
                for t in range(2):
                    act.wait_ge(yn_ready, 2 * g + t + 1)
                    nc.scalar.activation(y_hi[:, 2 * g + t, :], tmp[:, t, :], ACT.Copy).then_inc(y_hi_ready, 1)

            with act.Fori(0, GROUPS // 2 - 1) as i:
                group(i, 0)
                group(i, 1)
            group(GROUPS // 2 - 1, 0)
            group(GROUPS // 2 - 1, 1, last=True)

            def turn(i, first):
                b4 = S_OUT // 4 + i
                if not first:
                    prep_hi(act, b4, 2)
                    prep_hi(act, b4, 3)
                for jj in range(2):
                    prep_hi(act, b4, 4 + jj)
                    act.wait_ge(x_ready, 8 + 2 * i + jj + 1)
                    square(act, 2, 2 * i + jj)
            turn(0, True)
            with act.Fori(1, DT // 2) as i:
                turn(i, False)

        def ssm_vector(dve):
            n4 = S_IN // 4
            dve.wait_ge(ssm_loaded, 48)
            step = [0]

            def link(ins):
                step[0] += 1
                ins.then_inc(soft_dve, 1)
                dve.wait_ge(soft_dve, step[0])

            dve.wait_ge(wdt_split, 1)
            nc.vector.tensor_tensor(wdt_lo[:, :, :], wdt[:, :, :], wdt_hi[:, :, :], ALU.subtract).then_inc(wdt_split, 1)
            prep_lo(dve, n4, 2)
            prep_lo(dve, n4, 3)
            conv_vector(dve, 0, 0, 0, bank[0])
            conv_vector(dve, 0, 0, 1, bank[1])
            prep_lo(dve, n4, 4)
            prep_lo(dve, n4, 5)
            v, na, e, sv, s2 = (soft[:, q, :] for q in range(5))
            dtv = dt_tok[:, :, :].rearrange("p c h -> p (c h)")
            bias = ssm_rows[:, 0:HEADS].unsqueeze(1).broadcast_to([P, NCH, HEADS])
            dve.wait_ge(dtp_done, 2)
            link(nc.vector.tensor_tensor(v.rearrange("p (c h) -> p c h", c=NCH),
                                         bank[5][:, 0:NCH * HEADS].rearrange("p (c h) -> p c h", c=NCH), bias, ALU.add))
            link(nc.vector.scalar_tensor_tensor(na, v, -1.0, v, ALU.mult, ALU.min))
            dve.wait_ge(soft_act, 2)
            link(nc.vector.tensor_scalar(sv, e, 2.0, None, ALU.add))
            link(nc.vector.reciprocal(na, sv))
            link(nc.vector.tensor_tensor(sv, e, na, ALU.mult))
            link(nc.vector.tensor_tensor(s2, sv, sv, ALU.mult))
            link(nc.vector.tensor_scalar(na, s2, 1.0 / 17, None, ALU.mult))
            for odd in (15, 13, 11, 9, 7, 5, 3):
                link(nc.vector.scalar_tensor_tensor(na, na, 1.0 / odd, s2, ALU.add, ALU.mult))
            link(nc.vector.scalar_tensor_tensor(na, na, 1.0, sv, ALU.add, ALU.mult))
            link(nc.vector.tensor_scalar(v, v, 0.0, None, ALU.max))
            link(nc.vector.scalar_tensor_tensor(dtv, na, 2.0, v, ALU.mult, ALU.add))
            dve.wait_ge(soft_act, 3)
            ea = ssm_rows[:, HEADS:2 * HEADS].unsqueeze(1).broadcast_to([P, NCH, HEADS])
            nc.vector.scalar_tensor_tensor(a_tok[:, :, :], dt_tok[:, :, :], -1.0, ea, ALU.mult, ALU.mult).then_inc(soft_dve, 1)
            dve.wait_ge(soft_dve, SOFT_A + 1)
            conv_vector(dve, 0, 0, 2, bank[2])
            conv_vector(dve, 0, 0, 3, bank[3])
            dve.wait_ge(soft_act, 4)
            nc.vector.tensor_tensor(a_lo_tok[:, :, :], a_tok[:, :, :], a_hi_tok[:, :, :], ALU.subtract).then_inc(soft_dve, 1)
            nc.vector.tensor_tensor(dd_tok[:, :, :], dd_tok[:, :, :], dt_tok[:, :, :], ALU.mult).then_inc(soft_dve, 1)
            nc.vector.memset(x_pad[:, :, :, :], 0.0).then_inc(soft_dve, 1)
            nc.vector.memset(state[:, :, :, :], 0.0).then_inc(soft_dve, 1)
            dve.wait_ge(soft_dve, SOFT_A + 5)
            dve.wait_ge(ssm_consts, 6)

            def by_head(tok, c, g):
                return tok[:, c, :].rearrange("p (g h) -> p g h", h=HPG)[:, g, :]

            def decays(g, c):
                u = upto[:, :].unsqueeze(1).broadcast_to([P, HPG, P])
                for ta, tok in ((ta_hi, a_hi_tok), (ta_lo, a_lo_tok)):
                    a = by_head(tok, c, g).unsqueeze(2).broadcast_to([P, HPG, P])
                    op = nc.vector.tensor_tensor(ta[:, :, :], u, a, ALU.mult)
                op.then_inc(ta_ready, 1)

            def group(i, pp, last=False):
                g = 2 * i + pp
                b4 = n4 + 1 + 3 * i

                def mix(c):
                    dve.wait_ge(turned, 4 * g + c + 1)
                    xt = bank[4][:, 0:2 * P].rearrange("p (q r d) -> p q r d", q=2, r=2)
                    dt = by_head(dt_tok, c, g).rearrange("p (q r) -> p q r", q=2)
                    for r in range(2):
                        nc.vector.tensor_tensor(x_pad[:, r, :, r * HDIM:(r + 1) * HDIM], xt[:, :, r, :],
                                                dt[:, :, r].unsqueeze(2).broadcast_to([P, 2, HDIM]), ALU.mult)
                    dd = by_head(dd_tok, c, g).unsqueeze(2).broadcast_to([P, HPG, HDIM])
                    nc.vector.tensor_tensor(x_dec[:, :, :], bank[4][:, 0:2 * P].rearrange("p (h d) -> p h d", h=HPG), dd,
                                            ALU.mult)
                    nc.vector.tensor_copy(b_tok[:, :], bank[4][:, 2 * P:3 * P])
                    nc.vector.tensor_tensor(gm_t[:, :], cb, upto[:, :], ALU.mult).then_inc(g_ready, 1)
                    dve.wait_ge(g_ready, 4 * g + c + 1)
                    dve.wait_ge(el_ready, 4 * g + c + 1)
                    nc.vector.tensor_tensor(el[:, :, :], el[:, :, :], gm_t[:, :].unsqueeze(1).broadcast_to([P, HPG, P]),
                                            ALU.mult)
                    dve.wait_ge(ee_ready, 4 * g + c + 1)
                    nc.vector.tensor_copy(chunk_dec[:, :], ee[:, :, P - 1]).then_inc(cd_ready, 1)
                    dve.wait_ge(cd_ready, 4 * g + c + 1)
                    nc.vector.tensor_tensor(ee[:, :, :], ee[:, :, :],
                                            bc[:, pp, 1, chunk[c]].unsqueeze(1).broadcast_to([P, HPG, P]),
                                            ALU.mult).then_inc(mixed, 1)

                def carry(c):
                    dve.wait_ge(st_done, 3 * g + c + 1)
                    dve.wait_ge(mixed, 4 * g + c + 1)
                    for h in range(HPG):
                        r = h % 2
                        cur = state[:, r, h // 2, r * HDIM:(r + 1) * HDIM]
                        new = bank[7][:, h * HDIM:(h + 1) * HDIM]
                        if c == 0:
                            last_op = nc.vector.tensor_copy(cur, new)
                        else:
                            last_op = nc.vector.scalar_tensor_tensor(cur, cur, chunk_dec[:, h:h + 1], new,
                                                                     ALU.mult, ALU.add)
                    last_op.then_inc(state_ready, 1)
                    dve.wait_ge(state_ready, 3 * g + c + 1)

                for s in range(6):
                    if 1 < s < (4 if last else 6):
                        prep_lo(dve, b4, 6 * pp + s + 2)
                    if not last and s >= 3:
                        conv_vector(dve, g + 1, 1 - pp, s - 3, bank[(s - 3) % 2])
                    if 2 <= s <= 4:
                        carry(s - 2)
                    if 1 <= s <= 4:
                        mix(s - 1)
                    if 1 <= s <= 3:
                        decays(g, s)
                    if s == 1:
                        prep_lo(dve, b4, 6 * pp + 2)
                        prep_lo(dve, b4, 6 * pp + 3)
                dve.wait_ge(y_done, 4 * g + NCH)
                dve.wait_ge(silu_z, 2 * g + 2)
                dve.wait_ge(y_lo_ready, ONE + 2 * g)
                for t in range(2):
                    nc.vector.scalar_tensor_tensor(tmp[:, t, :], xs[:, pp, t, :],
                                                   ssm_cols[:, bass.ds(2 * g + (SSM_CONV + t), 1)],
                                                   bank[2 + t][:, :], ALU.mult, ALU.add).then_inc(gate_step, 1)
                    dve.wait_ge(gate_step, 4 * g + 2 * t + 1)
                    nc.vector.tensor_tensor(tmp[:, t, :], tmp[:, t, :], zs[:, t, :], ALU.mult).then_inc(gate_step, 1)
                if not last:
                    conv_vector(dve, g + 1, 1 - pp, 3, bank[1])
                    decays(g + 1, 0)
                dve.wait_ge(grs_step, 2 * g + 2)
                for t in range(2):
                    dve.wait_ge(gate_step, 4 * g + 2 * t + 2)
                    nc.vector.scalar_tensor_tensor(tmp[:, t, :], tmp[:, t, :],
                                                   ssm_cols[:, bass.ds(2 * g + (SSM_CONV + 16 + t), 1)],
                                                   rstd[:, :], ALU.mult, ALU.mult).then_inc(yn_ready, 1)
                for t in range(2):
                    dve.wait_ge(y_hi_ready, 2 * g + t + 1)
                    nc.vector.tensor_tensor(y_lo[:, 2 * g + t, :], tmp[:, t, :], y_hi[:, 2 * g + t, :],
                                            ALU.subtract).then_inc(y_lo_ready, 1)

            decays(0, 0)
            with dve.Fori(0, GROUPS // 2 - 1) as i:
                group(i, 0)
                group(i, 1)
            group(GROUPS // 2 - 1, 0)
            group(GROUPS // 2 - 1, 1, last=True)
            dve.wait_ge(y_lo_ready, ONE + 16)
            clear_sum(dve)

            def turn(i, first):
                b4 = S_OUT // 4 + i
                if not first:
                    prep_lo(dve, b4, 2)
                    prep_lo(dve, b4, 3)
                for jj in range(2):
                    j = 2 * i + jj
                    prep_lo(dve, b4, 4 + jj)
                    add_square(dve, 2, j)
                    dve.wait_ge(slab_used, RING + 4 * b4 + 3 + jj)
                    nc.vector.scalar_tensor_tensor(x[:, j, :], bank[jj][:, :], mod[:, M_GMA, bass.ds(j, 1)], x[:, j, :],
                                                   ALU.mult, ALU.add).then_inc(x_ready, 1)
            turn(0, True)
            with dve.Fori(1, DT // 2) as i:
                turn(i, False)

        k_ready, v_ready = sem("k_ready"), sem("v_ready")

        def kv_tensor(pe):
            n4 = S_KV // 4
            ready = lambda j: pe.wait_ge(h_lo_ready, 8 * 3 + j + 1)
            use_pair(pe, n4, 0, bank[0:2], hkv_hi, hkv_lo, ready)
            for l in range(2, 4):
                pe.wait_ge(w_lo, 4 * n4 + l + 1)
                for c in range(NCH):
                    for k in range(DT):
                        w = slice(k * P, (k + 1) * P)
                        mm = product3(bank[l][:, chunk[c]], hkv_hi[:, k, chunk[c]], hkv_lo[:, k, chunk[c]],
                                      w_hi_sb[:, l, w], w_lo_sb[:, l, w], k == 0, k == DT - 1)
                mm.then_inc(slab_used, 1)

        def kv_scalar(act):
            n4 = S_KV // 4
            prep_hi(act, n4, 2)
            prep_hi(act, n4, 3)
            norm_scalar(act, 4, M_SH1B, h_hi)
            for l in range(2):
                act.wait_ge(slab_used, RING + S_KV + l + 1)
                b = COLS["b_k"][0] + l
                nc.scalar.activation(k_all[:, l, :], bank[l][:, :], ACT.Identity, bias=cols[:, b:b + 1]).then_inc(k_ready, 1)
            prep_hi(act, n4, 4)
            prep_hi(act, n4, 5)

        def kv_vector(dve):
            n4 = S_KV // 4
            prep_lo(dve, n4, 2)
            prep_lo(dve, n4, 3)
            columns_vector(dve, 7, M_SC1B, col("nw_ffn2"))
            norm_vector(dve, 3, 4, M_SH1B, h_hi, h_lo)
            dve.wait_ge(att_loaded, 16)
            for l in range(2, 4):
                prep_lo(dve, n4, l + 2)
            for l in range(2, 4):
                dve.wait_ge(slab_used, RING + S_KV + l + 1)
                o = slice((l - 2) * P, (l - 1) * P)
                nc.vector.tensor_tensor(v_all[:, :, o], bank[l][:, :].rearrange("p (c d) -> p c d", c=NCH),
                                        att_rows[:, o].unsqueeze(1).broadcast_to([P, NCH, P]), ALU.add).then_inc(v_ready, 1)

        att_consts, bq_ready, q_ready, gb_step = sem("att_consts"), sem("bq_ready"), sem("q_ready"), sem("gb_step")
        pad_ready, q_cur_ready, scored = sem("pad_ready"), sem("q_cur_ready"), sem("scored")
        masked, max_step, exp_ready, sink_exp = sem("masked"), sem("max_step"), sem("exp_ready"), sem("sink_exp")
        den_step, normed, probs_turned = sem("den_step"), sem("normed"), sem("probs_turned")
        pt_ready, o_done, o_hi_ready, o_lo_ready = (
            sem("pt_ready"), sem("o_done"), sem("o_hi_ready"), sem("o_lo_ready"))

        def att_tensor(pe):
            ready = lambda j: pe.wait_ge(h_lo_ready, 8 * 5 + j + 1)
            with pe.Fori(0, 2) as i:
                pe.wait_ge(q_ready, ONE + 4 * i)
                use_pair(pe, S_Q // 4 + i, 0, bank[0:2], h_hi, h_lo, ready)
                use_pair(pe, S_Q // 4 + i, 2, bank[2:4], h_hi, h_lo)
            pe.wait_ge(att_consts, 6)

            def scores(kt, n):
                tt, half = n // 2, n % 2
                u = 8 * kt + n
                if n == 0:
                    pe.wait_ge(pad_ready, 3 * kt + 2)
                if half == 0:
                    pe.wait_ge(q_cur_ready, 4 * kt + tt + 1)
                pe.wait_ge(masked, ONE + 2 * (u - 1 if n > 1 else 8 * kt))
                for ab in range(2):
                    for b in range(2):
                        q0 = (2 * half + b) * P
                        mm = nc.tensor.matmul(bank[2 * half + ab][:, b * 2 * P:(b + 1) * 2 * P],
                                              q_cur[:, tt % 2, q0:q0 + P], k_pad[:, ab, q0:q0 + 2 * P],
                                              start=True, stop=True)
                    mm.then_inc(scored, 1)

            def turn(kt, n):
                half = n % 2
                pe.wait_ge(normed, 8 * kt + n + 1)
                for ab in range(2):
                    for b in range(2):
                        for part in range(2):
                            if half == 0 and b == 0 and part == 0:
                                continue
                            mm = nc.tensor.transpose(bank[4 + ab][:, (2 * b + part) * P:(2 * b + part + 1) * P],
                                                     probs[:, n % 3, 2 * ab + b, part * P:(part + 1) * P], ident_a[:, :])
                    mm.then_inc(probs_turned, 1)

            def values(kt, n):
                tt, half = n // 2, n % 2
                u = 8 * kt + n
                pe.wait_ge(pt_ready, 2 * u + 2)
                if n == 0:
                    pe.wait_ge(pad_ready, 3 * kt + 3)
                if half == 0:
                    pe.wait_ge(o_lo_ready, ONE + 4 * kt + max(tt - 1, 0))
                for b in range(2):
                    blk = 2 * half + b
                    parts = [(ab, part) for part in range(2) for ab in range(2) if blk + part > 0]
                    for m, (ab, part) in enumerate(parts):
                        mm = nc.tensor.matmul(bank[6 + tt % 2][:, blk * P:(blk + 1) * P], v_pad[:, blk - 1 + part, ab, :],
                                              probs_t[:, ab, 2 * b + part, :], start=(m == 0), stop=(m == len(parts) - 1))
                mm.then_inc(o_done, 1)

            with pe.Fori(0, 2) as kt:
                for n in range(3):
                    scores(kt, n)
                for n in range(8):
                    turn(kt, n)
                    if n + 3 < 8:
                        scores(kt, n + 3)
                    values(kt, n)
            project_tensor(pe, S_O, 8, 1, 4, o_hi, o_lo, lambda f: pe.wait_ge(o_lo_ready, ONE + f + 1), 5)

        def att_scalar(act):
            act.wait_ge(bq_ready, 1)
            with act.Fori(0, 2) as i:
                for u in range(2):
                    prep_hi(act, S_Q // 4 + i, 2 * u + 2)
                    prep_hi(act, S_Q // 4 + i, 2 * u + 3)
                    for t in range(2 * u, 2 * u + 2):
                        act.wait_ge(slab_used, RING + S_Q + 4 * i + t + 1)
                        nc.scalar.activation(q_all[:, 4 * i + t, :], bank[t][:, :], ACT.Identity,
                                             bias=bq8[:, bass.ds(4 * i + t, 1)], scale=HDIM ** -0.5).then_inc(q_ready, 1)
            act.wait_ge(q_ready, ONE + 8)

            def copy_q(kt, tt):
                if tt >= 2:
                    act.wait_ge(scored, ONE + 2 * (8 * kt + 2 * tt - 2))
                else:
                    act.wait_ge(scored, ONE + 16 * kt)
                nc.scalar.activation(q_cur[:, tt % 2, :], q_all[:, 4 * kt + tt, :], ACT.Copy).then_inc(q_cur_ready, 1)

            def exponentials(kt, n):
                u = 8 * kt + n
                st = stat4[:, n % 3, :, :]
                act.wait_ge(max_step, 4 * u + 4)
                for m in range(4):
                    nc.scalar.activation(probs[:, n % 3, m, :], probs[:, n % 3, m, :], ACT.Exp, bias=st[:, 1, m:m + 1],
                                         accum_out=st[:, 3, m:m + 1]).then_inc(exp_ready, 1)
                nc.scalar.activation(st[:, 2, :], st[:, 2, :], ACT.Exp).then_inc(sink_exp, 1)

            def turned(kt, n):
                lo = P if n % 2 == 0 else 0
                for ab in range(2):
                    act.wait_ge(probs_turned, 2 * (8 * kt + n) + ab + 1)
                    nc.scalar.activation(probs_t[:, ab, :, :].rearrange("p n q -> p (n q)")[:, lo:],
                                         bank[4 + ab][:, lo:], ACT.Copy).then_inc(pt_ready, 1)

            def output_hi(kt, tt):
                act.wait_ge(o_done, ONE + 8 * kt + 2 * tt + 2)
                nc.scalar.activation(o_hi[:, 4 * kt + tt, :], bank[6 + tt % 2][:, :], ACT.Copy).then_inc(o_hi_ready, 1)

            with act.Fori(0, 2) as kt:
                copy_q(kt, 0)
                copy_q(kt, 1)
                exponentials(kt, 0)
                exponentials(kt, 1)
                for n in range(8):
                    if n in (0, 1):
                        copy_q(kt, n + 2)
                    if n > 0 and n % 2 == 0:
                        output_hi(kt, n // 2 - 1)
                    turned(kt, n)
                    if n + 2 < 8:
                        exponentials(kt, n + 2)
                output_hi(kt, 3)
            project_scalar(act, S_O, 1, 4, 5)

        def att_vector(dve):
            b = COLS["b_q"][0]
            nc.vector.tensor_scalar(bq8[:, :], cols[:, b:b + DT], HDIM ** -0.5, None, ALU.mult).then_inc(bq_ready, 1)
            nc.vector.tensor_tensor(gb_o[:, :], mod[:, M_GMB, :], col("b_o"), ALU.mult).then_inc(gb_step, 1)
            dve.wait_ge(gb_step, 1)
            with dve.Fori(0, 2) as i:
                for t in range(4):
                    prep_lo(dve, S_Q // 4 + i, t + 2)
                    j = 4 * i + t
                    nc.vector.tensor_scalar(x[:, j, :], x[:, j, :], gb_o[:, bass.ds(j, 1)], None,
                                            ALU.add).then_inc(gb_step, 1)
            dve.wait_ge(att_consts, 8)
            dve.wait_ge(k_ready, 2)
            dve.wait_ge(v_ready, 2)

            def pads(kt):
                for ab in range(2):
                    half = slice(ab * HDIM, (ab + 1) * HDIM)
                    nc.vector.tensor_copy(k_pad[half, ab, P:], k_all[half, kt, :]).then_inc(pad_ready, 1)
                dve.wait_ge(o_done, ONE + 8 * kt)
                v = v_all[:, :, :].rearrange("p c (k d) -> p c k d", k=2)
                for ab in range(2):
                    half = slice(ab * HDIM, (ab + 1) * HDIM)
                    op = nc.vector.tensor_copy(v_pad[:, :, ab, half], v[:, :, kt, half])
                op.then_inc(pad_ready, 1)

            def mask_and_max(kt, n):
                tt, half = n // 2, n % 2
                u = 8 * kt + n
                st = stat4[:, n % 3, :, :]
                if n >= 3:
                    dve.wait_ge(probs_turned, 2 * (u - 2))
                for ab in range(2):
                    dve.wait_ge(scored, ONE + 2 * u + ab + 1)
                    nc.vector.tensor_tensor(probs[:, n % 3, 2 * ab:2 * ab + 2, :],
                                            bank[2 * half + ab][:, :].rearrange("p (b k) -> p b k", b=2),
                                            mask[:, half, :, :], ALU.add).then_inc(masked, 1)
                dve.wait_ge(masked, ONE + 2 * u + 2)
                nc.vector.tensor_reduce(st[:, 0, :], probs[:, n % 3, :, :], AX.X, ALU.max).then_inc(max_step, 1)
                dve.wait_ge(max_step, 4 * u + 1)
                sink = att_rows[:, KV * HDIM:].rearrange("p (t a) -> p t a", a=2)[:, 4 * kt + tt, :]
                sink = sink.unsqueeze(2).broadcast_to([P, 2, 2])
                four = lambda r: st[:, r, :].rearrange("p (a b) -> p a b", a=2)
                nc.vector.tensor_tensor(four(0), four(0), sink, ALU.max).then_inc(max_step, 1)
                dve.wait_ge(max_step, 4 * u + 2)
                nc.vector.tensor_scalar(st[:, 1, :], st[:, 0, :], -1.0, None, ALU.mult).then_inc(max_step, 1)
                nc.vector.tensor_tensor(four(2), sink, four(0), ALU.subtract).then_inc(max_step, 1)

            def normalise(kt, n):
                u = 8 * kt + n
                st = stat4[:, n % 3, :, :]
                dve.wait_ge(exp_ready, 4 * u + 4)
                dve.wait_ge(sink_exp, u + 1)
                nc.vector.tensor_tensor(st[:, 4, :], st[:, 3, :], st[:, 2, :], ALU.add).then_inc(den_step, 1)
                dve.wait_ge(den_step, 2 * u + 1)
                nc.vector.reciprocal(st[:, 5, :], st[:, 4, :]).then_inc(den_step, 1)
                dve.wait_ge(den_step, 2 * u + 2)
                for m in range(4):
                    op = nc.vector.tensor_scalar(probs[:, n % 3, m, :], probs[:, n % 3, m, :], st[:, 5, m:m + 1], None,
                                                 ALU.mult)
                op.then_inc(normed, 1)

            def output_lo(kt, tt):
                dve.wait_ge(o_hi_ready, 4 * kt + tt + 1)
                nc.vector.tensor_tensor(o_lo[:, 4 * kt + tt, :], bank[6 + tt % 2][:, :], o_hi[:, 4 * kt + tt, :],
                                        ALU.subtract).then_inc(o_lo_ready, 1)

            with dve.Fori(0, 2) as kt:
                pads(kt)
                mask_and_max(kt, 0)
                mask_and_max(kt, 1)
                normalise(kt, 0)
                for n in range(8):
                    if n + 2 < 8:
                        mask_and_max(kt, n + 2)
                    if n + 1 < 8:
                        normalise(kt, n + 1)
                    if n > 0 and n % 2 == 0:
                        output_lo(kt, n // 2 - 1)
                output_lo(kt, 3)
            dve.wait_ge(gb_step, 9)
            project_vector(dve, S_O, 1, 4, lambda j: mod[:, M_GMB, bass.ds(j, 1)], 5)

        mods0 = MOD_FIRST
        mods1 = MOD_FIRST + MOD_FFN

        @block.sync
        def _(sp):
            sp.dma_start(cols[:, :], cols_in).then_inc(in_loaded, 16)
            for m in range(8 * MOD_FIRST):
                sp.dma_start(first_mod[:, m, :], w_mod[m]).then_inc(first_loaded[m], 16)
                if m == 1:
                    sp.dma_start(x[:, :, :].rearrange("p j t -> p (j t)"), x_in).then_inc(x_loaded, 16)
            for n in range(RING):
                sp.dma_start(raw[:, n, :], w_stream[n]).then_inc(raw_loaded[n], 16)
            for m in range(2):
                load_mod(sp, 8 * MOD_FIRST + m, m, first=True)
            for n in (4, 5):
                load_slab(sp, n, n % RING)

            def slabs_and_mods(n0, m0):
                def gu_turn(i, blocks):
                    for u in range(2):
                        for q in range(2):
                            if blocks:
                                load_mod(sp, 4 * i + (m0 + 2 * u + q), q)
                            load_slab(sp, 4 * i + (n0 + 2 * u + q), (n0 + 2 * u + q) % RING)

                with sp.Fori(0, 2 * MOD_GU) as i:
                    gu_turn(i, True)
                gu_turn(2 * MOD_GU, False)

                def down_turn(i, last):
                    for jj in range(4):
                        for q in range(3 if jj % 2 else 5):
                            k = 8 * (jj // 2) + 5 * (jj % 2) + q
                            if not last or k < 14:
                                load_mod(sp, 16 * i + (m0 + 8 * MOD_GU + k), k % 2)
                            if q < DOWN_SPJ:
                                l = n0 + GU_SLABS + DOWN_SPJ * jj + q
                                load_slab(sp, 4 * DOWN_SPJ * i + l, l % RING)
                for i in range(2):
                    down_turn(i, i == 1)

            def slabs(n0, n1):
                whole = (n1 - n0) // RING
                with sp.Fori(0, whole) as i:
                    for q in range(RING):
                        load_slab(sp, 4 * i + (n0 + q), (n0 + q) % RING)
                for n in range(n0 + whole * RING, n1):
                    load_slab(sp, n, n % RING)

            slabs_and_mods(6, 8 * mods0 + 2)
            sp.wait_ge(slab_used, RING + S_IN)
            sp.dma_start(ssm_cols[:, :], ssm_cols_in).then_inc(ssm_loaded, 16)
            sp.dma_start(wdt[:, :, :].rearrange("p k h -> p (k h)"), w_dt).then_inc(ssm_loaded, 16)
            sp.dma_start(ssm_rows[:, :], ssm_rows_in.partition_broadcast(P)).then_inc(ssm_loaded, 16)
            slabs(S_IN + 6, S_FFN1 + 6)
            sp.wait_ge(slab_used, RING + S_FFN1)
            for m in range(2):
                load_mod(sp, 8 * mods1 + m, m)
            slabs_and_mods(S_FFN1 + 6, 8 * mods1 + 2)
            sp.wait_ge(mod_mm, NMOD)
            sp.dma_start(att_rows[:, :], att_rows_in.partition_broadcast(P)).then_inc(att_loaded, 16)
            slabs(S_KV + 6, SLABS)
            for j in range(DT):
                sp.wait_ge(out_ready, j + 1)
                sp.dma_start(out[:, j, :], x[:, j, :]).then_inc(out_stored, 16)
            sp.wait_ge(out_stored, 16 * DT)

        @block.gpsimd
        def _(pool):
            nc.gpsimd.memset(ones[:, :], 1.0).then_inc(slab_used, RING)
            nc.gpsimd.memset(eps[:, :], EPS).then_inc(consts, 1)
            for n, starts_at_one in enumerate((sq_ready, a_ready, a_lo_ready, y_lo_ready, gstat_done, q_ready, scored, masked,
                                               o_done, o_lo_ready)):
                nc.gpsimd.memset(spare[:, n:n + 1], 0.0).then_inc(starts_at_one, 1)
            pool.wait_ge(slab_used, RING + S_IN)
            pool.wait_ge(a_lo_ready, ONE + FT)
            for m, fill in ((after, 0.0), (upto, 1.0), (ident, 0.0)):
                nc.gpsimd.memset(m[:, :], fill).then_inc(ssm_consts, 1)
            pool.wait_ge(ssm_consts, 3)
            nc.gpsimd.affine_select(out=after[:, :], in_=after[:, :], compare_op=ALU.is_ge, fill=1.0, base=0,
                                    pattern=[[1, P]], channel_multiplier=-1).then_inc(ssm_consts, 1)
            nc.gpsimd.affine_select(out=upto[:, :], in_=upto[:, :], compare_op=ALU.is_ge, fill=0.0, base=0,
                                    pattern=[[1, P]], channel_multiplier=-1).then_inc(ssm_consts, 1)
            nc.gpsimd.affine_select(out=ident[:, :], in_=ident[:, :], compare_op=ALU.not_equal, fill=1.0, base=0,
                                    pattern=[[-1, P]], channel_multiplier=1).then_inc(ssm_consts, 1)
            pool.wait_ge(slab_used, RING + S_Q)
            nc.gpsimd.memset(mask[:, :, :, :], 0.0).then_inc(att_consts, 1)
            nc.gpsimd.memset(ident_a[:, :], 0.0).then_inc(att_consts, 1)
            nc.gpsimd.memset(k_pad[:, :, :], 0.0).then_inc(att_consts, 1)
            nc.gpsimd.memset(v_pad[:, :, :, :], 0.0).then_inc(att_consts, 1)
            pool.wait_ge(att_consts, 4)
            nc.gpsimd.affine_select(out=ident_a[:, :], in_=ident_a[:, :], compare_op=ALU.not_equal, fill=1.0, base=0,
                                    pattern=[[-1, P]], channel_multiplier=1).then_inc(att_consts, 1)
            m4 = mask[:, :, :, :].rearrange("p h b k -> p (h b) k")
            nc.gpsimd.affine_select(out=m4, in_=m4, compare_op=ALU.is_gt, fill=MASKED, base=0,
                                    pattern=[[0, 4], [1, 2 * P]], channel_multiplier=-1).then_inc(att_consts, 1)
            pool.wait_ge(att_consts, 6)
            nc.gpsimd.affine_select(out=m4, in_=m4, compare_op=ALU.is_ge, fill=MASKED, base=P,
                                    pattern=[[0, 4], [-1, 2 * P]], channel_multiplier=1).then_inc(att_consts, 1)
            pool.wait_ge(att_consts, 7)
            nc.gpsimd.memset(mask[:, 0, 0, 0:P], MASKED).then_inc(att_consts, 1)

        @block.scalar
        def _(act):
            act.wait_ge(in_loaded, 16)
            nc.scalar.activation(c_act[:, :], col("c"), ACT.Silu).then_inc(c_ready, 1)
            act.wait_ge(x_loaded, 16)
            for j in range(DT):
                nc.scalar.activation(first_sq[:, j, :], x[:, j, :], ACT.Square).then_inc(first_sq_ready, 1)
            act.wait_ge(consts, 1)
            rstd_scalar(act, 0)
            prep_hi(act, 0, 0)
            prep_hi(act, 0, 1)
            act.wait_ge(mod_col, 2)
            norm_scalar(act, 0, M_SH1A, h_hi)
            ffn_scalar(act, 0, S_FFN0, 1, mods0)
            rstd_scalar(act, 1)
            norm_scalar(act, 1, M_SHMA, h_hi)
            ssm_scalar(act)
            rstd_scalar(act, 2)
            norm_scalar(act, 2, M_SH2A, h_hi)
            ffn_scalar(act, 1, S_FFN1, 3, mods1)
            rstd_scalar(act, 3)
            norm_scalar(act, 3, M_KVSH, hkv_hi)
            kv_scalar(act)
            ffn_scalar(act, 2, S_FFN2, 4)
            rstd_scalar(act, 4)
            norm_scalar(act, 5, M_SHMB, h_hi)
            att_scalar(act)
            rstd_scalar(act, 5)
            norm_scalar(act, 6, M_SH2B, h_hi)
            ffn_scalar(act, 3, S_FFN3, 6, last=True)
            rstd_scalar(act, 6)

        @block.vector
        def _(dve):
            dve.wait_ge(c_ready, 1)
            for v in range(MOD_FIRST):
                for k in range(8):
                    mod_block(dve, v, k, first=True)
                if v == MOD_FIRST - 1:
                    prep_lo(dve, 0, 0)
                    prep_lo(dve, 0, 1)
                mod_collect(dve, v)
            dve.wait_ge(mod_col, 2)
            columns_vector(dve, 1, M_SC1A, col("nw_ffn0"))
            norm_vector(dve, 0, 0, M_SH1A, h_hi, h_lo)
            ffn_vector(dve, 0, S_FFN0, M_G1A, 1, mods0, 1)
            columns_vector(dve, 3, M_SCMA, col("nw_mix0"))
            norm_vector(dve, 1, 1, M_SHMA, h_hi, h_lo)
            ssm_vector(dve)
            columns_vector(dve, 4, M_SC2A, col("nw_ffn1"))
            norm_vector(dve, 2, 2, M_SH2A, h_hi, h_lo)
            ffn_vector(dve, 1, S_FFN1, M_G2A, 3, mods1, 4)
            columns_vector(dve, 6, M_KVSC, col("nw_kv"))
            norm_vector(dve, 3, 3, M_KVSH, hkv_hi, hkv_lo)
            kv_vector(dve)
            ffn_vector(dve, 2, S_FFN2, M_G1B, 4, None, 7)
            columns_vector(dve, 9, M_SCMB, col("nw_mix1"))
            norm_vector(dve, 4, 5, M_SHMB, h_hi, h_lo)
            att_vector(dve)
            columns_vector(dve, 10, M_SC2B, col("nw_ffn3"))
            norm_vector(dve, 5, 6, M_SH2B, h_hi, h_lo)
            ffn_vector(dve, 3, S_FFN3, M_G2B, 6, None, 10, last=True)
            dve.wait_ge(rs_step, 14)
            w = COLS["nw_final"][0]
            for j in range(DT):
                nc.vector.scalar_tensor_tensor(x[:, j, :], x[:, j, :], cols[:, w + j:w + j + 1], rstd[:, :],
                                               ALU.mult, ALU.mult).then_inc(out_ready, 1)

        @block.tensor
        def _(pe):
            pe.wait_ge(slab_used, RING)
            for j in range(DT):
                pe.wait_ge(first_sq_ready, j + 1)
                mm = nc.tensor.matmul(bank[6][:, :], ones[:, :], first_sq[:, j, :], start=(j == 0), stop=(j == DT - 1))
            mm.then_inc(stat_done, 1)
            mod_sum(pe, 0, first=True)
            mod_sum(pe, 1)
            ffn_tensor(pe, 0, S_FFN0, 0, 1, mods0)
            ssm_tensor(pe)
            ffn_tensor(pe, 1, S_FFN1, 2, 3, mods1)
            kv_tensor(pe)
            ffn_tensor(pe, 2, S_FFN2, 4, 4)
            att_tensor(pe)
            ffn_tensor(pe, 3, S_FFN3, 6, 6, last=True)


def lay_out(i):
    import numpy as np

    def tiles(w):
        kt, nt = w.shape[0] // P, w.shape[1] // P
        return np.ascontiguousarray(w.reshape(kt, P, nt, P).transpose(2, 1, 0, 3)).reshape(nt, P, kt * P)

    def cut(w, per):
        n, _, width = w.shape
        full = np.zeros((n, P, per * SLAB), w.dtype)
        full[:, :, :width] = w
        return full.reshape(n, P, per, SLAB).transpose(0, 2, 1, 3).reshape(n * per, P, SLAB)

    def ffn(layer, half):
        gu = i["ffn_w_gu"][layer, half]
        pairs = np.stack([tiles(gu[:, :FF]), tiles(gu[:, FF:])], 1).reshape(GU_SLABS, P, SLAB)
        return [pairs, cut(tiles(i["ffn_w_down"][layer, half]), DOWN_SPJ)]

    def columns(v):
        return v.reshape(-1, P).T

    w_in = i["ssm_w_in"][0]
    z, xbc = tiles(w_in[:, :DIN]), tiles(w_in[:, DIN:DIN + DIN + 2 * GROUPS * P])

    def group_order(t, g):
        return [t[2 * g], t[2 * g + 1], t[16 + g], t[24 + g]]

    order = group_order(xbc, 0)
    for g in range(GROUPS):
        order += [z[2 * g], z[2 * g + 1]]
        if g < GROUPS - 1:
            order += group_order(xbc, g + 1)
    w_out = cut(tiles(i["ssm_w_out"][0]), 2).reshape(DT // 2, 2, 2, P, SLAB).transpose(0, 2, 1, 3, 4)
    heads = [8 * kt + 4 * ab + tt for kt in range(2) for tt in range(4) for ab in range(2)]
    feats = np.concatenate([np.arange(HDIM) + h * HDIM for h in heads])
    stream = np.concatenate(
        ffn(0, 0) + [np.stack(order), w_out.reshape(OUT_SLABS, P, SLAB)] + ffn(0, 1) + [tiles(i["w_kv"])] + ffn(1, 0)
        + [tiles(i["attn_w_q"][0][:, feats]), tiles(i["attn_w_o"][0][feats])] + ffn(1, 1))
    mods = np.concatenate([i["mod_w"][0], i["kv_mod_w"], i["mod_w"][1]], 1)
    w_mod = np.ascontiguousarray(mods.reshape(DT, P, NMOD, D).transpose(2, 0, 1, 3)).reshape(NMOD * DT, P, D)
    mod_b = np.concatenate([i["mod_b"][0], i["kv_mod_b"], i["mod_b"][1]])
    w_dt = np.ascontiguousarray(w_in[:, -HEADS:].reshape(DT, P, HEADS).transpose(1, 0, 2)).reshape(P, DT * HEADS)
    cols = np.concatenate([columns(v) for v in (
        i["c"], mod_b, i["ffn_norm_w"][0, 0], i["ffn_norm_w"][0, 1], i["ffn_norm_w"][1, 0], i["ffn_norm_w"][1, 1],
        i["mix_norm_w"][0], i["mix_norm_w"][1], i["kv_norm_w"], i["final_norm_w"], i["attn_b_o"][0],
        i["attn_b_q"][0][feats], i["b_kv"][:KV * HDIM])], 1)
    taps = np.concatenate([i["ssm_conv_w"][0], i["ssm_conv_b"]], 0).reshape(5, 32, P)
    taps = np.stack([np.stack(group_order(taps.transpose(1, 2, 0), g)) for g in range(GROUPS)])
    ssm_cols = np.concatenate([taps.transpose(2, 0, 1, 3).reshape(P, SSM_CONV),
                               columns(np.repeat(i["ssm_d"][0], HDIM)), columns(i["ssm_norm_w"][0])], 1)
    ssm_rows = np.concatenate([i["ssm_dt_bias"][0], i["ssm_a_log"][0]])
    att_rows = np.concatenate([i["b_kv"][KV * HDIM:], i["attn_sinks"][0][np.array(heads)]])
    x_t = np.ascontiguousarray(i["x"][0].T.reshape(DT, P, T).transpose(1, 0, 2)).reshape(P, DT * T)
    return {"w_stream": stream, "w_mod": w_mod, "w_dt": w_dt, "x_in": x_t, "cols_in": np.ascontiguousarray(cols),
            "ssm_cols_in": np.ascontiguousarray(ssm_cols), "ssm_rows_in": ssm_rows, "att_rows_in": att_rows}


def kernel(**inputs):
    import numpy as np
    import concourse.bacc as bacc
    from concourse.bass_utils import run_bass_kernel_spmd

    arrays = lay_out({k: np.asarray(v) for k, v in inputs.items()})
    nc = bacc.Bacc("TRN2", target_bir_lowering=False, num_devices=1)
    args = [nc.dram_tensor(n, a.shape, mybir.dt.from_np(a.dtype), kind="ExternalInput").ap() for n, a in arrays.items()]
    out = nc.dram_tensor("trunk_out", (P, DT, T), F32, kind="ExternalOutput").ap()
    trunk(nc, *args, out)
    r = run_bass_kernel_spmd(nc, [arrays], core_ids=[0])
    got = r.results[0]["trunk_out"]
    return got.transpose(2, 1, 0).reshape(1, T, D)
```
